# Optimizing a Trainium2 kernel written in Bass

```python
import math
import jax, jax.numpy as jnp
from jax import lax
import numpy as np

D_MODEL = 1024
BATCH = 1
SEQ = 256
DEPTH = 2

EPS = 1e-6
RET_HEADS = 4
RET_QK_DIM = 128
RET_V_DIM = 256
RET_CHUNK = 128
RET_ROPE_BASE = 10000.0
SSM_HEADS = 16
SSM_HEAD_DIM = 64
SSM_GROUPS = 4
SSM_STATE = 128
SSM_CONV = 4
SSM_CHUNK = 128
SSM_INNER = SSM_HEADS * SSM_HEAD_DIM
SSM_XBC = SSM_INNER + 2 * SSM_GROUPS * SSM_STATE
ATT_PATTERNS = ((128, 1), (512, 4), (2048, 16))
ATT_SLOTS = 4
ATT_HEAD_DIM = 64
ATT_HEADS = len(ATT_PATTERNS) * ATT_SLOTS
N_BRANCHES = 3
D_FF = -(-8 * D_MODEL // (3 * 256)) * 256

IN_WIDTHS = (
    RET_HEADS * RET_QK_DIM,
    RET_HEADS * RET_QK_DIM,
    RET_HEADS * RET_V_DIM,
    RET_HEADS * RET_V_DIM,
    SSM_INNER,
    SSM_XBC,
    SSM_HEADS,
    ATT_HEADS * ATT_HEAD_DIM,
    ATT_HEADS * ATT_HEAD_DIM,
    ATT_HEADS * ATT_HEAD_DIM,
    N_BRANCHES * D_MODEL,
)
IN_WIDTH = sum(IN_WIDTHS)
IN_SPLITS = tuple(int(v) for v in np.cumsum(IN_WIDTHS)[:-1])

kernel_name = "hybrid_retention_ssd_dilated_attn_block"

def rms_norm(x, w):
    xf = x.astype(jnp.float32)
    y = xf * lax.rsqrt(jnp.mean(xf * xf, axis=-1, keepdims=True) + EPS)
    return (y * w.astype(jnp.float32)).astype(x.dtype)

def to_chunks(t, chunk):
    b, s = t.shape[:2]
    return jnp.moveaxis(t.reshape((b, s // chunk, chunk) + t.shape[2:]), 1, 0)

def from_chunks(t):
    t = jnp.moveaxis(t, 0, 1)
    return t.reshape((t.shape[0], t.shape[1] * t.shape[2]) + t.shape[3:])

def rotary(t, pos):
    half = t.shape[-1] // 2
    inv_freq = RET_ROPE_BASE ** (-jnp.arange(half, dtype=jnp.float32) / half)
    ang = pos[:, None] * inv_freq[None, :]
    cos, sin = jnp.cos(ang)[:, None, :], jnp.sin(ang)[:, None, :]
    t1, t2 = t[..., :half], t[..., half:]
    return jnp.concatenate([t1 * cos - t2 * sin, t1 * sin + t2 * cos], axis=-1)

def retention(q, k, v, g):
    dtype = v.dtype
    q, k, v, g = (t.astype(jnp.float32) for t in (q, k, v, g))
    b, s, h, dk = q.shape
    dv = v.shape[-1]
    pos = jnp.arange(s, dtype=jnp.float32)
    q = rotary(q, pos)
    k = rotary(k, pos) * (dk ** -0.5)
    log_gamma = jnp.log1p(-jnp.exp(jnp.linspace(math.log(1.0 / 32), math.log(1.0 / 512), h))).astype(jnp.float32)
    C = RET_CHUNK
    idx = jnp.arange(C, dtype=jnp.float32)
    diff = idx[:, None] - idx[None, :]
    intra = jnp.exp(jnp.where(diff[None] >= 0, diff[None] * log_gamma[:, None, None], -jnp.inf))
    cross_q = jnp.exp((idx[:, None] + 1.0) * log_gamma[None, :])[None, :, :, None]
    state_k = jnp.exp((C - 1.0 - idx[:, None]) * log_gamma[None, :])[None, :, :, None]
    chunk_decay = jnp.exp(C * log_gamma)[None, :, None, None]

    def step(R, inp):
        qc, kc, vc = inp
        scores = jnp.einsum('bihd,bjhd->bhij', qc, kc) * intra[None]
        inner = jnp.einsum('bhij,bjhe->bihe', scores, vc)
        cross = jnp.einsum('bihd,bhde->bihe', qc, R) * cross_q
        R = R * chunk_decay + jnp.einsum('bjhd,bjhe->bhde', kc * state_k, vc)
        return R, inner + cross

    R0 = jnp.zeros((b, h, dk, dv), jnp.float32)
    _, y = lax.scan(step, R0, (to_chunks(q, C), to_chunks(k, C), to_chunks(v, C)))
    y = from_chunks(y)
    mu = jnp.mean(y, axis=-1, keepdims=True)
    var = jnp.mean(jnp.square(y - mu), axis=-1, keepdims=True)
    y = (y - mu) * lax.rsqrt(var + EPS)
    out = jax.nn.silu(g) * y
    return out.reshape(b, s, h * dv).astype(dtype)

def causal_depthwise_conv(x, w, bias):
    ch = x.shape[-1]
    y = lax.conv_general_dilated(
        x, w[:, None, :], window_strides=(1,), padding=[(SSM_CONV - 1, 0)],
        dimension_numbers=('NWC', 'WIO', 'NWC'), feature_group_count=ch)
    return y + bias

def ssd_mixer(z, xbc, dt, conv_w, conv_b, dt_bias, a_log, d_skip, norm_w):
    dtype = z.dtype
    z, xbc, dt = (t.astype(jnp.float32) for t in (z, xbc, dt))
    conv_w, conv_b, dt_bias, a_log, d_skip, norm_w = (t.astype(jnp.float32) for t in (conv_w, conv_b, dt_bias, a_log, d_skip, norm_w))
    b, s, _ = xbc.shape
    G, R, P, N = SSM_GROUPS, SSM_HEADS // SSM_GROUPS, SSM_HEAD_DIM, SSM_STATE
    xbc = jax.nn.silu(causal_depthwise_conv(xbc, conv_w, conv_b))
    xs = xbc[..., :SSM_INNER].reshape(b, s, G, R, P)
    Bm = xbc[..., SSM_INNER:SSM_INNER + G * N].reshape(b, s, G, N)
    Cm = xbc[..., SSM_INNER + G * N:].reshape(b, s, G, N)
    dt = jax.nn.softplus(dt + dt_bias)
    A = -jnp.exp(a_log)
    dA = (dt * A).reshape(b, s, G, R)
    xdt = xs * dt.reshape(b, s, G, R, 1)
    L_ = SSM_CHUNK
    causal = jnp.tril(jnp.ones((L_, L_), dtype=bool))

    def step(state, inp):
        xc, ac, bc, cc = inp
        cs = jnp.cumsum(ac, axis=1)
        cst = jnp.moveaxis(cs, 1, -1)
        seg = cst[..., :, None] - cst[..., None, :]
        Lmat = jnp.exp(jnp.where(causal, seg, -jnp.inf))
        cb = jnp.einsum('blgn,bsgn->bgls', cc, bc)
        y_diag = jnp.einsum('bgls,bgrls,bsgrp->blgrp', cb, Lmat, xc)
        y_off = jnp.einsum('blgn,bgrpn->blgrp', cc, state) * jnp.exp(cs)[..., None]
        decay_to_end = jnp.exp(cs[:, -1:] - cs)
        state = state * jnp.exp(cs[:, -1])[..., None, None] + jnp.einsum('bsgn,bsgr,bsgrp->bgrpn', bc, decay_to_end, xc)
        return state, y_diag + y_off

    state0 = jnp.zeros((b, G, R, P, N), jnp.float32)
    _, y = lax.scan(step, state0, (to_chunks(xdt, L_), to_chunks(dA, L_), to_chunks(Bm, L_), to_chunks(Cm, L_)))
    y = from_chunks(y) + xs * d_skip.reshape(G, R, 1)
    y = y.reshape(b, s, SSM_INNER) * jax.nn.silu(z)
    yg = y.reshape(b, s, G, SSM_INNER // G)
    yg = yg * lax.rsqrt(jnp.mean(yg * yg, axis=-1, keepdims=True) + EPS)
    return (yg.reshape(b, s, SSM_INNER) * norm_w).astype(dtype)

def strided_band_attention(q, k, v, span, dil):
    b, s, h, e = q.shape
    L = s // dil
    nb = -(-L // span)
    pad = nb * span - L

    def strided_blocks(t):
        t = t.reshape(b, L, dil, h, e).transpose(0, 2, 1, 3, 4)
        t = jnp.pad(t, ((0, 0), (0, 0), (0, pad), (0, 0), (0, 0)))
        return t.reshape(b, dil, nb, span, h, e)

    qb, kb, vb = strided_blocks(q), strided_blocks(k), strided_blocks(v)

    def with_prev(t):
        prev = jnp.pad(t, ((0, 0), (0, 0), (1, 0), (0, 0), (0, 0), (0, 0)))[:, :, :-1]
        return jnp.concatenate([prev, t], axis=3)

    kk, vv = with_prev(kb), with_prev(vb)
    scores = jnp.einsum('bdnqhe,bdnkhe->bdnhqk', qb, kk) * (e ** -0.5)
    qi = jnp.arange(span)[:, None]
    kj = jnp.arange(2 * span)[None, :]
    dist = qi + span - kj
    band = (dist >= 0) & (dist <= span)
    key_pos = jnp.arange(nb)[:, None] * span - span + jnp.arange(2 * span)[None, :]
    valid = band[None] & (key_pos >= 0)[:, None, :]
    scores = jnp.where(valid[None, None, :, None], scores, -jnp.inf)
    m = jnp.max(scores, axis=-1, keepdims=True)
    lse = m + jnp.log(jnp.sum(jnp.exp(scores - m), axis=-1, keepdims=True))
    p = jnp.exp(scores - lse)
    o = jnp.einsum('bdnhqk,bdnkhe->bdnqhe', p, vv)
    o = o.reshape(b, dil, nb * span, h, e)[:, :, :L].transpose(0, 2, 1, 3, 4).reshape(b, s, h, e)
    lse = jnp.moveaxis(lse[..., 0], 3, 4)
    lse = lse.reshape(b, dil, nb * span, h)[:, :, :L].transpose(0, 2, 1, 3).reshape(b, s, h)
    return o, lse

def dilated_attention(q, k, v):
    dtype = v.dtype
    b, s, _ = q.shape
    n_g = len(ATT_PATTERNS)
    shp = (b, s, n_g, ATT_SLOTS, ATT_HEAD_DIM)
    q, k, v = (t.astype(jnp.float32).reshape(shp) for t in (q, k, v))
    outs, lses = [], []
    for gi, (window, dil) in enumerate(ATT_PATTERNS):
        o, lse = strided_band_attention(q[:, :, gi], k[:, :, gi], v[:, :, gi], window // dil, dil)
        outs.append(o)
        lses.append(lse)
    alpha = jax.nn.softmax(jnp.stack(lses, axis=0), axis=0)
    out = jnp.sum(alpha[..., None] * jnp.stack(outs, axis=0), axis=0)
    return out.reshape(b, s, ATT_SLOTS * ATT_HEAD_DIM).astype(dtype)

def setup_inputs(seed: int = 0) -> dict:
    key = jax.random.key(seed)
    ks = jax.random.split(key, 24)
    f32 = jnp.float32

    def nrm(k, shape, fan_in):
        return jax.random.normal(k, shape, f32) * (fan_in ** -0.5)

    def gain(k, shape):
        return 1.0 + 0.05 * jax.random.normal(k, shape, f32)

    dt0 = jnp.exp(jax.random.uniform(ks[8], (DEPTH, SSM_HEADS), f32, math.log(1e-3), math.log(1e-1)))
    return {
        "x": jax.random.normal(ks[0], (BATCH, SEQ, D_MODEL), f32),
        "c": jax.random.normal(ks[1], (BATCH, D_MODEL), f32),
        "ada_w": nrm(ks[2], (DEPTH, D_MODEL, 6 * D_MODEL), D_MODEL),
        "ada_b": 0.02 * jax.random.normal(ks[3], (DEPTH, 6 * D_MODEL), f32),
        "norm1_w": gain(ks[4], (DEPTH, D_MODEL)),
        "w_in": nrm(ks[5], (DEPTH, D_MODEL, IN_WIDTH), D_MODEL),
        "ssm_conv_w": nrm(ks[6], (DEPTH, SSM_CONV, SSM_XBC), SSM_CONV),
        "ssm_conv_b": 0.02 * jax.random.normal(ks[7], (DEPTH, SSM_XBC), f32),
        "ssm_dt_bias": dt0 + jnp.log(-jnp.expm1(-dt0)),
        "ssm_a_log": jnp.log(jax.random.uniform(ks[9], (DEPTH, SSM_HEADS), f32, 1.0, 16.0)),
        "ssm_d": 1.0 + 0.1 * jax.random.normal(ks[10], (DEPTH, SSM_HEADS), f32),
        "ssm_norm_w": gain(ks[11], (DEPTH, SSM_INNER)),
        "w_br_ret": nrm(ks[12], (DEPTH, RET_HEADS * RET_V_DIM, D_MODEL), RET_HEADS * RET_V_DIM),
        "w_br_ssm": nrm(ks[13], (DEPTH, SSM_INNER, D_MODEL), SSM_INNER),
        "w_br_att": nrm(ks[14], (DEPTH, ATT_SLOTS * ATT_HEAD_DIM, D_MODEL), ATT_SLOTS * ATT_HEAD_DIM),
        "w_out": nrm(ks[15], (DEPTH, D_MODEL, D_MODEL), D_MODEL),
        "norm2_w": gain(ks[16], (DEPTH, D_MODEL)),
        "w_ff1": nrm(ks[17], (DEPTH, D_MODEL, D_FF), D_MODEL),
        "w_ff3": nrm(ks[18], (DEPTH, D_MODEL, D_FF), D_MODEL),
        "w_ff2": nrm(ks[19], (DEPTH, D_FF, D_MODEL), D_FF),
        "final_norm_w": gain(ks[20], (D_MODEL,)),
    }

def reference(x, c, ada_w, ada_b, norm1_w, w_in, ssm_conv_w, ssm_conv_b, ssm_dt_bias, ssm_a_log,
              ssm_d, ssm_norm_w, w_br_ret, w_br_ssm, w_br_att, w_out, norm2_w, w_ff1, w_ff3, w_ff2,
              final_norm_w):
    b, s, _ = x.shape
    for i in range(DEPTH):
        ada = jax.nn.silu(c) @ ada_w[i] + ada_b[i]
        sh1, sc1, g1, sh2, sc2, g2 = jnp.split(ada[:, None, :], 6, axis=-1)

        h = rms_norm(x, norm1_w[i]) * (1.0 + sc1) + sh1
        proj = h @ w_in[i]
        (rq, rk, rv, rg, sz, sxbc, sdt, aq, ak, av, gate_logits) = jnp.split(proj, IN_SPLITS, axis=-1)
        y_ret = retention(rq.reshape(b, s, RET_HEADS, RET_QK_DIM), rk.reshape(b, s, RET_HEADS, RET_QK_DIM),
                          rv.reshape(b, s, RET_HEADS, RET_V_DIM), rg.reshape(b, s, RET_HEADS, RET_V_DIM))
        y_ssm = ssd_mixer(sz, sxbc, sdt, ssm_conv_w[i], ssm_conv_b[i], ssm_dt_bias[i], ssm_a_log[i],
                          ssm_d[i], ssm_norm_w[i])
        y_att = dilated_attention(aq, ak, av)
        gates = jax.nn.sigmoid(gate_logits).reshape(b, s, N_BRANCHES, D_MODEL)
        mixed = (gates[:, :, 0] * (y_ret @ w_br_ret[i])
                 + gates[:, :, 1] * (y_ssm @ w_br_ssm[i])
                 + gates[:, :, 2] * (y_att @ w_br_att[i]))
        x = x + g1 * (mixed @ w_out[i])

        h2 = rms_norm(x, norm2_w[i]) * (1.0 + sc2) + sh2
        ffn = (jax.nn.silu(h2 @ w_ff1[i]) * (h2 @ w_ff3[i])) @ w_ff2[i]
        x = x + g2 * ffn
    return rms_norm(x, final_norm_w)


_drawn_inputs = setup_inputs


def setup_inputs(seed=0):
    import zlib

    import numpy as np

    out = dict(_drawn_inputs(seed))
    spreads = {}
    factors = {'ssm_conv_b': 5.481}
    for name, (base, spread) in spreads.items():
        noise = np.random.default_rng([zlib.crc32(name.encode()), seed]).standard_normal(out[name].shape)
        drawn = base * np.exp(spread * noise) if base else spread * noise
        out[name] = __import__('jax').numpy.asarray(drawn.astype(out[name].dtype))
    for name, factor in factors.items():
        out[name] = (out[name] * factor).astype(out[name].dtype)
    return out
```

```python
from contextlib import ExitStack

import numpy as np
import concourse.bass as bass
from concourse import mybir

P = 128
D = 1024
KB = D // P
S = 256
NT = S // P
L = 2
EPS = 1e-6
RH, RQK, RV = 4, 128, 256
SH, SHD, SG = 16, 64, 4
AG, AS, AHD = 3, 4, 64
FF = 2816
FB = FF // P
COL = 256
HALF = KB * COL // 2
XBC = 2048
C_QK, C_TOK, C_XBC = 0, 1024, 4096
C_DT = C_XBC + XBC
C_AQK = C_DT + SH
C_AV = C_AQK + 2 * AG * AS * AHD
C_GATE = C_AV + AG * AS * AHD
U_ADA, N_ADA = 0, 8
U_QK, N_QK = 8, 4
U_XBC, N_XBC = 12, 8
U_AQK, N_AQK = 20, 6
U_TOK, N_TOK = 26, 24
U_AV, N_AV = 50, 3
U_DT = 53
U_MIX, N_MIX = 54, 16
U_BR = 70
U_ATT = 78
U_OUT, N_OUT = 79, 4
U_FF, N_FF = 83, 22
U_FF2, N_FF2 = 105, 11
UNITS = 116
RAW = 4
SPL = 2
BANK0 = 2

F32 = mybir.dt.float32
F32R = mybir.dt.float32r
ALU = mybir.AluOpType
ACT = mybir.ActivationFunctionType
AXX = mybir.AxisListType.X

T_COS, T_SIN, T_RET, T_ATT = 0, 256, 512, 1536
T_CB, T_TRI, T_ID = 2304, 2688, 2816
T_END = 2944
Q_ADAB, Q_N1, Q_N2, Q_SN, Q_CB = 0, 48, 56, 64, 72
Q_CW, Q_DTB, Q_ALOG, Q_DSK = 88, 152, 168, 184
Q_END = 200
N_ROW0 = 88


class Unit:

    def __init__(self, base, per=0, j=None):
        self.base, self.per, self.j = base, per, j

    def plus(self, d):
        return Unit(self.base + d, self.per, self.j)

    def over(self, k, times=1, off=0):
        c = self.base // k * times + off
        return c if self.j is None else self.j * (self.per // k * times) + c

    def mod(self, k):
        assert self.j is None or self.per % k == 0
        return self.base % k


def units(eng, base, count, per, fn):
    full = count // per
    done = 0
    if full > 1:
        with eng.Fori(0, full) as j:
            for b in range(per):
                fn(Unit(base + b, per, j), Unit(b, per, j))
        done = full * per
    for b in range(done, count):
        fn(Unit(base + b), Unit(b))


def build(nc, x, c, ada_w, ada_b, norm1_w, w_in, conv_w, conv_b, dt_bias, a_log, ssm_d, ssm_norm_w,
          w_br_ret, w_br_ssm, w_br_att, w_out, norm2_w, w_ff1, w_ff3, w_ff2, final_norm_w,
          table, select, out):
    with ExitStack() as ctx:
        at = [nc.sbuf_base + (-nc.sbuf_base) % 64]

        def sb(name, shape, dt=F32, offset=None):
            size = 4 * int(np.prod(shape[1:]))
            if offset is None:
                offset = at[0]
                at[0] += size + (-size) % 32
            return nc.alloc_sbuf_tensor_at(name, shape, dt, offset=offset)

        def region(size):
            at[0] += size
            return at[0] - size

        def sem(name):
            return ctx.enter_context(nc.semaphore(name))

        raw = sb("raw", [P, RAW, 2 * HALF])
        w_hi = sb("w_hi", [P, SPL, 2 * HALF], F32R)
        w_lo = sb("w_lo", [P, SPL, 2 * HALF], F32R)
        xf = sb("xf", [P, KB, S])
        r_h = region(2 * KB * S * 4)
        h_hi = sb("h_hi", [P, KB, S], F32R, r_h)
        h_lo = sb("h_lo", [P, KB, S], F32R, r_h + KB * S * 4)
        m_hi = sb("m_hi", [P, KB, S], F32R, r_h)
        m_lo = sb("m_lo", [P, KB, S], F32R, r_h + KB * S * 4)
        r_z1 = region(36 * S * 4)
        xbc = sb("xbc", [P, 16, S], F32, r_z1)
        aqk = sb("aqk", [P, 12, S], F32, r_z1 + 16 * S * 4)
        qk = sb("qk", [P, 4, 2, S], F32, r_z1 + 28 * S * 4)
        y_hi = sb("y_hi", [P, 18, S], F32R, r_z1)
        y_lo = sb("y_lo", [P, 18, S], F32R, r_z1 + 18 * S * 4)
        sq = sb("sq", [P, KB, S], F32, r_z1)
        hn = sb("hn", [P, KB, S], F32, r_z1 + KB * S * 4)
        r_tok = region(3 * NT * D * 4)
        tok = sb("tok", [P, 3, NT, D], F32, r_tok)
        mixed = sb("mixed", [P, KB, S], F32, r_tok + NT * D * 4)
        av = sb("av", [P, NT, AG * AS * AHD])
        yatt = sb("yatt", [P, NT, AS * AHD])
        r_gate = region(24 * S * 4)
        gates = sb("gates", [P, 24, S], F32, r_gate)
        x_tok = sb("x_tok", [P, NT, D], F32, r_gate)
        tab = sb("tab", [P, T_END])
        sel = sb("sel", [SH, SH * P])
        f_hi = sb("f_hi", [P, FB, S], F32R, r_z1)
        f_lo = sb("f_lo", [P, FB, S], F32R, r_gate)
        assert 22 * S * 4 <= 36 * S * 4
        r_l = region(SG * 384 * 4)
        decay = sb("decay", [P, 4, 384], F32, r_l)
        p_t = sb("p_t", [P, 9, P], F32, r_l)
        xpad = sb("xpad", [P, 2, 2, S + 3], F32, r_l)
        rope_c = sb("rope_c", [P, 2, S], F32, r_l)
        rope_s = sb("rope_s", [P, 2, S], F32, r_l + 2 * S * 4)
        sil = sb("sil", [P, 2 * S], F32, r_l)
        hid = sb("hid", [P, 2 * S], F32, r_l + 2 * S * 4)
        br = sb("br", [P, 2 * S], F32, r_l)
        att_s = sb("att_s", [P, 9 * P])
        cbm = sb("cbm", [P, 384])
        xdt = sb("xdt", [P, NT, 4 * SHD])
        ytmp = sb("ytmp", [P, NT, 4 * SHD])
        m_ret = sb("m_ret", [P, 384])
        csr = sb("csr", [SH, S])
        rstd = sb("rstd", [P, S])
        junk = rstd[:, :]
        rows = sb("rows", [P, 2, P])
        rowv = sb("rowv", [1, 3 * SH])
        crow = sb("crow", [16, P], F32, r_gate + NT * D * 4)
        par = sb("par", [P, Q_END])
        fnw = sb("fnw", [P, KB])
        c32 = sb("c32", [P, KB])
        cc = sb("cc", [P, KB, 2], F32R)
        ada = sb("ada", [P, 48])
        a1 = sb("a1", [P, 2, KB])
        g1h = sb("g1h", [P, KB])
        eps = sb("eps", [P, 1])
        one = sb("one", [P, 1])
        dt_x = sb("dt_x", [P, NT * SH])
        dt_e = sb("dt_e", [P, NT * SH])
        dt = sb("dt", [P, NT, SH])
        exp_a = sb("exp_a", [P, SH])
        d_a = sb("d_a", [P, NT, SH])
        cs = sb("cs", [P, NT, SH])
        negmax = sb("negmax", [P, 2])
        ssum = sb("ssum", [P, 2])
        rsum = sb("rsum", [P, 2])
        bst = sb("bst", [P, NT, 6])
        mv = sb("mv", [P, RH, NT, 2])
        ss = sb("ss", [P, SG, NT])
        sd = sb("sd", [P, 2, 8])
        ri = sb("ri", [P, 2, 8])
        assert at[0] <= nc.sbuf_usable_end, (at[0], nc.sbuf_usable_end)

        bank = [ctx.enter_context(nc.psum_tensor(f"bank{i}", [P, 512], F32)) for i in range(8)]
        cos, sin = tab[:, T_COS:T_COS + S], tab[:, T_SIN:T_SIN + S]
        ret_mask = tab[:, T_RET:T_RET + RH * S].rearrange("p (h t) -> p h t", h=RH)
        att_mask = tab[:, T_ATT:T_ATT + AG * S].rearrange("p (g t) -> p g t", g=AG)
        cb_mask = tab[:, T_CB:T_CB + 384]
        ones = tab[:, T_CB + P:T_CB + 2 * P]
        tri = [tab[:, T_TRI:T_TRI + P], tab[:, T_CB:T_CB + P]]
        ident = tab[:, T_ID:T_ID + P]
        conv_wp = par[:, Q_CW:Q_CW + 64].rearrange("p (j k) -> p j k", j=4)

        s_in = sem("inputs_landed")
        s_par = sem("params_landed")
        landed = [sem(f"raw_landed{i}") for i in range(RAW)]
        hi_ready = sem("w_hi_ready")
        lo_ready = sem("w_lo_ready")
        half_done = sem("half_multiplied")
        bank_free = [sem("bank0_free"), sem("bank1_free")]
        x_turned = sem("x_transposed")
        c_ready = sem("c_silu_ready")
        c_split = sem("c_split")
        x_ready = sem("x_ready")
        par_turned = sem("params_transposed")
        ada_ready = sem("ada_ready")
        sq_ready = sem("squares_ready")
        ss_ready = sem("sumsq_ready")
        sd_ready = sem("std_ready")
        hn_ready = sem("normed_ready")
        h32_ready = sem("h_ready")
        h_split = sem("h_split")
        rot_in = sem("rotary_products")
        rot_out = sem("rotary_done")
        xpad_ready = sem("conv_input_ready")
        conv_ready = sem("conv_ready")
        xbc_ready = sem("xbc_ready")
        dtx_ready = sem("dt_input_ready")
        dte_ready = sem("dt_exp_ready")
        da_ready = sem("dA_ready")
        cs_ps = sem("cumsum_in_psum")
        cs_ready = sem("cumsum_ready")
        sc_ps = sem("scores_in_psum")
        mret_ready = sem("retention_weights_ready")
        max_ready = sem("attention_max_ready")
        p_ready = sem("attention_exp_ready")
        pv_ret = sem("retention_out_in_psum")
        pt_ps = sem("attention_probs_turned")
        pt_ready = sem("attention_probs_copied")
        yret_ready = sem("retention_out_ready")
        s2_ps = sem("attention_out_xs_cb_in_psum")
        s2_ready = sem("attention_out_xs_cb_ready")
        csb_ps = sem("cumsum_rows_in_psum")
        seg_ready = sem("segments_ready")
        dec_ready = sem("decay_ready")
        mssd_ready = sem("ssd_weights_ready")
        y_ps = sem("ssd_out_in_psum")
        yssd_ready = sem("ssd_out_ready")
        ssq_ready = sem("group_stats_ready")
        gsd_ready = sem("group_std_ready")
        ynorm_ready = sem("branch_normed")
        yt_ps = sem("branch_turned")
        yt_hi = sem("branch_hi_ready")
        yt_lo = sem("branch_lo_ready")
        mix_ready = sem("mixed_ready")
        mix_hi = sem("mixed_hi_ready")
        mix_lo = sem("mixed_lo_ready")
        sil_ready = sem("silu_ready")
        hid_ready = sem("hidden_ready")
        hid_hi = sem("hidden_hi_ready")
        hid_lo = sem("hidden_lo_ready")
        ff2_done = sem("ffn_out_in_psum")
        out_turned = sem("out_transposed")
        out_ready = sem("out_ready")
        stored = sem("out_stored")

        rearr = {
            "ada": ada_w, "in": w_in, "ret": w_br_ret, "ssm": w_br_ssm, "att": w_br_att,
            "out": w_out, "ff1": w_ff1, "ff3": w_ff3, "ff2": w_ff2,
        }
        w_dram = {k: v.rearrange("l (k p) n -> p (l k) n", p=P) for k, v in rearr.items()}

        def n_landed(l, u):
            return l * (16 * UNITS // RAW) + u.over(RAW, 16, 16)

        def n_half(l, u, h):
            return l * (2 * UNITS) + u.over(1, 2, h + 1)

        def n_bank(l, u):
            return l * (UNITS // 2) + u.over(2, 1, 1)

        FREE_HALVES = 2 * SPL
        FREE_RAW = 2 * RAW

        def parts(u, cn, h, dst, src, lead=None):
            half = slice(h * HALF, h * HALF + cn // 2)
            from_raw = slice(h * cn // 2, (h + 1) * cn // 2)
            if u.j is None and U_QK <= u.base < U_QK + N_QK:
                for b in range(2):
                    def at_b(v, pattern, **n):
                        return v[:, half].rearrange(pattern, **n)[:, :, :, b, :]
                    raw_order = dict(a=2, b=2, c=RQK // 2)
                    out = dst[:, half].rearrange("p (k b a c) -> p k b a c", b=2, a=2, c=RQK // 2)[:, :, b, :, :]
                    ops = [out, at_b(src, "p (k a b c) -> p k a b c", **raw_order)]
                    if lead is not None:
                        ops.append(lead[:, half].rearrange("p (k b a c) -> p k b a c", b=2, a=2,
                                                           c=RQK // 2)[:, :, b, :, :])
                    yield ops
            else:
                yield [dst[:, half], src[:, from_raw]] + ([lead[:, half]] if lead is not None else [])

        block = ctx.enter_context(nc.Block())

        @block.sync
        def _(sp):
            with sp.Fori(0, L) as l:
                r = rows[:, 0, :]
                pieces = [(ada_b, 48, Q_ADAB), (norm1_w, 8, Q_N1), (norm2_w, 8, Q_N2),
                          (ssm_norm_w, 8, Q_SN), (conv_b, 16, Q_CB)]
                for src, n, q in pieces:
                    sp.dma_start(r[q:q + n, :], src.rearrange("l (k p) -> (l k) p", p=P)[bass.ds(l * n, n), :])\
                      .then_inc(s_par, 16)
                sp.dma_start(rows[0:64, 1, :],
                             conv_w.rearrange("l j (k p) -> (l j k) p", p=P)[bass.ds(l * 64, 64), :])\
                  .then_inc(s_par, 16)
                for n, src in enumerate((dt_bias, a_log, ssm_d)):
                    sp.dma_start(rowv[0:1, n * SH:(n + 1) * SH], src[bass.ds(l, 1), :]).then_inc(s_par, 16)

                def load(u, name, k0, kn, col, cn):
                    s = u.mod(RAW)
                    sp.wait_ge(lo_ready, n_half(l, u, 1))
                    dst = raw[:, s, 0:kn * cn].rearrange("p (k n) -> p k n", k=kn)
                    sp.dma_start(dst, w_dram[name][:, bass.ds(k0, kn), bass.ds(col, cn)])\
                      .then_inc(landed[s], 16)

                def cols(name, first):
                    return lambda u, i: load(u, name, l * KB, KB, i.over(1, COL, first), COL)

                units(sp, U_ADA, N_ADA, 4, cols("ada", 0))
                units(sp, U_QK, N_QK, 4, cols("in", C_QK))
                units(sp, U_XBC, N_XBC, 4, cols("in", C_XBC))
                units(sp, U_AQK, N_AQK, 4, cols("in", C_AQK))

                def tok_ada(u, i):
                    if i.base % 2 == 0:
                        load(u, "in", l * KB, KB, i.over(2, COL, C_TOK), COL)
                    else:
                        load(u, "ada", l * KB, KB, i.over(2, COL, 12 * COL), COL)
                units(sp, U_TOK, N_TOK, 4, tok_ada)
                units(sp, U_AV, N_AV, 4, cols("in", C_AV))
                load(Unit(U_DT), "in", l * KB, KB, C_DT, SH)

                def mix(u, i):
                    if i.base % 4 < 3:
                        load(u, "in", l * KB, KB, i.over(4, 3 * COL, C_GATE + i.base % 4 * COL), COL)
                    else:
                        load(u, "ada", l * KB, KB, i.over(4, COL, 8 * COL), COL)
                units(sp, U_MIX, N_MIX, 4, mix)
                units(sp, U_BR, 4, 4, cols("ret", 0))
                units(sp, U_BR + 4, 4, 4, cols("ssm", 0))
                load(Unit(U_ATT), "att", l * 2, 2, 0, D)
                units(sp, U_OUT, N_OUT, 4, cols("out", 0))

                def ff(u, i):
                    load(u, "ff3" if i.base % 2 else "ff1", l * KB, KB, i.over(2, COL, 0), COL)
                units(sp, U_FF, N_FF, 4, ff)
                units(sp, U_FF2, N_FF2, 4, lambda u, i: load(u, "ff2", l * FB + i.over(1, 2, 0), 2, 0, D))
            sp.wait_ge(out_ready, 1)
            sp.dma_start(out.rearrange("a (t p) n -> p (a t) n", p=P), x_tok[:, :, :]).then_inc(stored, 16)
            sp.wait_ge(stored, 16)

        @block.tensor
        def _(pe):
            pe.sem_inc(half_done, FREE_HALVES)

            def weights(src, s, cn):
                return src[:, s, 0:2 * HALF].rearrange("p (k n) -> p k n", n=cn)

            def three(o, hi, lo, xh, xl, first, last, swap=False, skip=False):
                ps = [(hi, xh), (hi, xl), (lo, xh)]
                if swap:
                    ps = [(xh, hi), (xh, lo), (xl, hi)]
                for n, (a, b) in enumerate(ps):
                    done = pe.matmul(o, a, b, start=first and n == 0, stop=last and n == 2,
                                     skip_group_check=skip)
                return done

            def two_halves(l, u, body, own_bank=True):
                s = u.mod(SPL)
                for h in range(2):
                    pe.wait_ge(lo_ready, n_half(l, u, FREE_RAW + h))
                    if h == 0 and own_bank:
                        pe.wait_ge(bank_free[u.mod(2)], n_bank(l, u))
                    body(s, h).then_inc(half_done, 1)
                if not own_bank:
                    pe.sem_inc(bank_free[u.mod(2)], 1)

            def feature(l, u, ah=h_hi, al=h_lo, k0=0):
                def body(s, h):
                    hi, lo = weights(w_hi, s, COL), weights(w_lo, s, COL)
                    for m in range(2):
                        o = bank[u.mod(2)][:, m * S:(m + 1) * S]
                        for k in range(h * 4, h * 4 + 4):
                            a = [w[:, k, m * P:(m + 1) * P] for w in (hi, lo)]
                            last = three(o, a[0], a[1], ah[:, k0 + k, :], al[:, k0 + k, :],
                                         k == 0 and m == 0, k == KB - 1, skip=True)
                    return last
                two_halves(l, u, body)

            def token(l, u, cn=COL):
                def body(s, h):
                    hi, lo = (w[:, s, h * HALF:h * HALF + KB * cn // 2].rearrange("p (k n) -> p k n", n=cn)
                              for w in (w_hi, w_lo))
                    for t in range(NT):
                        o = bank[u.mod(2)][:, t * S:t * S + cn]
                        for k in range(h * 4, h * 4 + 4):
                            tk = slice(t * P, (t + 1) * P)
                            last = three(o, hi[:, k % 4, :], lo[:, k % 4, :], h_hi[:, k, tk], h_lo[:, k, tk],
                                         k == 0 and t == 0, k == KB - 1, swap=True, skip=True)
                    return last
                two_halves(l, u, body)

            def adaln(l, u):
                def body(s, h):
                    for m in range(2):
                        o = bank[u.mod(2)][:, 2 * m:2 * m + 2]
                        for k in range(h * 4, h * 4 + 4):
                            for n, w in enumerate((w_hi, w_lo)):
                                a = weights(w, s, COL)[:, k, m * P:(m + 1) * P]
                                last = pe.matmul(o, a, cc[:, k, :], start=k == 0 and m == 0 and n == 0,
                                                 stop=k == KB - 1 and n == 1, skip_group_check=True)
                    return last
                two_halves(l, u, body)

            def whole_rows(l, u, ah, al, k0, first, last_unit):
                def body(s, h):
                    hi, lo = weights(w_hi, s, D), weights(w_lo, s, D)
                    for m in range(KB):
                        o = bank[4 + m // 2][:, m % 2 * S:(m % 2 + 1) * S]
                        last = three(o, hi[:, h, m * P:(m + 1) * P], lo[:, h, m * P:(m + 1) * P],
                                     ah(k0, h), al(k0, h), first and h == 0 and m % 2 == 0,
                                     last_unit and h == 1, skip=True)
                    return last
                two_halves(l, u, body, own_bank=False)

            def norm_sum(n):
                pe.wait_ge(sq_ready, n)
                for k in range(KB):
                    last = pe.matmul(bank[2][:, 0:S], ones, sq[:, k, :], start=k == 0, stop=k == KB - 1)
                last.then_inc(ss_ready, 1)

            pe.wait_ge(s_in, 16 * 5)
            for k in range(KB):
                for t in range(NT):
                    pe.transpose(bank[2 + k // 2][:, k % 2 * S + t * P:k % 2 * S + (t + 1) * P],
                                 x_tok[:, t, k * P:(k + 1) * P], ident)
            pe.transpose(bank[6][:, 0:16], crow[:, :], ident[0:16, 0:16]).then_inc(x_turned, 1)

            with pe.Fori(0, L) as l:
                pe.wait_ge(s_par, l * 144 + 144)
                pe.wait_ge(x_ready, l * 2 + 1)
                pe.transpose(bank[3][:, 0:N_ROW0], rows[0:N_ROW0, 0, :], ident[0:N_ROW0, 0:N_ROW0])
                pe.transpose(bank[3][:, Q_CW:Q_CW + 64], rows[0:64, 1, :], ident[0:64, 0:64])
                pe.matmul(bank[3][:, Q_DTB:Q_END], ones[0:1, :], rowv[:, :], start=True, stop=True)\
                  .then_inc(par_turned, 1)
                norm_sum(l * 2 + 1)
                pe.wait_ge(c_split, 1)
                units(pe, U_ADA, N_ADA, 4, lambda u, i: adaln(l, u))
                pe.wait_ge(h_split, l * 2 + 1)
                units(pe, U_QK, N_QK, 4, lambda u, i: feature(l, u))
                units(pe, U_XBC, N_XBC, 4, lambda u, i: feature(l, u))
                units(pe, U_AQK, N_AQK, 2, lambda u, i: feature(l, u))
                units(pe, U_TOK, N_TOK, 4, lambda u, i: token(l, u) if i.base % 2 == 0 else adaln(l, u))
                for i in range(N_AV):
                    token(l, Unit(U_AV + i))
                token(l, Unit(U_DT), SH)

                def s_scores(j):
                    n = l * 4 + j + 1
                    q0, pr = j % 2 * 64, j // 2
                    hd = slice(q0, q0 + 64)
                    if j == 0:
                        pe.wait_ge(rot_out, l * 4 + 4)
                    else:
                        pe.wait_ge(seg_ready, n - 1)
                    for t in range(NT):
                        for b in range(2):
                            pe.matmul(bank[2][:, t * S:t * S + S - t * P],
                                      qk[hd, 2 + pr, b, t * P:(t + 1) * P], qk[hd, pr, b, t * P:S],
                                      start=b == 0, stop=b == 1)
                    for g in range(AG):
                        pe.matmul(bank[5][:, g * P:(g + 1) * P], aqk[hd, 2 * g + pr, 0:P],
                                  aqk[hd, 6 + 2 * g + pr, 0:P], start=True, stop=True)
                    for g in range(AG):
                        last = pe.matmul(bank[6 + g // 2][:, g % 2 * S:(g % 2 + 1) * S],
                                         aqk[hd, 2 * g + pr, P:S], aqk[hd, 6 + 2 * g + pr, :],
                                         start=True, stop=True)
                    last.then_inc(sc_ps, 1)

                def s_ret_out_and_turn(j):
                    n = l * 4 + j + 1
                    pe.wait_ge(mret_ready, n)
                    v = [tok[:, 0, t, j * RV:(j + 1) * RV] for t in range(NT)]
                    pe.matmul(bank[2][:, 0:S], m_ret[:, 0:P], v[0], start=True, stop=True)
                    pe.matmul(bank[2][:, S:2 * S], m_ret[:, P:2 * P], v[0], start=True, stop=False)
                    pe.matmul(bank[2][:, S:2 * S], m_ret[:, 2 * P:3 * P], v[1], start=False, stop=True)\
                      .then_inc(pv_ret, 1)
                    pe.wait_ge(p_ready, n)
                    for i in range(9):
                        last = pe.transpose(bank[5 + i // 4][:, i % 4 * P:(i % 4 + 1) * P],
                                            att_s[:, i * P:(i + 1) * P], ident)
                    last.then_inc(pt_ps, 1)

                def s_att_out_xs_cb(j):
                    n = l * 4 + j + 1
                    pe.wait_ge(pt_ready, n)

                    def value(g, t):
                        hcol = (g * AS + j) * AHD
                        return av[:, t, hcol:hcol + AHD]
                    for g in range(AG):
                        pe.matmul(bank[5][:, 0:AHD], p_t[:, g, :], value(g, 0), start=g == 0, stop=g == AG - 1)
                    for i in range(6):
                        pe.matmul(bank[5][:, AHD:2 * AHD], p_t[:, 3 + i, :], value(i // 2, i % 2),
                                  start=i == 0, stop=i == 5)
                    if j == 0:
                        pe.wait_ge(xbc_ready, l * N_XBC + N_XBC)
                    else:
                        pe.wait_ge(yssd_ready, n - 1)
                    for t in range(NT):
                        for b in range(2):
                            pe.transpose(bank[6][:, t * S + b * P:t * S + (b + 1) * P],
                                         xbc[:, 2 * j + b, t * P:(t + 1) * P], ident)
                    pe.matmul(bank[3][:, 0:S], xbc[:, 8 + j, 0:P], xbc[:, 12 + j, :], start=True, stop=True)
                    pe.matmul(bank[3][:, S:S + P], xbc[:, 8 + j, P:S], xbc[:, 12 + j, P:S],
                              start=True, stop=True).then_inc(s2_ps, 1)

                def s_cumsum_rows(j):
                    for r in range(4):
                        h = 4 * j + r
                        last = pe.matmul(bank[7 if r < 2 else 4][:, r % 2 * S:(r % 2 + 1) * S],
                                         sel[:, h * P:(h + 1) * P], csr[:, :], start=True, stop=True)
                    last.then_inc(csb_ps, 1)

                def s_ssd_out(j):
                    n = l * 4 + j + 1
                    pe.wait_ge(mssd_ready, n)
                    for r in range(4):
                        pc = slice(r * SHD, (r + 1) * SHD)
                        pe.matmul(bank[3][:, r * SHD:(r + 1) * SHD], decay[:, r, 0:P], xdt[:, 0, pc],
                                  start=True, stop=True)
                        o = bank[3][:, S + r * SHD:S + (r + 1) * SHD]
                        pe.matmul(o, decay[:, r, P:2 * P], xdt[:, 0, pc], start=True, stop=False)
                        last = pe.matmul(o, decay[:, r, 2 * P:3 * P], xdt[:, 1, pc], start=False, stop=True)
                    last.then_inc(y_ps, 1)

                pe.wait_ge(da_ready, l + 1)
                for t in range(NT):
                    pe.matmul(bank[3][:, t * SH:(t + 1) * SH], tri[t], d_a[:, t, :], start=True, stop=True)
                for t in range(NT):
                    last = pe.matmul(bank[4][0:SH, t * P:(t + 1) * P], d_a[:, t, :], tri[t],
                                     start=True, stop=True)
                last.then_inc(cs_ps, 1)
                for j in range(4):
                    u = Unit(U_MIX + 4 * j)
                    feature(l, u)
                    if j:
                        s_ssd_out(j - 1)
                    else:
                        pe.wait_ge(cs_ready, l + 1)
                    s_scores(j)
                    feature(l, u.plus(1))
                    s_ret_out_and_turn(j)
                    feature(l, u.plus(2))
                    s_att_out_xs_cb(j)
                    adaln(l, u.plus(3))
                    pe.wait_ge(s2_ready, l * 4 + j + 1)
                    s_cumsum_rows(j)
                s_ssd_out(3)

                for i in range(9):
                    if i in (0, 4):
                        pe.wait_ge(ynorm_ready, l * 2 + i // 4 + 1)
                    if i >= 6:
                        pe.wait_ge(yt_lo, l * 9 + i - 5)
                    for b in range(2):
                        for t in range(NT):
                            src = (yatt[:, t, b * P:(b + 1) * P] if i == 8 else
                                   tok[:, i // 4 * 2, t, (i % 4 * 2 + b) * P:(i % 4 * 2 + b + 1) * P])
                            last = pe.transpose(bank[2 + i % 6][:, b * S + t * P:b * S + (t + 1) * P],
                                                src, ident)
                    last.then_inc(yt_ps, 1)
                pe.wait_ge(yt_lo, l * 9 + 9)
                for i in range(8):
                    feature(l, Unit(U_BR + i), y_hi, y_lo, i // 4 * KB)
                whole_rows(l, Unit(U_ATT), lambda k, h: y_hi[:, 16 + h, :], lambda k, h: y_lo[:, 16 + h, :],
                           0, True, True)
                pe.wait_ge(mix_lo, l + 1)
                for i in range(N_OUT):
                    feature(l, Unit(U_OUT + i), m_hi, m_lo)
                norm_sum(l * 2 + 2)

                def ffn_in(u, i):
                    if i.base % 4 == 0:
                        pe.wait_ge(h_split, l * 2 + 2)
                    feature(l, u)
                units(pe, U_FF, N_FF, 4, ffn_in)
                pe.wait_ge(hid_lo, l * (N_FF // 2) + N_FF // 2)

                def hidden(f):
                    return lambda k, h: f[:, k * 2 + h, :]
                for i in range(N_FF2):
                    whole_rows(l, Unit(U_FF2 + i), hidden(f_hi), hidden(f_lo), i, i == 0, i == N_FF2 - 1)

            norm_sum(2 * L + 1)
            pe.wait_ge(h32_ready, 2 * L + 1)
            for k in range(KB):
                for t in range(NT):
                    last = pe.transpose(bank[2 + t + 2 * (k // 4)][:, k % 4 * P:(k % 4 + 1) * P],
                                        hn[:, k, t * P:(t + 1) * P], ident)
            last.then_inc(out_turned, 1)

        @block.scalar
        def _(act):
            act.dma_start(tab[:, :], table).then_inc(s_in, 16)
            act.dma_start(x_tok[:, :, :], x.rearrange("a (t p) n -> p (a t) n", p=P)).then_inc(s_in, 16)
            act.dma_start(crow[0:8, :], c.rearrange("a (k p) -> (a k) p", p=P)).then_inc(s_in, 16)
            act.dma_start(crow[8:16, :], final_norm_w.rearrange("(k p) -> k p", p=P)).then_inc(s_in, 16)
            act.dma_start(sel[:, :], select).then_inc(s_in, 16)

            def hi(l, u, cn=2 * HALF):
                s, r = u.mod(SPL), u.mod(RAW)
                act.wait_ge(landed[r], n_landed(l, u))
                for h in range(2):
                    act.wait_ge(half_done, n_half(l, u, h))
                    for dst, src in parts(u, cn, h, w_hi[:, s, :], raw[:, r, :]):
                        last = act.activation(dst, src, ACT.Copy)
                    last.then_inc(hi_ready, 1)

            def size(u):
                return KB * SH if u.j is None and u.base == U_DT else 2 * HALF

            def ahead(l, u):
                v = u.plus(2)
                if v.j is not None or v.base < UNITS:
                    hi(l, v, size(v))

            def result(l, u):
                act.wait_ge(half_done, n_half(l, u, 1 + FREE_HALVES))
                return bank[u.mod(2)]

            def squares(n):
                act.wait_ge(x_ready, n)
                act.activation(sq[:, :, :], xf[:, :, :], ACT.Square).then_inc(sq_ready, 1)

            def std(n):
                act.wait_ge(ss_ready, n)
                act.activation(rstd[:, :], bank[2][:, 0:S], ACT.Sqrt, bias=eps[:, 0:1], scale=1.0 / D)\
                   .then_inc(sd_ready, 1)

            def modulate(n, a, sh):
                act.wait_ge(hn_ready, n)
                act.wait_ge(ada_ready, n)
                for k in range(KB):
                    act.activation(hn[:, k, :], hn[:, k, :], ACT.Identity, bias=ada[:, sh + k:sh + k + 1],
                                   scale=a1[:, a, k:k + 1])
                act.drain()
                act.activation(h_hi[:, :, :], hn[:, :, :], ACT.Copy).then_inc(h32_ready, 1)

            act.wait_ge(x_turned, 1)
            act.activation(c32[:, :], bank[6][:, 0:8], ACT.Silu)
            act.drain()
            act.activation(cc[:, :, 0], c32[:, :], ACT.Copy).then_inc(c_ready, 1)

            with act.Fori(0, L) as l:
                hi(l, Unit(0))
                hi(l, Unit(1))
                squares(l * 2 + 1)
                std(l * 2 + 1)
                for i in range(N_ADA):
                    ahead(l, Unit(i))
                modulate(l * 2 + 1, 0, 0)
                for i in range(N_QK):
                    ahead(l, Unit(U_QK + i))

                def silu_xbc(i):
                    act.wait_ge(conv_ready, l * N_XBC + i.over(1, 1, 1))
                    v = xbc[:, bass.ds(i.over(1, 2, 0), 2), :]
                    act.activation(v, v, ACT.Silu).then_inc(xbc_ready, 1)

                def conv_in(u, i):
                    ahead(l, u)
                    b = result(l, u)
                    act.activation(xpad[:, u.mod(2), :, 3:S + 3], b[:, :].rearrange("p (m t) -> p m t", m=2),
                                   ACT.Copy).then_inc(bank_free[u.mod(2)], 1)
                act.wait_ge(xpad_ready, l + 1)
                conv_in(Unit(U_XBC), Unit(0))
                for i in range(1, N_XBC):
                    silu_xbc(Unit(i - 1))
                    conv_in(Unit(U_XBC + i), Unit(i))
                silu_xbc(Unit(N_XBC - 1))

                def copy_aqk(u, i):
                    ahead(l, u)
                    b = result(l, u)
                    act.activation(aqk[:, 2 * i.base:2 * i.base + 2, :],
                                   b[:, :].rearrange("p (m t) -> p m t", m=2), ACT.Copy)\
                       .then_inc(bank_free[u.mod(2)], 1)
                for i in range(N_AQK):
                    copy_aqk(Unit(U_AQK + i), Unit(i))
                for i in range(N_TOK):
                    u = Unit(U_TOK + i)
                    ahead(l, u)
                    if i % 2 == 0:
                        b, w = result(l, u), i // 2
                        act.activation(tok[:, w // 4, :, w % 4 * COL:(w % 4 + 1) * COL],
                                       b[:, :].rearrange("p (t n) -> p t n", t=NT),
                                       ACT.Silu if w >= 4 else ACT.Copy).then_inc(bank_free[u.mod(2)], 1)
                for i in range(N_AV):
                    u = Unit(U_AV + i)
                    ahead(l, u)
                    b = result(l, u)
                    act.activation(av[:, :, i * COL:(i + 1) * COL], b[:, :].rearrange("p (t n) -> p t n", t=NT),
                                   ACT.Copy).then_inc(bank_free[u.mod(2)], 1)
                ahead(l, Unit(U_DT))
                act.wait_ge(dtx_ready, l + 1)
                act.activation(dt_e[:, :], dt_e[:, :], ACT.Exp, scale=-1.0)
                act.activation(exp_a[:, :], par[:, Q_ALOG:Q_ALOG + SH], ACT.Exp)
                act.drain()
                act.activation(dt_e[:, :], dt_e[:, :], ACT.Ln, bias=one[:, 0:1]).then_inc(dte_ready, 1)

                def gate(u, g):
                    ahead(l, u)
                    b = result(l, u)
                    act.activation(gates[:, 2 * g:2 * g + 2, :], b[:, :].rearrange("p (m t) -> p m t", m=2),
                                   ACT.Tanh, scale=0.5).then_inc(bank_free[u.mod(2)], 1)

                def square_sums(j):
                    act.wait_ge(yssd_ready, l * 4 + j + 1)
                    for t in range(NT):
                        last = act.activation(junk, tok[:, 2, t, j * COL:(j + 1) * COL], ACT.Square,
                                              accum_out=ss[:, j, t:t + 1])
                        if t == 0:
                            act.drain()
                    last.then_inc(ssq_ready, 1)

                for j in range(4):
                    n = l * 4 + j + 1
                    u = Unit(U_MIX + 4 * j)
                    gate(u, 3 * j)
                    act.wait_ge(max_ready, n)
                    act.activation(att_s[:, 0:384], att_s[:, 0:384], ACT.Exp, bias=negmax[:, 0:1],
                                   accum_out=ssum[:, 0:1])
                    act.activation(att_s[:, 384:1152], att_s[:, 384:1152], ACT.Exp, bias=negmax[:, 1:2],
                                   accum_out=ssum[:, 1:2]).then_inc(p_ready, 1)
                    gate(u.plus(1), 3 * j + 1)
                    act.wait_ge(pt_ps, n)
                    act.activation(p_t[:, 0:4, :], bank[5][:, :].rearrange("p (i n) -> p i n", i=4), ACT.Copy)
                    act.activation(p_t[:, 4:8, :], bank[6][:, :].rearrange("p (i n) -> p i n", i=4), ACT.Copy)
                    act.activation(p_t[:, 8, :], bank[7][:, 0:P], ACT.Copy).then_inc(pt_ready, 1)
                    if j:
                        square_sums(j - 1)
                    gate(u.plus(2), 3 * j + 2)
                    ahead(l, u.plus(3))
                    act.wait_ge(seg_ready, n)
                    act.activation(decay[:, :, :], decay[:, :, :], ACT.Exp).then_inc(dec_ready, 1)
                square_sums(3)
                act.wait_ge(ssq_ready, l * 4 + 4)
                act.wait_ge(yssd_ready, l * 4 + 4)
                act.activation(sd[:, 0, :], mv[:, :, :, 1].rearrange("p h t -> p (h t)"), ACT.Sqrt,
                               bias=eps[:, 0:1])
                act.activation(sd[:, 1, :], ss[:, :, :].rearrange("p h t -> p (h t)"), ACT.Sqrt,
                               bias=eps[:, 0:1], scale=1.0 / COL).then_inc(gsd_ready, 1)
                for i in range(9):
                    act.wait_ge(yt_ps, l * 9 + i + 1)
                    b = bank[2 + i % 6]
                    if i // 4 == 1:
                        for m in range(2):
                            k = (i - 4) * 2 + m
                            last = act.activation(y_hi[:, 2 * i + m, :], b[:, m * S:(m + 1) * S], ACT.Copy,
                                                  scale=par[:, Q_SN + k:Q_SN + k + 1])
                    else:
                        last = act.activation(y_hi[:, 2 * i:2 * i + 2, :],
                                              b[:, :].rearrange("p (m t) -> p m t", m=2), ACT.Copy)
                    last.then_inc(yt_hi, 1)
                for i in range(9):
                    ahead(l, Unit(U_BR + i))
                act.wait_ge(mix_ready, l + 1)
                act.activation(m_hi[:, :, :], mixed[:, :, :], ACT.Copy).then_inc(mix_hi, 1)
                for i in range(N_OUT):
                    ahead(l, Unit(U_OUT + i))
                squares(l * 2 + 2)
                std(l * 2 + 2)
                modulate(l * 2 + 2, 1, 24)

                def hidden_hi(i):
                    act.wait_ge(hid_ready, l * (N_FF // 2) + i.over(2, 1, 0))
                    act.activation(f_hi[:, bass.ds(i.over(2, 2, -2), 2), :],
                                   hid[:, :].rearrange("p (m t) -> p m t", m=2), ACT.Copy).then_inc(hid_hi, 1)

                def ffn(u, i, first=False):
                    ahead(l, u)
                    if i.base % 2 == 0:
                        if not first:
                            hidden_hi(i)
                        b = result(l, u)
                        act.activation(sil[:, :], b[:, :], ACT.Silu).then_inc(sil_ready, 1)
                ffn(Unit(U_FF), Unit(0), True)
                ffn(Unit(U_FF + 1), Unit(1), True)
                units_from(act, U_FF, 2, N_FF, 4, ffn)
                hidden_hi(Unit(N_FF))
                for i in range(N_FF2):
                    ahead(l, Unit(U_FF2 + i))
            squares(2 * L + 1)
            std(2 * L + 1)
            act.wait_ge(hn_ready, 2 * L + 1)
            for k in range(KB):
                last = act.activation(hn[:, k, :], hn[:, k, :], ACT.Copy, scale=fnw[:, k:k + 1])
            last.then_inc(h32_ready, 1)

        @block.vector
        def _(dve):
            dve.sem_inc(lo_ready, FREE_RAW)
            dve.sem_inc(bank_free[0], 1)
            dve.sem_inc(bank_free[1], 1)
            dve.memset(eps[:, :], EPS)
            dve.memset(one[:, :], 1.0)

            def lo(l, u, cn=2 * HALF):
                s, r = u.mod(SPL), u.mod(RAW)
                for h in range(2):
                    dve.wait_ge(hi_ready, n_half(l, u, h))
                    for dst, src, lead in parts(u, cn, h, w_lo[:, s, :], raw[:, r, :],
                                                w_hi[:, s, :].bitcast(F32)):
                        last = dve.tensor_tensor(dst, src, lead, ALU.subtract)
                    last.then_inc(lo_ready, 1)

            def size(u):
                return KB * SH if u.j is None and u.base == U_DT else 2 * HALF

            def ahead(l, u):
                v = u.plus(2)
                if v.j is not None or v.base < UNITS:
                    lo(l, v, size(v))

            def result(l, u):
                dve.wait_ge(half_done, n_half(l, u, 1 + FREE_HALVES))
                return bank[u.mod(2)]

            def normed(n):
                dve.wait_ge(sd_ready, n)
                dve.reciprocal(rstd[:, :], rstd[:, :])
                dve.drain()
                dve.tensor_tensor(hn[:, :, :], xf[:, :, :], rstd[:, None, :].to_broadcast([P, KB, S]),
                                  ALU.mult).then_inc(hn_ready, 1)

            def split_h(n):
                dve.wait_ge(h32_ready, n)
                dve.tensor_tensor(h_lo[:, :, :], hn[:, :, :], h_hi[:, :, :].bitcast(F32), ALU.subtract)\
                   .then_inc(h_split, 1)

            def ada_sum(l, u, col):
                b = result(l, u)
                dve.tensor_reduce(ada[:, col:col + 2], b[:, 0:4].rearrange("p (m n) -> p m n", m=2), AXX,
                                  ALU.add).then_inc(bank_free[u.mod(2)], 1)

            def ada_bias(lo_, hi_):
                dve.drain()
                dve.tensor_tensor(ada[:, lo_:hi_], ada[:, lo_:hi_], par[:, Q_ADAB + lo_:Q_ADAB + hi_], ALU.add)
                dve.drain()

            def norm_scale(a, sc, w):
                dve.scalar_tensor_tensor(out=a1[:, a, :], in0=ada[:, sc:sc + KB], scalar=1.0,
                                         in1=par[:, w:w + KB], op0=ALU.add, op1=ALU.mult)\
                   .then_inc(ada_ready, 1)

            dve.wait_ge(x_turned, 1)
            for i in range(4):
                dve.tensor_copy(xf[:, 2 * i:2 * i + 2, :], bank[2 + i][:, :].rearrange("p (m t) -> p m t", m=2))
            dve.wait_ge(c_ready, 1)
            dve.tensor_copy(fnw[:, :], bank[6][:, 8:16]).then_inc(x_ready, 1)
            dve.tensor_tensor(cc[:, :, 1], c32[:, :], cc[:, :, 0].bitcast(F32), ALU.subtract).then_inc(c_split, 1)

            with dve.Fori(0, L) as l:
                lo(l, Unit(0))
                lo(l, Unit(1))
                dve.wait_ge(par_turned, l + 1)
                dve.tensor_copy(par[:, :], bank[3][:, 0:Q_END])
                normed(l * 2 + 1)
                for i in range(N_ADA):
                    ahead(l, Unit(i))
                    ada_sum(l, Unit(i), 2 * i)
                ada_bias(0, 16)
                norm_scale(0, 8, Q_N1)
                split_h(l * 2 + 1)
                for i in range(N_QK):
                    u = Unit(U_QK + i)
                    ahead(l, u)
                    b = result(l, u)[:, :].rearrange("p (m t) -> p m t", m=2)
                    if i:
                        dve.wait_ge(rot_out, l * N_QK + i)
                    dve.tensor_tensor(rope_c[:, :, :], b, cos[:, None, :].to_broadcast([P, 2, S]), ALU.mult)
                    dve.tensor_tensor(rope_s[:, :, :], b, sin[:, None, :].to_broadcast([P, 2, S]), ALU.mult)\
                       .then_inc(bank_free[u.mod(2)], 1)
                dve.wait_ge(rot_out, l * N_QK + N_QK)
                dve.memset(xpad[:, :, :, 0:3], 0.0).then_inc(xpad_ready, 1)
                for i in range(N_XBC):
                    u = Unit(U_XBC + i)
                    ahead(l, u)
                    dve.wait_ge(bank_free[u.mod(2)], n_bank(l, u.plus(2)))
                    for t in range(3, -1, -1):
                        for m in range(2):
                            k = 2 * i + m
                            src = xpad[:, u.mod(2), m, t:t + S]
                            w = conv_wp[:, t, k:k + 1]
                            if t == 3:
                                last = dve.tensor_scalar(xbc[:, k, :], src, w, par[:, Q_CB + k:Q_CB + k + 1],
                                                         ALU.mult, ALU.add)
                            else:
                                last = dve.scalar_tensor_tensor(out=xbc[:, k, :], in0=src, scalar=w,
                                                                in1=xbc[:, k, :], op0=ALU.mult, op1=ALU.add)
                        if t:
                            dve.drain()
                    last.then_inc(conv_ready, 1)
                for i in range(N_AQK):
                    ahead(l, Unit(U_AQK + i))
                for i in range(N_TOK):
                    u = Unit(U_TOK + i)
                    ahead(l, u)
                    if i % 2:
                        ada_sum(l, u, 24 + i - 1)
                for i in range(N_AV):
                    ahead(l, Unit(U_AV + i))
                u = Unit(U_DT)
                ahead(l, u)
                b = result(l, u)
                dve.tensor_tensor(dt_x[:, :].rearrange("p (t h) -> p t h", t=NT),
                                  b[:, :].rearrange("p (t n) -> p t n", t=NT)[:, :, 0:SH],
                                  par[:, None, Q_DTB:Q_DTB + SH].to_broadcast([P, NT, SH]), ALU.add)\
                   .then_inc(bank_free[u.mod(2)], 1)
                dve.drain()
                dve.scalar_tensor_tensor(out=dt_e[:, :], in0=dt_x[:, :], scalar=-1.0, in1=dt_x[:, :],
                                         op0=ALU.mult, op1=ALU.max).then_inc(dtx_ready, 1)
                dve.wait_ge(dte_ready, l + 1)
                dt_flat = dt[:, :, :].rearrange("p t h -> p (t h)")
                dve.scalar_tensor_tensor(out=dt_flat, in0=dt_x[:, :], scalar=0.0, in1=dt_e[:, :],
                                         op0=ALU.max, op1=ALU.add)
                dve.drain()
                for t in range(NT):
                    last = dve.scalar_tensor_tensor(out=d_a[:, t, :], in0=dt[:, t, :], scalar=-1.0,
                                                    in1=exp_a[:, :], op0=ALU.mult, op1=ALU.mult)
                last.then_inc(da_ready, 1)
                dve.wait_ge(cs_ps, l + 1)
                dve.tensor_copy(cs[:, :, :], bank[3][:, 0:2 * SH].rearrange("p (t h) -> p t h", t=NT))
                dve.tensor_copy(csr[:, :], bank[4][0:SH, 0:S]).then_inc(cs_ready, 1)

                def ssd_out(j):
                    dve.wait_ge(y_ps, l * 4 + j + 1)
                    f = ytmp[:, :, :].rearrange("p t n -> p (t n)")
                    dve.tensor_tensor(f, bank[3][:, :], f, ALU.add)
                    dve.drain()
                    z = tok[:, 2, :, j * COL:(j + 1) * COL]
                    dve.tensor_tensor(z, z, ytmp[:, :, :], ALU.mult).then_inc(yssd_ready, 1)

                for j in range(4):
                    n = l * 4 + j + 1
                    u = Unit(U_MIX + 4 * j)
                    ahead(l, u)
                    if j:
                        ssd_out(j - 1)
                    dve.wait_ge(sc_ps, n)
                    dve.tensor_tensor(m_ret[:, 0:S], bank[2][:, 0:S], ret_mask[:, j, :], ALU.mult)
                    dve.tensor_tensor(m_ret[:, S:S + P], bank[2][:, S:S + P], ret_mask[:, j, 0:P], ALU.mult)\
                       .then_inc(mret_ready, 1)
                    a3 = att_s[:, :].rearrange("p (i n) -> p i n", n=P)
                    dve.scalar_tensor_tensor(out=a3[:, 0:3, :], in0=bank[5][:, 0:384].rearrange("p (g n) -> p g n", g=AG),
                                             scalar=AHD ** -0.5, in1=att_mask[:, :, P:S], op0=ALU.mult, op1=ALU.add)
                    dve.scalar_tensor_tensor(out=att_s[:, 384:896], in0=bank[6][:, :], scalar=AHD ** -0.5,
                                             in1=tab[:, T_ATT:T_ATT + 512], op0=ALU.mult, op1=ALU.add)
                    dve.scalar_tensor_tensor(out=att_s[:, 896:1152], in0=bank[7][:, 0:S], scalar=AHD ** -0.5,
                                             in1=att_mask[:, 2, :], op0=ALU.mult, op1=ALU.add)
                    dve.drain()
                    dve.tensor_reduce(rsum[:, 0:1], att_s[:, 0:384], AXX, ALU.max)
                    dve.tensor_reduce(rsum[:, 1:2], att_s[:, 384:1152], AXX, ALU.max)
                    dve.drain()
                    dve.tensor_scalar(negmax[:, :], rsum[:, :], -1.0, None, ALU.mult).then_inc(max_ready, 1)
                    ahead(l, u.plus(1))
                    dve.wait_ge(pv_ret, n)
                    for t in range(NT):
                        dve.bn_stats(bst[:, t, :], bank[2][:, t * S:(t + 1) * S])
                    dve.drain()
                    for t in range(NT):
                        dve.bn_aggr(mv[:, j, t, :], bst[:, t, :])
                    dve.drain()
                    for t in range(NT):
                        last = dve.tensor_scalar(tok[:, 0, t, j * RV:(j + 1) * RV], bank[2][:, t * S:(t + 1) * S],
                                                 mv[:, j, t, 0:1], None, ALU.subtract)
                    last.then_inc(yret_ready, 1)
                    ahead(l, u.plus(2))
                    dve.wait_ge(s2_ps, n)
                    dve.reciprocal(rsum[:, :], ssum[:, :])
                    dve.drain()
                    for t in range(NT):
                        dve.tensor_scalar(yatt[:, t, j * AHD:(j + 1) * AHD], bank[5][:, t * AHD:(t + 1) * AHD],
                                          rsum[:, t:t + 1], None, ALU.mult)
                    for t in range(NT):
                        xs = bank[6][:, t * S:(t + 1) * S].rearrange("p (r n) -> p r n", r=4)
                        dve.tensor_tensor(xdt[:, t, :].rearrange("p (r n) -> p r n", r=4), xs,
                                          dt[:, t, 4 * j:4 * j + 4, None].to_broadcast([P, 4, SHD]), ALU.mult)
                        dve.tensor_tensor(ytmp[:, t, :].rearrange("p (r n) -> p r n", r=4), xs,
                                          par[:, Q_DSK + 4 * j:Q_DSK + 4 * j + 4, None].to_broadcast([P, 4, SHD]),
                                          ALU.mult)
                    dve.tensor_tensor(cbm[:, :], bank[3][:, 0:384], cb_mask, ALU.mult).then_inc(s2_ready, 1)
                    ahead(l, u.plus(3))
                    ada_sum(l, u.plus(3), 16 + 2 * j)
                    dve.wait_ge(csb_ps, n)
                    for r in range(4):
                        h = 4 * j + r
                        b = bank[7 if r < 2 else 4][:, r % 2 * S:(r % 2 + 1) * S]
                        dve.tensor_scalar(decay[:, r, 0:S], b, cs[:, 0, h:h + 1], 0.0, ALU.subtract, ALU.min)
                        last = dve.tensor_scalar(decay[:, r, S:S + P], b[:, P:S], cs[:, 1, h:h + 1], 0.0,
                                                 ALU.subtract, ALU.min)
                    last.then_inc(seg_ready, 1)
                ssd_out(3)
                ada_bias(16, 48)
                dve.tensor_scalar(g1h[:, :], ada[:, 16:24], 0.5, None, ALU.mult)
                norm_scale(1, 32, Q_N2)
                dve.wait_ge(gsd_ready, l + 1)
                dve.reciprocal(ri[:, :, :], sd[:, :, :])
                dve.drain()
                for which in range(2):
                    for j in range(4):
                        for t in range(NT):
                            y = tok[:, 2 * which, t, j * COL:(j + 1) * COL]
                            r = ri[:, which, 2 * j + t:2 * j + t + 1]
                            if which == 0:
                                last = dve.scalar_tensor_tensor(out=y, in0=y, scalar=r,
                                                                in1=tok[:, 1, t, j * COL:(j + 1) * COL],
                                                                op0=ALU.mult, op1=ALU.mult)
                            else:
                                last = dve.tensor_scalar(y, y, r, None, ALU.mult)
                    last.then_inc(ynorm_ready, 1)
                for i in range(9):
                    dve.wait_ge(yt_hi, l * 9 + i + 1)
                    b = bank[2 + i % 6]
                    if i // 4 == 1:
                        for m in range(2):
                            k = (i - 4) * 2 + m
                            last = dve.scalar_tensor_tensor(out=y_lo[:, 2 * i + m, :], in0=b[:, m * S:(m + 1) * S],
                                                            scalar=par[:, Q_SN + k:Q_SN + k + 1],
                                                            in1=y_hi[:, 2 * i + m, :].bitcast(F32),
                                                            op0=ALU.mult, op1=ALU.subtract)
                    else:
                        last = dve.tensor_tensor(y_lo[:, 2 * i:2 * i + 2, :],
                                                 b[:, :].rearrange("p (m t) -> p m t", m=2),
                                                 y_hi[:, 2 * i:2 * i + 2, :].bitcast(F32), ALU.subtract)
                    last.then_inc(yt_lo, 1)

                def gated(ps, g, k, first):
                    gt = gates[:, g * KB + k:g * KB + k + 2, :].rearrange("p m t -> p (m t)")
                    mx = mixed[:, k:k + 2, :].rearrange("p m t -> p (m t)")
                    if first:
                        return dve.scalar_tensor_tensor(out=mx, in0=gt, scalar=1.0, in1=ps, op0=ALU.add,
                                                        op1=ALU.mult)
                    i = dve.scalar_tensor_tensor(out=br[:, :], in0=gt, scalar=1.0, in1=ps, op0=ALU.add,
                                                 op1=ALU.mult)
                    return i

                def add_branch(k):
                    dve.drain()
                    mx = mixed[:, k:k + 2, :].rearrange("p m t -> p (m t)")
                    i = dve.tensor_tensor(mx, mx, br[:, :], ALU.add)
                    dve.drain()
                    return i
                for i in range(8):
                    u = Unit(U_BR + i)
                    ahead(l, u)
                    b = result(l, u)
                    gated(b[:, :], i // 4, i % 4 * 2, i < 4).then_inc(bank_free[u.mod(2)], 1)
                    if i >= 4:
                        add_branch(i % 4 * 2)
                u = Unit(U_ATT)
                ahead(l, u)
                result(l, u)
                for i in range(4):
                    gated(bank[4 + i][:, :], 2, 2 * i, False)
                    last = add_branch(2 * i)
                last.then_inc(mix_ready, 1)
                dve.wait_ge(mix_hi, l + 1)
                dve.tensor_tensor(m_lo[:, :, :], mixed[:, :, :], m_hi[:, :, :].bitcast(F32), ALU.subtract)\
                   .then_inc(mix_lo, 1)
                for i in range(N_OUT):
                    u = Unit(U_OUT + i)
                    ahead(l, u)
                    b = result(l, u)
                    for m in range(2):
                        k = 2 * i + m
                        last = dve.scalar_tensor_tensor(out=xf[:, k, :], in0=b[:, m * S:(m + 1) * S],
                                                        scalar=g1h[:, k:k + 1], in1=xf[:, k, :],
                                                        op0=ALU.mult, op1=ALU.add)
                    last.then_inc(bank_free[u.mod(2)], 1)
                dve.drain().then_inc(x_ready, 1)
                normed(l * 2 + 2)
                split_h(l * 2 + 2)

                def hidden_lo(i):
                    dve.wait_ge(hid_hi, l * (N_FF // 2) + i.over(2, 1, 0))
                    v = bass.ds(i.over(2, 2, -2), 2)
                    dve.tensor_tensor(f_lo[:, v, :], hid[:, :].rearrange("p (m t) -> p m t", m=2),
                                      f_hi[:, v, :].bitcast(F32), ALU.subtract).then_inc(hid_lo, 1)

                def ffn(u, i, first=False):
                    ahead(l, u)
                    if i.base % 2 == 0:
                        if not first:
                            hidden_lo(i)
                        dve.wait_ge(sil_ready, l * (N_FF // 2) + i.over(2, 1, 1))
                        dve.sem_inc(bank_free[u.mod(2)], 1)
                    else:
                        b = result(l, u)
                        if not first:
                            dve.wait_ge(hid_lo, l * (N_FF // 2) + i.over(2, 1, 0))
                        dve.tensor_tensor(hid[:, :], b[:, :], sil[:, :], ALU.mult)\
                           .then_inc(bank_free[u.mod(2)], 1)
                        dve.drain().then_inc(hid_ready, 1)
                ffn(Unit(U_FF), Unit(0), True)
                ffn(Unit(U_FF + 1), Unit(1), True)
                units_from(dve, U_FF, 2, N_FF, 4, ffn)
                hidden_lo(Unit(N_FF))
                for i in range(N_FF2):
                    ahead(l, Unit(U_FF2 + i))
                result(l, Unit(U_FF2 + N_FF2 - 1))
                for k in range(KB):
                    last = dve.scalar_tensor_tensor(out=xf[:, k, :], in0=bank[4 + k // 2][:, k % 2 * S:(k % 2 + 1) * S],
                                                    scalar=ada[:, 40 + k:41 + k], in1=xf[:, k, :],
                                                    op0=ALU.mult, op1=ALU.add)
                last.then_inc(x_ready, 1)
            normed(2 * L + 1)
            dve.wait_ge(out_turned, 1)
            for t in range(NT):
                for q in range(2):
                    last = dve.tensor_copy(x_tok[:, t, q * 512:(q + 1) * 512], bank[2 + t + 2 * q][:, :])
            last.then_inc(out_ready, 1)

        @block.gpsimd
        def _(pool):
            with pool.Fori(0, L) as l:
                for i in range(N_QK):
                    u = Unit(U_QK + i)
                    pool.wait_ge(bank_free[u.mod(2)], n_bank(l, u.plus(2)))
                    pool.tensor_tensor(qk[:, i, 0, :], rope_c[:, 0, :], rope_s[:, 1, :], ALU.subtract)
                    pool.tensor_tensor(qk[:, i, 1, :], rope_s[:, 0, :], rope_c[:, 1, :], ALU.add)\
                        .then_inc(rot_out, 1)
                for j in range(SG):
                    pool.wait_ge(dec_ready, l * SG + j + 1)
                    pool.tensor_tensor(decay[:, :, :], decay[:, :, :],
                                       cbm[:, None, :].to_broadcast([P, 4, 384]), ALU.mult)\
                        .then_inc(mssd_ready, 1)


def units_from(eng, base, start, count, per, fn):
    full = (count - start) // per
    assert start + full * per == count
    with eng.Fori(0, full) as j:
        for b in range(per):
            fn(Unit(base + start + b, per, j), Unit(start + b, per, j))


def tables():
    f = np.float32
    t = np.zeros((P, T_END), f)
    half = RQK // 2
    inv = f(10000.0) ** (-np.arange(half, dtype=f) / f(half))
    ang = (np.arange(S, dtype=f)[None, :] * inv.astype(f)[:, None]).astype(f)
    t[:, T_COS:T_COS + S] = np.tile(np.cos(ang.astype(np.float64)), (2, 1))
    t[:, T_SIN:T_SIN + S] = np.tile(np.sin(ang.astype(np.float64)), (2, 1))
    key = np.arange(P, dtype=np.float64)[:, None]
    qry = np.arange(S, dtype=np.float64)[None, :]
    lg = np.log1p(-np.exp(np.linspace(np.log(1.0 / 32), np.log(1.0 / 512), RH)))
    for h in range(RH):
        m = np.where(qry >= key, np.exp((qry - key) * lg[h]), 0.0) * RQK ** -0.5
        t[:, T_RET + h * S:T_RET + (h + 1) * S] = m
    q = P + np.arange(P)[:, None]
    k = np.arange(S)[None, :]
    for g, (window, dil) in enumerate(((128, 1), (512, 4), (2048, 16))):
        ok = (q >= k) & ((q - k) % dil == 0) & (q - k <= window)
        t[:, T_ATT + g * S:T_ATT + (g + 1) * S] = np.where(ok, 0.0, -1e30)
    low = (np.arange(P)[None, :] >= np.arange(P)[:, None]).astype(f)
    t[:, T_CB:T_CB + P] = low
    t[:, T_CB + P:T_CB + 2 * P] = 1.0
    t[:, T_CB + 2 * P:T_CB + 3 * P] = low
    t[:, T_TRI:T_TRI + P] = low - 1.0
    t[:, T_ID:T_ID + P] = np.eye(P)
    return t, np.kron(np.eye(SH), np.ones((1, P))).astype(f)


_INS = ["x", "c", "ada_w", "ada_b", "norm1_w", "w_in", "ssm_conv_w", "ssm_conv_b", "ssm_dt_bias",
        "ssm_a_log", "ssm_d", "ssm_norm_w", "w_br_ret", "w_br_ssm", "w_br_att", "w_out", "norm2_w",
        "w_ff1", "w_ff3", "w_ff2", "final_norm_w"]


def kernel(**inputs):
    import numpy as _np
    import concourse.bacc as _bacc
    from concourse import mybir as _mybir
    from concourse.bass_utils import run_bass_kernel_spmd as _run

    nc = _bacc.Bacc("TRN2", target_bir_lowering=False, num_devices=1, dynamic_dma_scratch_size=1024)
    arrays, args = {}, []
    named = {name: _np.ascontiguousarray(inputs[name]) for name in _INS}
    named["table"], named["select"] = tables()
    for name, a in named.items():
        arrays[f"in_{name}_dram"] = a
        args.append(nc.dram_tensor(f"in_{name}_dram", a.shape, _mybir.dt.from_np(a.dtype), kind="ExternalInput").ap())
    args.append(nc.dram_tensor("out_0_dram", (1, S, D), _mybir.dt.float32, kind="ExternalOutput").ap())
    build(nc, *args)
    r = _run(nc, [arrays], core_ids=[0])
    return r.results[0]["out_0_dram"]
```

```python
from contextlib import ExitStack

import numpy as np
import concourse.bass as bass
from concourse import mybir

P = 128
D = 1024
KB = D // P
S = 256
NT = S // P
L = 2
EPS = 1e-6
RH, RQK, RV = 4, 128, 256
SH, SHD, SG = 16, 64, 4
AG, AS, AHD = 3, 4, 64
FF = 2816
FB = FF // P
COL = 256
HALF = KB * COL // 2
XBC = 2048
C_QK, C_TOK, C_XBC = 0, 1024, 4096
C_DT = C_XBC + XBC
C_AQK = C_DT + SH
C_AV = C_AQK + 2 * AG * AS * AHD
C_GATE = C_AV + AG * AS * AHD
EARLY, LATE = 8, 16
PLAN = [("ada", EARLY), ("qk", 3), ("ada", 1), ("qk", 1), ("xbc", 2), ("ada", 1)]
PLAN += [("xbc", 3), ("ada", 1)] * 2 + [("aqk", 3), ("ada", 1)] * 2 + [("tok", 3), ("ada", 1)] * 4
PLAN += [("dt", 1), ("av", 1), ("ada", 1), ("av", 2)] + [("gate", 2), ("ada", 1), ("gate", 1)] * 4
PLAN += [("ret", 1), ("ada", 1), ("ret", 3), ("att", 1), ("ssm", 4), ("out", 4), ("ff", 22), ("ff2", 11)]
KIND = [k for k, n in PLAN for _ in range(n)]
UNITS = len(KIND)
SPLIT_UNITS = [r for r, k in enumerate(KIND) if k != "ada"]
SPLITS = len(SPLIT_UNITS)
S_OF = {r: i for i, r in enumerate(SPLIT_UNITS)}
A_OF = {r: i for i, r in enumerate(r for r, k in enumerate(KIND) if k == "ada")}
ADAS = len(A_OF)
N_QK, N_XBC, N_AQK, N_TOK, N_AV, N_GATE = 4, 8, 6, 12, 3, 12
U_TOK, U_DT, U_ATT, U_SSM = (KIND.index(k) for k in ("tok", "dt", "att", "ssm"))
TOK_UNITS = KIND.index("dt") - U_TOK
U_OUT, N_OUT = KIND.index("out"), 4
U_FF, N_FF = KIND.index("ff"), 22
U_FF2, N_FF2 = KIND.index("ff2"), 11
assert UNITS % 4 == 0 and SPLITS % 2 == 0
RAW = 4
SPL = 2
BANK0 = 2

F32 = mybir.dt.float32
F32R = mybir.dt.float32r
ALU = mybir.AluOpType
ACT = mybir.ActivationFunctionType
AXX = mybir.AxisListType.X

T_COS, T_SIN, T_RET, T_ATT = 0, 256, 512, 1536
T_CB, T_TRI, T_ID = 2304, 2688, 2816
T_END = 2944
Q_ADAB, Q_N1, Q_N2, Q_SN, Q_CB = 0, 48, 56, 64, 72
Q_CW, Q_DTB, Q_ALOG, Q_DSK = 88, 152, 168, 184
Q_END = 200
N_ROW0 = 88


class Unit:

    def __init__(self, base, per=0, j=None, split_per=None):
        self.base, self.per, self.j = base, per, j
        self.split_per = per if split_per is None else split_per

    def plus(self, d):
        return Unit(self.base + d, self.per, self.j, self.split_per)

    def over(self, k, times=1, off=0):
        c = self.base // k * times + off
        return c if self.j is None else self.j * (self.per // k * times) + c

    def mod(self, k):
        assert self.j is None or self.per % k == 0
        return self.base % k

    def split(self):
        return Unit(S_OF[self.base], self.split_per, self.j)

    def ahead(self):
        n = S_OF[self.base] + SPL
        if self.j is not None:
            return self.plus(SPL)
        return Unit(SPLIT_UNITS[n]) if n < SPLITS else None


def nth(kind, i):
    return Unit([r for r, k in enumerate(KIND) if k == kind][i])


def units(eng, base, count, per, fn):
    full = count // per
    done = 0
    if full > 1:
        with eng.Fori(0, full) as j:
            for b in range(per):
                fn(Unit(base + b, per, j), Unit(b, per, j))
        done = full * per
    for b in range(done, count):
        fn(Unit(base + b), Unit(b))


def build(nc, x, c, ada_w, ada_b, norm1_w, w_in, conv_w, conv_b, dt_bias, a_log, ssm_d, ssm_norm_w,
          w_br_ret, w_br_ssm, w_br_att, w_out, norm2_w, w_ff1, w_ff3, w_ff2, final_norm_w,
          table, out):
    with ExitStack() as ctx:
        at = [nc.sbuf_base + (-nc.sbuf_base) % 64]

        def sb(name, shape, dt=F32, offset=None):
            size = 4 * int(np.prod(shape[1:]))
            if offset is None:
                offset = at[0]
                at[0] += size + (-size) % 32
            return nc.alloc_sbuf_tensor_at(name, shape, dt, offset=offset)

        def region(size):
            at[0] += size
            return at[0] - size

        def sem(name):
            return ctx.enter_context(nc.semaphore(name))

        raw = sb("raw", [P, RAW, 2 * HALF])
        w_hi = sb("w_hi", [P, SPL, 2 * HALF], F32R)
        w_lo = sb("w_lo", [P, SPL, 2 * HALF], F32R)
        xf = sb("xf", [P, KB, S])
        r_h = region(2 * KB * S * 4)
        h_hi = sb("h_hi", [P, KB, S], F32R, r_h)
        h_lo = sb("h_lo", [P, KB, S], F32R, r_h + KB * S * 4)
        m_hi = sb("m_hi", [P, KB, S], F32R, r_h)
        m_lo = sb("m_lo", [P, KB, S], F32R, r_h + KB * S * 4)
        r_z1 = region(36 * S * 4)
        xbc = sb("xbc", [P, 16, S], F32, r_z1)
        aqk = sb("aqk", [P, 12, S], F32, r_z1 + 16 * S * 4)
        qk = sb("qk", [P, 4, 2, S], F32, r_z1 + 28 * S * 4)
        y_hi = sb("y_hi", [P, 18, S], F32R, r_z1)
        y_lo = sb("y_lo", [P, 18, S], F32R, r_z1 + 18 * S * 4)
        sq = sb("sq", [P, KB, S], F32, r_z1)
        hn = sb("hn", [P, KB, S], F32, r_z1 + KB * S * 4)
        r_tok = region(3 * NT * D * 4)
        tok = sb("tok", [P, 3, NT, D], F32, r_tok)
        ada_row = sb("ada_row", [1, EARLY * COL], F32, r_tok)
        mixed = sb("mixed", [P, KB, S], F32, r_tok + NT * D * 4)
        av = sb("av", [P, NT, AG * AS * AHD])
        yatt = sb("yatt", [P, NT, AS * AHD])
        r_gate = region(24 * S * 4)
        gates = sb("gates", [P, 24, S], F32, r_gate)
        x_tok = sb("x_tok", [P, NT, D], F32, r_gate)
        tab = sb("tab", [P, T_END])
        f_hi = sb("f_hi", [P, FB, S], F32R, r_z1)
        f_lo = sb("f_lo", [P, FB, S], F32R, r_gate)
        assert 22 * S * 4 <= 36 * S * 4
        r_l = region(SG * 384 * 4)
        decay = sb("decay", [P, 4, 384], F32, r_l)
        p_t = sb("p_t", [P, 9, P], F32, r_l)
        xpad = sb("xpad", [P, 2, 2, S + 3], F32, r_l)
        rope_c = sb("rope_c", [P, 2, S], F32, r_l)
        rope_s = sb("rope_s", [P, 2, S], F32, r_l + 2 * S * 4)
        sil = sb("sil", [P, 2 * S], F32, r_l)
        hid = sb("hid", [P, 2 * S], F32, r_l + 2 * S * 4)
        br = sb("br", [P, 2, 2 * S], F32, r_l)
        att_s = sb("att_s", [P, 9 * P])
        cbm = sb("cbm", [P, 384])
        xdt = sb("xdt", [P, NT, 4 * SHD])
        ytmp = sb("ytmp", [P, NT, 4 * SHD])
        m_ret = sb("m_ret", [P, 384])
        mac = sb("mac", [P, 4, COL])
        acc = sb("acc", [P, 2, COL])
        rstd = sb("rstd", [P, S])
        junk = rstd[:, :]
        rows = sb("rows", [P, 2, P])
        rowv = sb("rowv", [1, 3 * SH])
        crow = sb("crow", [16, P], F32, r_gate + NT * D * 4)
        par = sb("par", [P, Q_END])
        fnw = sb("fnw", [P, KB])
        c32 = sb("c32", [P, KB])
        ada = sb("ada", [P, 48])
        a1 = sb("a1", [P, 2, KB])
        g1h = sb("g1h", [P, KB])
        eps = sb("eps", [P, 1])
        one = sb("one", [P, 1])
        dt_x = sb("dt_x", [P, NT * SH])
        dt_e = sb("dt_e", [P, NT * SH])
        dt = sb("dt", [P, NT, SH])
        exp_a = sb("exp_a", [P, SH])
        d_a = sb("d_a", [P, NT, SH])
        cs = sb("cs", [P, NT, SH])
        negmax = sb("negmax", [P, 2])
        ssum = sb("ssum", [P, 2])
        rsum = sb("rsum", [P, 2])
        bst = sb("bst", [P, NT, 6])
        mv = sb("mv", [P, RH, NT, 2])
        ss = sb("ss", [P, SG, NT])
        sd = sb("sd", [P, 2, 8])
        ri = sb("ri", [P, 2, 8])
        assert at[0] <= nc.sbuf_usable_end, (at[0], nc.sbuf_usable_end)

        bank = [ctx.enter_context(nc.psum_tensor(f"bank{i}", [P, 512], F32)) for i in range(8)]
        cos, sin = tab[:, T_COS:T_COS + S], tab[:, T_SIN:T_SIN + S]
        ret_mask = tab[:, T_RET:T_RET + RH * S].rearrange("p (h t) -> p h t", h=RH)
        att_mask = tab[:, T_ATT:T_ATT + AG * S].rearrange("p (g t) -> p g t", g=AG)
        cb_mask = tab[:, T_CB:T_CB + 384]
        ones = tab[:, T_CB + P:T_CB + 2 * P]
        tri = [tab[:, T_TRI:T_TRI + P], tab[:, T_CB:T_CB + P]]
        ident = tab[:, T_ID:T_ID + P]
        conv_wp = par[:, Q_CW:Q_CW + 64].rearrange("p (j k) -> p j k", j=4)

        s_in = sem("inputs_landed")
        s_par = sem("params_landed")
        landed = [sem(f"raw_landed{i}") for i in range(RAW)]
        hi_ready = sem("w_hi_ready")
        lo_ready = sem("w_lo_ready")
        half_done = sem("half_multiplied")
        bank_free = [sem("bank0_free"), sem("bank1_free")]
        x_turned = sem("x_transposed")
        c_ready = sem("c_silu_ready")
        x_ready = sem("x_ready")
        par_turned = sem("params_transposed")
        row_ps = sem("modulation_row_in_psum")
        row_ready = sem("modulation_row_copied")
        early_turned = sem("early_modulation_turned")
        mac_done = sem("ada_raw_read")
        acc_ready = sem("ada_partial_sums_ready")
        acc_summed = sem("ada_partial_sums_read")
        ada_taken = sem("late_modulation_taken")
        ada_ready = sem("ada_ready")
        sq_ready = sem("squares_ready")
        ss_ready = sem("sumsq_ready")
        sd_ready = sem("std_ready")
        hn_ready = sem("normed_ready")
        h32_ready = sem("h_ready")
        h_split = sem("h_split")
        rot_out = sem("rotary_done")
        xpad_ready = sem("conv_input_ready")
        conv_ready = sem("conv_ready")
        xbc_ready = sem("xbc_ready")
        dtx_ready = sem("dt_input_ready")
        dte_ready = sem("dt_exp_ready")
        da_ready = sem("dA_ready")
        cs_ps = sem("cumsum_in_psum")
        cs_ready = sem("cumsum_ready")
        sc_ps = sem("scores_in_psum")
        mret_ready = sem("retention_weights_ready")
        max_ready = sem("attention_max_ready")
        p_ready = sem("attention_exp_ready")
        pv_ret = sem("retention_out_in_psum")
        pt_ps = sem("attention_probs_turned")
        pt_ready = sem("attention_probs_copied")
        yret_ready = sem("retention_out_ready")
        s2_ps = sem("attention_out_xs_cb_in_psum")
        s2_ready = sem("attention_out_xs_cb_ready")
        csb_ps = sem("cumsum_rows_in_psum")
        seg_ready = sem("segments_ready")
        dec_ready = sem("decay_ready")
        mssd_ready = sem("ssd_weights_ready")
        y_ps = sem("ssd_out_in_psum")
        yssd_ready = sem("ssd_out_ready")
        ssq_ready = sem("group_stats_ready")
        gsd_ready = sem("group_std_ready")
        ynorm_ready = sem("branch_normed")
        yt_ps = sem("branch_turned")
        yt_hi = sem("branch_hi_ready")
        yt_lo = sem("branch_lo_ready")
        mix_ready = sem("mixed_ready")
        mix_hi = sem("mixed_hi_ready")
        mix_lo = sem("mixed_lo_ready")
        hid_ready = sem("hidden_ready")
        hid_hi = sem("hidden_hi_ready")
        hid_lo = sem("hidden_lo_ready")
        fin_ready = sem("final_norm_ready")
        out_turned = sem("out_transposed")
        out_ready = sem("out_ready")
        stored = sem("out_stored")

        rearr = {
            "ada": ada_w, "in": w_in, "ret": w_br_ret, "ssm": w_br_ssm, "att": w_br_att,
            "out": w_out, "ff1": w_ff1, "ff3": w_ff3, "ff2": w_ff2,
        }
        w_dram = {k: v.rearrange("l (k p) n -> p (l k) n", p=P) for k, v in rearr.items()}

        def n_landed(l, u):
            return l * (16 * UNITS // RAW) + u.over(RAW, 16, 16)

        def n_half(l, u, h):
            return l * (2 * SPLITS) + u.split().over(1, 2, h + 1)

        def n_bank(l, u):
            return l * (SPLITS // 2) + u.split().over(2, 1, 1)

        FREE_HALVES = 2 * SPL
        FREE_RAW = 2 * RAW

        def cols_of(u):
            return KB * SH if u.j is None and u.base == U_DT else 2 * HALF

        def parts(u, h, dst, src, lead=None):
            cn = cols_of(u)
            half = slice(h * HALF, h * HALF + cn // 2)
            from_raw = slice(h * cn // 2, (h + 1) * cn // 2)
            if KIND[u.base] == "qk":
                mine = dict(b=2, a=2, c=RQK // 2)
                for b in range(2):
                    ops = [dst[:, half].rearrange("p (k b a c) -> p k b a c", **mine)[:, :, b, :, :],
                           src[:, half].rearrange("p (k a b c) -> p k a b c", **mine)[:, :, :, b, :]]
                    if lead is not None:
                        ops.append(lead[:, half].rearrange("p (k b a c) -> p k b a c", **mine)[:, :, b, :, :])
                    yield ops
            else:
                yield [dst[:, half], src[:, from_raw]] + ([lead[:, half]] if lead is not None else [])

        block = ctx.enter_context(nc.Block())

        @block.sync
        def _(sp):
            with sp.Fori(0, L) as l:
                pieces = [(ada_b, 48, Q_ADAB), (norm1_w, 8, Q_N1), (norm2_w, 8, Q_N2),
                          (ssm_norm_w, 8, Q_SN), (conv_b, 16, Q_CB)]
                for src, n, q in pieces:
                    sp.dma_start(rows[q:q + n, 0, :],
                                 src.rearrange("l (k p) -> (l k) p", p=P)[bass.ds(l * n, n), :])\
                      .then_inc(s_par, 16)
                sp.dma_start(rows[0:64, 1, :],
                             conv_w.rearrange("l j (k p) -> (l j k) p", p=P)[bass.ds(l * 64, 64), :])\
                  .then_inc(s_par, 16)
                for n, src in enumerate((dt_bias, a_log, ssm_d)):
                    sp.dma_start(rowv[0:1, n * SH:(n + 1) * SH], src[bass.ds(l, 1), :]).then_inc(s_par, 16)

                def load(u, name, k0, kn, col, cn):
                    s = u.mod(RAW)
                    before = u.plus(-RAW)
                    a = A_OF.get(before.base)
                    if a is not None and a < EARLY:
                        sp.wait_ge(row_ps, l * EARLY + a + 1)
                    elif a is not None:
                        sp.wait_ge(mac_done, l * LATE + a - EARLY + 1)
                    elif before.base >= 0:
                        sp.wait_ge(lo_ready, n_half(l, before, FREE_RAW + 1))
                    else:
                        sp.wait_ge(lo_ready, l * (2 * SPLITS) + FREE_RAW + 2 * before.base + 2)
                    dst = raw[:, s, 0:kn * cn].rearrange("p (k n) -> p k n", k=kn)
                    sp.dma_start(dst, w_dram[name][:, bass.ds(k0, kn), bass.ds(col, cn)])\
                      .then_inc(landed[s], 16)

                first = {"qk": C_QK, "xbc": C_XBC, "aqk": C_AQK, "tok": C_TOK, "av": C_AV, "gate": C_GATE}
                seen = {}
                for r, kind in enumerate(KIND[:U_FF]):
                    i = seen[kind] = seen.get(kind, -1) + 1
                    if kind == "dt":
                        load(Unit(r), "in", l * KB, KB, C_DT, SH)
                    elif kind == "att":
                        load(Unit(r), "att", l * 2, 2, 0, D)
                    elif kind in first:
                        load(Unit(r), "in", l * KB, KB, first[kind] + i * COL, COL)
                    else:
                        load(Unit(r), kind, l * KB, KB, i * COL, COL)

                def ff(u, i):
                    load(u, "ff3" if i.base % 2 else "ff1", l * KB, KB, i.over(2, COL, 0), COL)
                for i in range(6):
                    ff(Unit(U_FF + i), Unit(i))
                units_from(sp, U_FF, 6, N_FF, 4, ff)

                def ff2(u, i):
                    load(u, "ff2", l * FB + i.over(1, 2, 0), 2, 0, D)
                for i in range(3):
                    ff2(Unit(U_FF2 + i), Unit(i))
                units_from(sp, U_FF2, 3, N_FF2, 4, ff2)
            for t in range(NT):
                sp.wait_ge(out_ready, t + 1)
                sp.dma_start(out[0, t * P:(t + 1) * P, :], x_tok[:, t, :]).then_inc(stored, 16)
            sp.wait_ge(stored, 16 * NT)

        @block.tensor
        def _(pe):
            pe.sem_inc(half_done, FREE_HALVES)
            pe.sem_inc(acc_summed, 1)

            def three(o, hi, lo, xh, xl, first, last, swap=False):
                ps = [(hi, xh), (hi, xl), (lo, xh)]
                if swap:
                    ps = [(xh, hi), (xh, lo), (xl, hi)]
                for n, (a, b) in enumerate(ps):
                    done = pe.matmul(o, a, b, start=first and n == 0, stop=last and n == 2,
                                     skip_group_check=True)
                return done

            def two_halves(l, u, body, own_bank=True, before=None):
                s = u.split().mod(SPL)
                for h in range(2):
                    pe.wait_ge(lo_ready, n_half(l, u, FREE_RAW + h))
                    if h == 0 and own_bank:
                        pe.wait_ge(bank_free[u.split().mod(2)], n_bank(l, u))
                    if before:
                        before(h)
                    body(s, h).then_inc(half_done, 1)
                if not own_bank:
                    pe.sem_inc(bank_free[u.split().mod(2)], 1)

            def feature(l, u, ah=h_hi, al=h_lo, k0=0, before=None):
                def body(s, h):
                    hi, lo = (w[:, s, :].rearrange("p (k n) -> p k n", n=COL) for w in (w_hi, w_lo))
                    for m in range(2):
                        o = bank[u.split().mod(2)][:, m * S:(m + 1) * S]
                        mc = slice(m * P, (m + 1) * P)
                        for k in range(h * 4, h * 4 + 4):
                            last = three(o, hi[:, k, mc], lo[:, k, mc], ah[:, k0 + k, :], al[:, k0 + k, :],
                                         k == 0 and m == 0, k == KB - 1)
                    return last
                two_halves(l, u, body, before=before)

            def token(l, u, cn=COL):
                def body(s, h):
                    hi, lo = (w[:, s, h * HALF:h * HALF + KB * cn // 2].rearrange("p (k n) -> p k n", n=cn)
                              for w in (w_hi, w_lo))
                    for t in range(NT):
                        o = bank[u.split().mod(2)][:, t * S:t * S + cn]
                        tk = slice(t * P, (t + 1) * P)
                        for k in range(h * 4, h * 4 + 4):
                            last = three(o, hi[:, k % 4, :], lo[:, k % 4, :], h_hi[:, k, tk], h_lo[:, k, tk],
                                         k == 0 and t == 0, k == KB - 1, swap=True)
                    return last
                two_halves(l, u, body)

            def ada_row_unit(l, i):
                u = nth("ada", i)
                pe.wait_ge(landed[u.mod(RAW)], n_landed(l, u))
                w = raw[:, u.mod(RAW), :].rearrange("p (k n) -> p k n", n=COL)
                for k in range(KB):
                    last = pe.matmul(bank[4 + i // 2][0:1, i % 2 * COL:(i % 2 + 1) * COL], c32[:, k:k + 1],
                                     w[:, k, :], start=k == 0, stop=k == KB - 1)
                last.then_inc(row_ps, 1)

            def turn_row(l, q):
                pe.wait_ge(row_ready, l * (EARLY // 2) + q + 1)
                for m in range(4 * q, 4 * q + 4):
                    last = pe.matmul(bank[0][:, m:m + 1], ada_row[0:1, m * P:(m + 1) * P],
                                     ones[0:1, 0:1], start=True, stop=True)
                return last

            def ada_sum(l, a):
                pe.wait_ge(acc_ready, l * LATE + a.over(1, 1, 1))
                for m in range(2):
                    last = pe.matmul(bank[4][:, bass.ds(a.over(1, 2, m), 1)],
                                     acc[:, a.mod(2), m * P:(m + 1) * P], ones[:, 0:1], start=True, stop=True)
                last.then_inc(acc_summed, 1)

            def whole_rows(l, u, ah, al, k0, first, last_unit, before=None):
                def body(s, h):
                    hi, lo = (w[:, s, :].rearrange("p (k n) -> p k n", n=D) for w in (w_hi, w_lo))
                    for m in range(KB):
                        o = bank[4 + m // 2][:, m % 2 * S:(m % 2 + 1) * S]
                        mc = slice(m * P, (m + 1) * P)
                        last = three(o, hi[:, h, mc], lo[:, h, mc], ah[:, k0 + h, :], al[:, k0 + h, :],
                                     first and h == 0 and m % 2 == 0, last_unit and h == 1)
                    return last
                two_halves(l, u, body, own_bank=False, before=before)

            def norm_sum(n, i):
                pe.wait_ge(sq_ready, n * 4 + i + 1)
                for k in (2 * i, 2 * i + 1):
                    last = pe.matmul(bank[2][:, 0:S], ones, sq[:, k, :], start=k == 0, stop=k == KB - 1)
                if i == 3:
                    last.then_inc(ss_ready, 1)

            pe.wait_ge(s_in, 16 * 4)
            for k in range(KB):
                for t in range(NT):
                    pe.transpose(bank[2 + k // 2][:, k % 2 * S + t * P:k % 2 * S + (t + 1) * P],
                                 x_tok[:, t, k * P:(k + 1) * P], ident)
            pe.transpose(bank[6][:, 0:16], crow[:, :], ident[0:16, 0:16]).then_inc(x_turned, 1)

            with pe.Fori(0, L) as l:
                pe.wait_ge(x_ready, l * 8 + 4)
                pe.wait_ge(s_par, l * 144 + 144)
                pe.transpose(bank[3][:, 0:N_ROW0], rows[0:N_ROW0, 0, :], ident[0:N_ROW0, 0:N_ROW0])
                pe.transpose(bank[3][:, Q_CW:Q_CW + 64], rows[0:64, 1, :], ident[0:64, 0:64])
                pe.matmul(bank[3][:, Q_DTB:Q_END], ones[0:1, :], rowv[:, :], start=True, stop=True)\
                  .then_inc(par_turned, 1)
                for i in range(4):
                    norm_sum(l * 2, i)
                pe.wait_ge(c_ready, 1)
                pe.wait_ge(bank_free[0], n_bank(l, nth("qk", 0)))
                for i in range(EARLY):
                    ada_row_unit(l, i)
                    if i % 2 == 0 and i:
                        turn_row(l, i // 2 - 1)
                turn_row(l, EARLY // 2 - 1).then_inc(early_turned, 1)

                def h_pairs(n):
                    return lambda h: pe.wait_ge(h_split, (l * 2 + n) * 4 + 2 * h + 2)
                for i in range(N_QK):
                    feature(l, nth("qk", i), before=h_pairs(0))
                for i in range(N_XBC):
                    feature(l, nth("xbc", i))
                    if i % 3 == 1 and i > 3:
                        ada_sum(l, Unit(i // 3 - 1))
                for i in range(N_AQK):
                    feature(l, nth("aqk", i))
                    if i % 3 == 2:
                        ada_sum(l, Unit(2 + i // 3))
                with pe.Fori(0, 2) as j:
                    for b in range(TOK_UNITS // 2):
                        u = Unit(U_TOK + b, TOK_UNITS // 2, j, N_TOK // 2)
                        if b % 4 == 3:
                            ada_sum(l, Unit(4 + b // 4, 2, j))
                        else:
                            token(l, u)
                token(l, Unit(U_DT), SH)
                token(l, nth("av", 0))
                ada_sum(l, Unit(8))
                token(l, nth("av", 1))
                token(l, nth("av", 2))

                def s_scores(j):
                    q0, pr = j % 2 * 64, j // 2
                    hd = slice(q0, q0 + 64)
                    if j == 0:
                        pe.wait_ge(rot_out, l * 4 + 4)
                    else:
                        pe.wait_ge(seg_ready, l * 4 + j)
                    for t in range(NT):
                        for b in range(2):
                            pe.matmul(bank[2][:, t * S:t * S + S - t * P],
                                      qk[hd, 2 + pr, b, t * P:(t + 1) * P], qk[hd, pr, b, t * P:S],
                                      start=b == 0, stop=b == 1)
                    for g in range(AG):
                        pe.matmul(bank[5][:, g * P:(g + 1) * P], aqk[hd, 2 * g + pr, 0:P],
                                  aqk[hd, 6 + 2 * g + pr, 0:P], start=True, stop=True)
                    for g in range(AG):
                        last = pe.matmul(bank[6 + g // 2][:, g % 2 * S:(g % 2 + 1) * S],
                                         aqk[hd, 2 * g + pr, P:S], aqk[hd, 6 + 2 * g + pr, :],
                                         start=True, stop=True)
                    last.then_inc(sc_ps, 1)

                def s_ret_out_and_turn(j):
                    n = l * 4 + j + 1
                    pe.wait_ge(mret_ready, n)
                    v = [tok[:, 0, t, j * RV:(j + 1) * RV] for t in range(NT)]
                    pe.matmul(bank[2][:, 0:S], m_ret[:, 0:P], v[0], start=True, stop=True)
                    pe.matmul(bank[2][:, S:2 * S], m_ret[:, P:2 * P], v[0], start=True, stop=False)
                    pe.matmul(bank[2][:, S:2 * S], m_ret[:, 2 * P:3 * P], v[1], start=False, stop=True)\
                      .then_inc(pv_ret, 1)
                    pe.wait_ge(p_ready, n)
                    for i in range(9):
                        last = pe.transpose(bank[5 + i // 4][:, i % 4 * P:(i % 4 + 1) * P],
                                            att_s[:, i * P:(i + 1) * P], ident)
                    last.then_inc(pt_ps, 1)

                def s_att_out_xs_cb(j):
                    n = l * 4 + j + 1
                    pe.wait_ge(pt_ready, n)

                    def value(g, t):
                        hcol = (g * AS + j) * AHD
                        return av[:, t, hcol:hcol + AHD]
                    for g in range(AG):
                        pe.matmul(bank[5][:, 0:AHD], p_t[:, g, :], value(g, 0), start=g == 0, stop=g == AG - 1)
                    for i in range(6):
                        pe.matmul(bank[5][:, AHD:2 * AHD], p_t[:, 3 + i, :], value(i // 2, i % 2),
                                  start=i == 0, stop=i == 5)
                    if j == 0:
                        pe.wait_ge(xbc_ready, l * N_XBC + N_XBC)
                    else:
                        pe.wait_ge(yssd_ready, n - 1)
                    for t in range(NT):
                        for b in range(2):
                            pe.transpose(bank[6][:, t * S + b * P:t * S + (b + 1) * P],
                                         xbc[:, 2 * j + b, t * P:(t + 1) * P], ident)
                    pe.matmul(bank[3][:, 0:S], xbc[:, 8 + j, 0:P], xbc[:, 12 + j, :], start=True, stop=True)
                    pe.matmul(bank[3][:, S:S + P], xbc[:, 8 + j, P:S], xbc[:, 12 + j, P:S],
                              start=True, stop=True).then_inc(s2_ps, 1)

                def s_cumsum_rows(j):
                    for r in range(4):
                        h = 4 * j + r
                        for t in range(NT):
                            o = r % 2 * S + t * P
                            last = pe.matmul(bank[7 if r < 2 else 5][:, o:o + P],
                                             d_a[:, t, h:h + 1].to_broadcast([P, P]), tri[t],
                                             start=True, stop=True)
                    last.then_inc(csb_ps, 1)

                def s_ssd_out(j):
                    pe.wait_ge(mssd_ready, l * 4 + j + 1)
                    for r in range(4):
                        pc = slice(r * SHD, (r + 1) * SHD)
                        pe.matmul(bank[3][:, r * SHD:(r + 1) * SHD], decay[:, r, 0:P], xdt[:, 0, pc],
                                  start=True, stop=True)
                        o = bank[3][:, S + r * SHD:S + (r + 1) * SHD]
                        pe.matmul(o, decay[:, r, P:2 * P], xdt[:, 0, pc], start=True, stop=False)
                        last = pe.matmul(o, decay[:, r, 2 * P:3 * P], xdt[:, 1, pc], start=False, stop=True)
                    last.then_inc(y_ps, 1)

                pe.wait_ge(da_ready, l + 1)
                for t in range(NT):
                    last = pe.matmul(bank[3][:, t * SH:(t + 1) * SH], tri[t], d_a[:, t, :], start=True, stop=True)
                last.then_inc(cs_ps, 1)
                for j in range(4):
                    feature(l, nth("gate", 3 * j))
                    s_scores(j)
                    if j:
                        s_ssd_out(j - 1)
                    feature(l, nth("gate", 3 * j + 1))
                    s_ret_out_and_turn(j)
                    ada_sum(l, Unit(9 + j))
                    feature(l, nth("gate", 3 * j + 2))
                    s_att_out_xs_cb(j)
                    pe.wait_ge(s2_ready, l * 4 + j + 1)
                    s_cumsum_rows(j)

                def turn(i):
                    if i == 0:
                        pe.wait_ge(seg_ready, l * 4 + 4)
                    if i == 0 or i == 5:
                        pe.wait_ge(ynorm_ready, l * 2 + i // 5 + 1)
                    if 4 <= i < 8:
                        pe.wait_ge(yt_lo, l * 9 + i - 3)
                    for b in range(2):
                        for t in range(NT):
                            if i == 4:
                                src = yatt[:, t, b * P:(b + 1) * P]
                            else:
                                k = (i if i < 4 else i - 5) * 2 + b
                                src = tok[:, 0 if i < 4 else 2, t, k * P:(k + 1) * P]
                            last = pe.transpose(bank[turn_bank(i)][:, b * S + t * P:b * S + (t + 1) * P],
                                                src, ident)
                    last.then_inc(yt_ps, 1)
                for i in range(5):
                    turn(i)

                def from_turned(count):
                    return lambda h: pe.wait_ge(yt_lo, l * 9 + count + 2 * h)
                for i in range(4):
                    feature(l, nth("ret", i), y_hi, y_lo, 0, from_turned(2))
                    if i == 0:
                        s_ssd_out(3)
                        for a in (13, 14):
                            ada_sum(l, Unit(a))
                    if i == 3:
                        for q in range(5, 9):
                            turn(q)
                        ada_sum(l, Unit(15))

                def banks_free(h):
                    pe.wait_ge(yt_lo, l * 9 + 9)
                    pe.wait_ge(ada_taken, l + 1)
                whole_rows(l, Unit(U_ATT), y_hi, y_lo, 8, True, True, before=banks_free)
                for i in range(4):
                    feature(l, Unit(U_SSM + i), y_hi, y_lo, 10)
                for i in range(N_OUT):
                    feature(l, Unit(U_OUT + i), m_hi, m_lo,
                            before=lambda h: pe.wait_ge(mix_lo, l * 4 + 2 + 2 * h))
                    if i:
                        norm_sum(l * 2 + 1, i - 1)
                norm_sum(l * 2 + 1, 3)

                def ffn_in(u, i):
                    feature(l, u, before=h_pairs(1) if i.base % 4 == 0 else None)
                units(pe, U_FF, N_FF, 4, ffn_in)
                for i in range(N_FF2):
                    whole_rows(l, Unit(U_FF2 + i), f_hi, f_lo, 2 * i, i == 0, i == N_FF2 - 1,
                               before=lambda h, i=i: pe.wait_ge(hid_lo, l * (N_FF // 2) + i + 1))

            for i in range(4):
                norm_sum(2 * L, i)
            for t in range(NT):
                for k in range(KB):
                    if t == 0 and k % 2 == 0:
                        pe.wait_ge(fin_ready, k // 2 + 1)
                    last = pe.transpose(bank[3 + 2 * t + k // 4][:, k % 4 * P:(k % 4 + 1) * P],
                                        hn[:, k, t * P:(t + 1) * P], ident)
                last.then_inc(out_turned, 1)

        @block.scalar
        def _(act):
            act.dma_start(x_tok[:, :, :], x.rearrange("a (t p) n -> p (a t) n", p=P)).then_inc(s_in, 16)
            act.dma_start(tab[:, :], table).then_inc(s_in, 16)
            act.dma_start(crow[0:8, :], c.rearrange("a (k p) -> (a k) p", p=P)).then_inc(s_in, 16)
            act.dma_start(crow[8:16, :], final_norm_w.rearrange("(k p) -> k p", p=P)).then_inc(s_in, 16)

            def hi(l, u):
                if u is None:
                    return
                s, r = u.split().mod(SPL), u.mod(RAW)
                act.wait_ge(landed[r], n_landed(l, u))
                for h in range(2):
                    act.wait_ge(half_done, n_half(l, u, h))
                    for dst, src in parts(u, h, w_hi[:, s, :], raw[:, r, :]):
                        last = act.activation(dst, src, ACT.Copy)
                    last.then_inc(hi_ready, 1)

            def result(l, u):
                act.wait_ge(half_done, n_half(l, u, 1 + FREE_HALVES))
                return bank[u.split().mod(2)]

            def squares(n, i):
                act.wait_ge(x_ready, n * 4 + i + 1)
                act.activation(sq[:, 2 * i:2 * i + 2, :], xf[:, 2 * i:2 * i + 2, :], ACT.Square)\
                   .then_inc(sq_ready, 1)

            def std(n):
                act.wait_ge(ss_ready, n + 1)
                act.activation(rstd[:, :], bank[2][:, 0:S], ACT.Sqrt, bias=eps[:, 0:1], scale=1.0 / D)\
                   .then_inc(sd_ready, 1)

            def modulate(n, a, sh):
                act.wait_ge(ada_ready, n + 1)
                for i in range(4):
                    act.wait_ge(hn_ready, n * 4 + i + 1)
                    for k in (2 * i, 2 * i + 1):
                        act.activation(hn[:, k, :], hn[:, k, :], ACT.Identity, bias=ada[:, sh + k:sh + k + 1],
                                       scale=a1[:, a, k:k + 1])
                    act.drain()
                    act.activation(h_hi[:, 2 * i:2 * i + 2, :], hn[:, 2 * i:2 * i + 2, :], ACT.Copy)\
                       .then_inc(h32_ready, 1)

            act.wait_ge(x_turned, 1)
            act.activation(fnw[:, :], bank[6][:, 8:16], ACT.Copy)
            act.activation(c32[:, :], bank[6][:, 0:8], ACT.Silu).then_inc(c_ready, 1)

            with act.Fori(0, L) as l:
                for i in range(4):
                    squares(l * 2, i)
                std(l * 2)
                for q in range(EARLY // 2):
                    act.wait_ge(row_ps, l * EARLY + 2 * q + 2)
                    act.activation(ada_row[0:1, 2 * q * COL:(2 * q + 2) * COL], bank[4 + q][0:1, :], ACT.Copy)\
                       .then_inc(row_ready, 1)
                hi(l, Unit(SPLIT_UNITS[0]))
                hi(l, Unit(SPLIT_UNITS[1]))
                modulate(l * 2, 0, 0)
                for i in range(N_QK):
                    hi(l, nth("qk", i).ahead())

                def silu_xbc(i):
                    act.wait_ge(conv_ready, l * N_XBC + i + 1)
                    v = xbc[:, 2 * i:2 * i + 2, :]
                    act.activation(v, v, ACT.Silu).then_inc(xbc_ready, 1)

                act.wait_ge(xpad_ready, l + 1)
                for i in range(N_XBC):
                    u = nth("xbc", i)
                    b = result(l, u)
                    act.activation(xpad[:, i % 2, :, 3:S + 3], b[:, :].rearrange("p (m t) -> p m t", m=2),
                                   ACT.Copy).then_inc(bank_free[u.split().mod(2)], 1)
                    hi(l, u.ahead())
                    if i:
                        silu_xbc(i - 1)
                silu_xbc(N_XBC - 1)

                for i in range(N_AQK):
                    u = nth("aqk", i)
                    b = result(l, u)
                    act.activation(aqk[:, 2 * i:2 * i + 2, :], b[:, :].rearrange("p (m t) -> p m t", m=2),
                                   ACT.Copy).then_inc(bank_free[u.split().mod(2)], 1)
                    hi(l, u.ahead())
                for i in range(N_TOK):
                    u = nth("tok", i)
                    b = result(l, u)
                    act.activation(tok[:, i // 4, :, i % 4 * COL:(i % 4 + 1) * COL],
                                   b[:, :].rearrange("p (t n) -> p t n", t=NT),
                                   ACT.Silu if i >= 4 else ACT.Copy).then_inc(bank_free[u.split().mod(2)], 1)
                    hi(l, u.ahead())
                hi(l, Unit(U_DT).ahead())
                for i in range(N_AV):
                    u = nth("av", i)
                    b = result(l, u)
                    act.activation(av[:, :, i * COL:(i + 1) * COL], b[:, :].rearrange("p (t n) -> p t n", t=NT),
                                   ACT.Copy).then_inc(bank_free[u.split().mod(2)], 1)
                    hi(l, u.ahead())
                    if i == 0:
                        act.wait_ge(dtx_ready, l + 1)
                        act.activation(dt_e[:, :], dt_e[:, :], ACT.Exp, scale=-1.0)
                        act.activation(exp_a[:, :], par[:, Q_ALOG:Q_ALOG + SH], ACT.Exp)
                        act.drain()
                        act.activation(dt_e[:, :], dt_e[:, :], ACT.Ln, bias=one[:, 0:1]).then_inc(dte_ready, 1)

                def gate(g):
                    u = nth("gate", g)
                    b = result(l, u)
                    act.activation(gates[:, 2 * g:2 * g + 2, :], b[:, :].rearrange("p (m t) -> p m t", m=2),
                                   ACT.Tanh, scale=0.5).then_inc(bank_free[u.split().mod(2)], 1)
                    hi(l, u.ahead())

                def square_sums(j):
                    act.wait_ge(yssd_ready, l * 4 + j + 1)
                    for t in range(NT):
                        last = act.activation(junk, tok[:, 2, t, j * COL:(j + 1) * COL], ACT.Square,
                                              accum_out=ss[:, j, t:t + 1])
                        if t == 0:
                            act.drain()
                    last.then_inc(ssq_ready, 1)

                def turned_hi(i):
                    act.wait_ge(yt_ps, l * 9 + i + 1)
                    b = bank[turn_bank(i)]
                    if i >= 5:
                        for m in range(2):
                            k = (i - 5) * 2 + m
                            last = act.activation(y_hi[:, 2 * i + m, :], b[:, m * S:(m + 1) * S], ACT.Copy,
                                                  scale=par[:, Q_SN + k:Q_SN + k + 1])
                    else:
                        last = act.activation(y_hi[:, 2 * i:2 * i + 2, :],
                                              b[:, :].rearrange("p (m t) -> p m t", m=2), ACT.Copy)
                    last.then_inc(yt_hi, 1)

                def decays(j):
                    act.wait_ge(seg_ready, l * 4 + j + 1)
                    act.activation(decay[:, :, :], decay[:, :, :], ACT.Exp).then_inc(dec_ready, 1)

                for j in range(4):
                    n = l * 4 + j + 1
                    if j:
                        decays(j - 1)
                    gate(3 * j)
                    act.wait_ge(max_ready, n)
                    act.activation(att_s[:, 0:384], att_s[:, 0:384], ACT.Exp, bias=negmax[:, 0:1],
                                   accum_out=ssum[:, 0:1])
                    act.activation(att_s[:, 384:1152], att_s[:, 384:1152], ACT.Exp, bias=negmax[:, 1:2],
                                   accum_out=ssum[:, 1:2]).then_inc(p_ready, 1)
                    gate(3 * j + 1)
                    act.wait_ge(pt_ps, n)
                    act.activation(p_t[:, 0:4, :], bank[5][:, :].rearrange("p (i n) -> p i n", i=4), ACT.Copy)
                    act.activation(p_t[:, 4:8, :], bank[6][:, :].rearrange("p (i n) -> p i n", i=4), ACT.Copy)
                    act.activation(p_t[:, 8, :], bank[7][:, 0:P], ACT.Copy).then_inc(pt_ready, 1)
                    if j:
                        square_sums(j - 1)
                    if j == 3:
                        act.wait_ge(yret_ready, n)
                        act.activation(sd[:, 0, :], mv[:, :, :, 1].rearrange("p h t -> p (h t)"), ACT.Sqrt,
                                       bias=eps[:, 0:1]).then_inc(gsd_ready, 1)
                    gate(3 * j + 2)
                decays(3)
                for i in range(5):
                    turned_hi(i)
                for i in range(4):
                    hi(l, nth("ret", i).ahead())
                    if i == 1:
                        square_sums(3)
                        act.wait_ge(ssq_ready, l * 4 + 4)
                        act.activation(sd[:, 1, :], ss[:, :, :].rearrange("p h t -> p (h t)"), ACT.Sqrt,
                                       bias=eps[:, 0:1], scale=1.0 / COL).then_inc(gsd_ready, 1)
                for i in range(5, 9):
                    turned_hi(i)
                hi(l, Unit(U_ATT).ahead())
                for i in range(4):
                    hi(l, Unit(U_SSM + i).ahead())
                    act.wait_ge(mix_ready, l * 4 + i + 1)
                    act.activation(m_hi[:, 2 * i:2 * i + 2, :], mixed[:, 2 * i:2 * i + 2, :], ACT.Copy)\
                       .then_inc(mix_hi, 1)
                for i in range(N_OUT):
                    hi(l, Unit(U_OUT + i).ahead())
                    squares(l * 2 + 1, i)
                std(l * 2 + 1)
                modulate(l * 2 + 1, 1, 24)

                def hidden_hi(i):
                    act.wait_ge(hid_ready, l * (N_FF // 2) + i.over(2, 1, 0))
                    act.activation(f_hi[:, bass.ds(i.over(2, 2, -2), 2), :],
                                   hid[:, :].rearrange("p (m t) -> p m t", m=2), ACT.Copy).then_inc(hid_hi, 1)

                def ffn(u, i, first=False):
                    if i.base % 2 == 0:
                        if not first:
                            hidden_hi(i)
                        b = result(l, u)
                        act.activation(sil[:, :], b[:, :], ACT.Silu).then_inc(bank_free[u.split().mod(2)], 1)
                    hi(l, u.ahead())
                ffn(Unit(U_FF), Unit(0), True)
                ffn(Unit(U_FF + 1), Unit(1))
                units_from(act, U_FF, 2, N_FF, 4, ffn)
                hidden_hi(Unit(N_FF))
                for i in range(N_FF2):
                    hi(l, Unit(U_FF2 + i).ahead())
            for i in range(4):
                squares(2 * L, i)
            std(2 * L)
            for i in range(4):
                act.wait_ge(hn_ready, 2 * L * 4 + i + 1)
                for k in (2 * i, 2 * i + 1):
                    last = act.activation(hn[:, k, :], hn[:, k, :], ACT.Copy, scale=fnw[:, k:k + 1])
                last.then_inc(fin_ready, 1)

        @block.vector
        def _(dve):
            dve.sem_inc(lo_ready, FREE_RAW)
            dve.sem_inc(bank_free[0], 1)
            dve.sem_inc(bank_free[1], 1)
            dve.memset(eps[:, :], EPS)
            dve.memset(one[:, :], 1.0)

            def lo(l, u):
                if u is None:
                    return
                s, r = u.split().mod(SPL), u.mod(RAW)
                for h in range(2):
                    dve.wait_ge(hi_ready, n_half(l, u, h))
                    for dst, src, lead in parts(u, h, w_lo[:, s, :], raw[:, r, :], w_hi[:, s, :].bitcast(F32)):
                        last = dve.tensor_tensor(dst, src, lead, ALU.subtract)
                    last.then_inc(lo_ready, 1)

            def result(l, u):
                dve.wait_ge(half_done, n_half(l, u, 1 + FREE_HALVES))
                return bank[u.split().mod(2)]

            def normed(n):
                dve.wait_ge(sd_ready, n + 1)
                dve.reciprocal(rstd[:, :], rstd[:, :])
                dve.drain()
                for i in range(4):
                    dve.tensor_tensor(hn[:, 2 * i:2 * i + 2, :], xf[:, 2 * i:2 * i + 2, :],
                                      rstd[:, None, :].to_broadcast([P, 2, S]), ALU.mult).then_inc(hn_ready, 1)

            def split_h(n):
                for i in range(4):
                    dve.wait_ge(h32_ready, n * 4 + i + 1)
                    v = slice(2 * i, 2 * i + 2)
                    dve.tensor_tensor(h_lo[:, v, :], hn[:, v, :], h_hi[:, v, :].bitcast(F32), ALU.subtract)\
                       .then_inc(h_split, 1)

            def ada_take(first, count, src):
                v = slice(2 * first, 2 * (first + count))
                return dve.tensor_tensor(ada[:, v], src, par[:, v], ALU.add)

            def norm_scale(a, sc, w):
                dve.drain()
                dve.scalar_tensor_tensor(out=a1[:, a, :], in0=ada[:, sc:sc + KB], scalar=1.0,
                                         in1=par[:, w:w + KB], op0=ALU.add, op1=ALU.mult)\
                   .then_inc(ada_ready, 1)

            dve.wait_ge(x_turned, 1)
            for i in range(4):
                dve.tensor_copy(xf[:, 2 * i:2 * i + 2, :], bank[2 + i][:, :].rearrange("p (m t) -> p m t", m=2))\
                   .then_inc(x_ready, 1)

            with dve.Fori(0, L) as l:
                dve.wait_ge(par_turned, l + 1)
                dve.tensor_copy(par[:, :], bank[3][:, 0:Q_END])
                dve.drain()
                normed(l * 2)
                dve.wait_ge(early_turned, l + 1)
                ada_take(0, EARLY, bank[0][:, 0:2 * EARLY])
                norm_scale(0, 8, Q_N1)
                lo(l, Unit(SPLIT_UNITS[0]))
                lo(l, Unit(SPLIT_UNITS[1]))
                split_h(l * 2)
                for i in range(N_QK):
                    u = nth("qk", i)
                    b = result(l, u)[:, :].rearrange("p (m t) -> p m t", m=2)
                    dve.tensor_tensor(rope_c[:, :, :], b, cos[:, None, :].to_broadcast([P, 2, S]), ALU.mult)
                    dve.tensor_tensor(rope_s[:, :, :], b, sin[:, None, :].to_broadcast([P, 2, S]), ALU.mult)\
                       .then_inc(bank_free[u.split().mod(2)], 1)
                    dve.drain()
                    dve.tensor_tensor(qk[:, i, 0, :], rope_c[:, 0, :], rope_s[:, 1, :], ALU.subtract)
                    dve.tensor_tensor(qk[:, i, 1, :], rope_s[:, 0, :], rope_c[:, 1, :], ALU.add)
                    dve.drain().then_inc(rot_out, 1)
                    lo(l, u.ahead())
                dve.memset(xpad[:, :, :, 0:3], 0.0).then_inc(xpad_ready, 1)
                for i in range(N_XBC):
                    u = nth("xbc", i)
                    lo(l, u.ahead())
                    dve.wait_ge(bank_free[u.split().mod(2)], n_bank(l, u) + 1)
                    for t in range(3, -1, -1):
                        for m in range(2):
                            k = 2 * i + m
                            src = xpad[:, i % 2, m, t:t + S]
                            w = conv_wp[:, t, k:k + 1]
                            if t == 3:
                                last = dve.tensor_scalar(xbc[:, k, :], src, w, par[:, Q_CB + k:Q_CB + k + 1],
                                                         ALU.mult, ALU.add)
                            else:
                                last = dve.scalar_tensor_tensor(out=xbc[:, k, :], in0=src, scalar=w,
                                                                in1=xbc[:, k, :], op0=ALU.mult, op1=ALU.add)
                        if t:
                            dve.drain()
                    last.then_inc(conv_ready, 1)
                for i in range(N_AQK):
                    lo(l, nth("aqk", i).ahead())
                for i in range(N_TOK):
                    lo(l, nth("tok", i).ahead())
                u = Unit(U_DT)
                b = result(l, u)
                dve.tensor_tensor(dt_x[:, :].rearrange("p (t h) -> p t h", t=NT),
                                  b[:, :].rearrange("p (t n) -> p t n", t=NT)[:, :, 0:SH],
                                  par[:, None, Q_DTB:Q_DTB + SH].to_broadcast([P, NT, SH]), ALU.add)\
                   .then_inc(bank_free[u.split().mod(2)], 1)
                dve.drain()
                dve.scalar_tensor_tensor(out=dt_e[:, :], in0=dt_x[:, :], scalar=-1.0, in1=dt_x[:, :],
                                         op0=ALU.mult, op1=ALU.max).then_inc(dtx_ready, 1)
                lo(l, u.ahead())
                lo(l, nth("av", 0).ahead())
                dve.wait_ge(dte_ready, l + 1)
                dt_flat = dt[:, :, :].rearrange("p t h -> p (t h)")
                dve.scalar_tensor_tensor(out=dt_flat, in0=dt_x[:, :], scalar=0.0, in1=dt_e[:, :],
                                         op0=ALU.max, op1=ALU.add)
                dve.drain()
                for t in range(NT):
                    last = dve.scalar_tensor_tensor(out=d_a[:, t, :], in0=dt[:, t, :], scalar=-1.0,
                                                    in1=exp_a[:, :], op0=ALU.mult, op1=ALU.mult)
                last.then_inc(da_ready, 1)
                lo(l, nth("av", 1).ahead())
                lo(l, nth("av", 2).ahead())
                dve.wait_ge(cs_ps, l + 1)
                dve.tensor_copy(cs[:, :, :], bank[3][:, 0:2 * SH].rearrange("p (t h) -> p t h", t=NT))\
                   .then_inc(cs_ready, 1)

                def ssd_out(j):
                    dve.wait_ge(y_ps, l * 4 + j + 1)
                    f = ytmp[:, :, :].rearrange("p t n -> p (t n)")
                    dve.tensor_tensor(f, bank[3][:, :], f, ALU.add)
                    dve.drain()
                    z = tok[:, 2, :, j * COL:(j + 1) * COL]
                    dve.tensor_tensor(z, z, ytmp[:, :, :], ALU.mult).then_inc(yssd_ready, 1)

                def scale_branch(which):
                    for j in range(4):
                        for t in range(NT):
                            y = tok[:, 2 * which, t, j * COL:(j + 1) * COL]
                            r = ri[:, which, 2 * j + t:2 * j + t + 1]
                            if which == 0:
                                last = dve.scalar_tensor_tensor(out=y, in0=y, scalar=r,
                                                                in1=tok[:, 1, t, j * COL:(j + 1) * COL],
                                                                op0=ALU.mult, op1=ALU.mult)
                            else:
                                last = dve.tensor_scalar(y, y, r, None, ALU.mult)
                    last.then_inc(ynorm_ready, 1)

                def turned_lo(i):
                    dve.wait_ge(yt_hi, l * 9 + i + 1)
                    b = bank[turn_bank(i)]
                    if i >= 5:
                        for m in range(2):
                            k = (i - 5) * 2 + m
                            last = dve.scalar_tensor_tensor(out=y_lo[:, 2 * i + m, :], in0=b[:, m * S:(m + 1) * S],
                                                            scalar=par[:, Q_SN + k:Q_SN + k + 1],
                                                            in1=y_hi[:, 2 * i + m, :].bitcast(F32),
                                                            op0=ALU.mult, op1=ALU.subtract)
                    else:
                        last = dve.tensor_tensor(y_lo[:, 2 * i:2 * i + 2, :],
                                                 b[:, :].rearrange("p (m t) -> p m t", m=2),
                                                 y_hi[:, 2 * i:2 * i + 2, :].bitcast(F32), ALU.subtract)
                    last.then_inc(yt_lo, 1)

                for j in range(4):
                    n = l * 4 + j + 1
                    lo(l, nth("gate", 3 * j).ahead())
                    dve.wait_ge(sc_ps, n)
                    dve.tensor_tensor(m_ret[:, 0:S], bank[2][:, 0:S], ret_mask[:, j, :], ALU.mult)
                    dve.tensor_tensor(m_ret[:, S:S + P], bank[2][:, S:S + P], ret_mask[:, j, 0:P], ALU.mult)\
                       .then_inc(mret_ready, 1)
                    a3 = att_s[:, :].rearrange("p (i n) -> p i n", n=P)
                    dve.scalar_tensor_tensor(out=a3[:, 0:3, :],
                                             in0=bank[5][:, 0:384].rearrange("p (g n) -> p g n", g=AG),
                                             scalar=AHD ** -0.5, in1=att_mask[:, :, P:S], op0=ALU.mult, op1=ALU.add)
                    dve.scalar_tensor_tensor(out=att_s[:, 384:896], in0=bank[6][:, :], scalar=AHD ** -0.5,
                                             in1=tab[:, T_ATT:T_ATT + 512], op0=ALU.mult, op1=ALU.add)
                    dve.scalar_tensor_tensor(out=att_s[:, 896:1152], in0=bank[7][:, 0:S], scalar=AHD ** -0.5,
                                             in1=att_mask[:, 2, :], op0=ALU.mult, op1=ALU.add)
                    dve.drain()
                    dve.tensor_reduce(rsum[:, 0:1], att_s[:, 0:384], AXX, ALU.max)
                    dve.tensor_reduce(rsum[:, 1:2], att_s[:, 384:1152], AXX, ALU.max)
                    dve.drain()
                    dve.tensor_scalar(negmax[:, :], rsum[:, :], -1.0, None, ALU.mult).then_inc(max_ready, 1)
                    if j:
                        ssd_out(j - 1)
                    lo(l, nth("gate", 3 * j + 1).ahead())
                    dve.wait_ge(pv_ret, n)
                    for t in range(NT):
                        dve.bn_stats(bst[:, t, :], bank[2][:, t * S:(t + 1) * S])
                    dve.drain()
                    for t in range(NT):
                        dve.bn_aggr(mv[:, j, t, :], bst[:, t, :])
                    dve.drain()
                    for t in range(NT):
                        last = dve.tensor_scalar(tok[:, 0, t, j * RV:(j + 1) * RV], bank[2][:, t * S:(t + 1) * S],
                                                 mv[:, j, t, 0:1], None, ALU.subtract)
                    last.then_inc(yret_ready, 1)
                    lo(l, nth("gate", 3 * j + 2).ahead())
                    dve.wait_ge(s2_ps, n)
                    dve.reciprocal(rsum[:, :], ssum[:, :])
                    dve.drain()
                    for t in range(NT):
                        dve.tensor_scalar(yatt[:, t, j * AHD:(j + 1) * AHD], bank[5][:, t * AHD:(t + 1) * AHD],
                                          rsum[:, t:t + 1], None, ALU.mult)
                    for t in range(NT):
                        xs = bank[6][:, t * S:(t + 1) * S].rearrange("p (r n) -> p r n", r=4)
                        dve.tensor_tensor(xdt[:, t, :].rearrange("p (r n) -> p r n", r=4), xs,
                                          dt[:, t, 4 * j:4 * j + 4, None].to_broadcast([P, 4, SHD]), ALU.mult)
                        dve.tensor_tensor(ytmp[:, t, :].rearrange("p (r n) -> p r n", r=4), xs,
                                          par[:, Q_DSK + 4 * j:Q_DSK + 4 * j + 4, None].to_broadcast([P, 4, SHD]),
                                          ALU.mult)
                    dve.tensor_tensor(cbm[:, :], bank[3][:, 0:384], cb_mask, ALU.mult).then_inc(s2_ready, 1)
                    if j == 3:
                        dve.wait_ge(gsd_ready, l * 2 + 1)
                        dve.reciprocal(ri[:, 0, :], sd[:, 0, :])
                        dve.drain()
                        scale_branch(0)
                    dve.wait_ge(csb_ps, n)
                    for r in range(4):
                        h = 4 * j + r
                        b = bank[7 if r < 2 else 5][:, r % 2 * S:(r % 2 + 1) * S]
                        dve.tensor_scalar(decay[:, r, 0:S], b, cs[:, 0, h:h + 1], 0.0, ALU.subtract, ALU.min)
                        last = dve.tensor_scalar(decay[:, r, S:S + P], b[:, P:S], cs[:, 1, h:h + 1], 0.0,
                                                 ALU.subtract, ALU.min)
                    last.then_inc(seg_ready, 1)
                for i in range(5):
                    turned_lo(i)

                def gated(ps, g, k, first):
                    gt = gates[:, g * KB + k:g * KB + k + 2, :].rearrange("p m t -> p (m t)")
                    mx = mixed[:, k:k + 2, :].rearrange("p m t -> p (m t)")
                    return dve.scalar_tensor_tensor(out=mx if first else br[:, k // 2 % 2, :], in0=gt, scalar=1.0,
                                                    in1=ps, op0=ALU.add, op1=ALU.mult)

                def add_branch(k):
                    dve.drain()
                    mx = mixed[:, k:k + 2, :].rearrange("p m t -> p (m t)")
                    return dve.tensor_tensor(mx, mx, br[:, k // 2 % 2, :], ALU.add)
                for i in range(4):
                    u = nth("ret", i)
                    b = result(l, u)
                    gated(b[:, :], 0, 2 * i, True).then_inc(bank_free[u.split().mod(2)], 1)
                    if i == 0:
                        ssd_out(3)
                    lo(l, u.ahead())
                    if i == 1:
                        dve.wait_ge(gsd_ready, l * 2 + 2)
                        dve.reciprocal(ri[:, 1, :], sd[:, 1, :])
                        dve.drain()
                        scale_branch(1)
                dve.wait_ge(acc_summed, l * LATE + LATE + 1)
                ada_take(EARLY, LATE, bank[4][:, 0:2 * LATE]).then_inc(ada_taken, 1)
                dve.drain()
                dve.tensor_scalar(g1h[:, :], ada[:, 16:24], 0.5, None, ALU.mult)
                norm_scale(1, 32, Q_N2)
                for q in range(5, 9):
                    turned_lo(q)
                u = Unit(U_ATT)
                result(l, u)
                for i in range(4):
                    gated(bank[4 + i][:, :], 2, 2 * i, False)
                    add_branch(2 * i)
                lo(l, u.ahead())
                for i in range(4):
                    u = Unit(U_SSM + i)
                    b = result(l, u)
                    gated(b[:, :], 1, 2 * i, False).then_inc(bank_free[u.split().mod(2)], 1)
                    add_branch(2 * i).then_inc(mix_ready, 1)
                    lo(l, u.ahead())
                    dve.wait_ge(mix_hi, l * 4 + i + 1)
                    v = slice(2 * i, 2 * i + 2)
                    dve.tensor_tensor(m_lo[:, v, :], mixed[:, v, :], m_hi[:, v, :].bitcast(F32), ALU.subtract)\
                       .then_inc(mix_lo, 1)
                for i in range(N_OUT):
                    u = Unit(U_OUT + i)
                    b = result(l, u)
                    for m in range(2):
                        k = 2 * i + m
                        last = dve.scalar_tensor_tensor(out=xf[:, k, :], in0=b[:, m * S:(m + 1) * S],
                                                        scalar=g1h[:, k:k + 1], in1=xf[:, k, :],
                                                        op0=ALU.mult, op1=ALU.add)
                    last.then_inc(bank_free[u.split().mod(2)], 1)
                    dve.drain().then_inc(x_ready, 1)
                    lo(l, u.ahead())
                normed(l * 2 + 1)
                split_h(l * 2 + 1)

                def hidden_lo(i):
                    dve.wait_ge(hid_hi, l * (N_FF // 2) + i.over(2, 1, 0))
                    v = bass.ds(i.over(2, 2, -2), 2)
                    dve.tensor_tensor(f_lo[:, v, :], hid[:, :].rearrange("p (m t) -> p m t", m=2),
                                      f_hi[:, v, :].bitcast(F32), ALU.subtract).then_inc(hid_lo, 1)

                def ffn(u, i, first=False):
                    if i.base % 2 == 0:
                        if not first:
                            hidden_lo(i)
                    else:
                        b = result(l, u)
                        if not first:
                            dve.wait_ge(hid_lo, l * (N_FF // 2) + i.over(2, 1, 0))
                        dve.tensor_tensor(hid[:, :], b[:, :], sil[:, :], ALU.mult)\
                           .then_inc(bank_free[u.split().mod(2)], 1)
                        dve.drain().then_inc(hid_ready, 1)
                    lo(l, u.ahead())
                ffn(Unit(U_FF), Unit(0), True)
                ffn(Unit(U_FF + 1), Unit(1), True)
                units_from(dve, U_FF, 2, N_FF, 4, ffn)
                hidden_lo(Unit(N_FF))
                for i in range(N_FF2):
                    lo(l, Unit(U_FF2 + i).ahead())
                result(l, Unit(U_FF2 + N_FF2 - 1))
                for k in range(KB):
                    last = dve.scalar_tensor_tensor(out=xf[:, k, :], in0=bank[4 + k // 2][:, k % 2 * S:(k % 2 + 1) * S],
                                                    scalar=ada[:, 40 + k:41 + k], in1=xf[:, k, :],
                                                    op0=ALU.mult, op1=ALU.add)
                    if k % 2:
                        last.then_inc(x_ready, 1)
            normed(2 * L)
            for t in range(NT):
                dve.wait_ge(out_turned, t + 1)
                for q in range(2):
                    last = dve.tensor_copy(x_tok[:, t, q * 512:(q + 1) * 512], bank[3 + 2 * t + q][:, :])
                last.then_inc(out_ready, 1)

        @block.gpsimd
        def _(pool):
            pool.wait_ge(c_ready, 1)
            with pool.Fori(0, L) as l:
                def ada_products(a):
                    u = nth("ada", EARLY + a)
                    r = u.mod(RAW)
                    pool.wait_ge(landed[r], n_landed(l, u))
                    w = raw[:, r, :].rearrange("p (k n) -> p k n", k=KB)
                    pool.tensor_tensor(w, w, c32[:, :, None].to_broadcast([P, KB, COL]), ALU.mult)
                    pool.drain()
                    pool.tensor_tensor(mac[:, :, :], w[:, 0:4, :], w[:, 4:8, :], ALU.add).then_inc(mac_done, 1)
                    pool.drain()
                    pool.tensor_tensor(mac[:, 0:2, :], mac[:, 0:2, :], mac[:, 2:4, :], ALU.add)
                    pool.drain()
                    pool.wait_ge(acc_summed, l * LATE + max(a, 1))
                    pool.tensor_tensor(acc[:, a % 2, :], mac[:, 0, :], mac[:, 1, :], ALU.add).then_inc(acc_ready, 1)

                def decayed_scores(j):
                    pool.wait_ge(dec_ready, l * SG + j + 1)
                    pool.tensor_tensor(decay[:, :, :], decay[:, :, :],
                                       cbm[:, None, :].to_broadcast([P, 4, 384]), ALU.mult)\
                        .then_inc(mssd_ready, 1)
                for a in range(11):
                    ada_products(a)
                for j in range(SG):
                    ada_products(11 + j)
                    decayed_scores(j)
                ada_products(15)


def turn_bank(i):
    return (2, 5, 6, 7, 2, 5, 6, 7, 3)[i]


def units_from(eng, base, start, count, per, fn):
    full = (count - start) // per
    assert start + full * per == count
    with eng.Fori(0, full) as j:
        for b in range(per):
            fn(Unit(base + start + b, per, j), Unit(start + b, per, j))


def tables():
    f = np.float32
    t = np.zeros((P, T_END), f)
    half = RQK // 2
    inv = f(10000.0) ** (-np.arange(half, dtype=f) / f(half))
    ang = (np.arange(S, dtype=f)[None, :] * inv.astype(f)[:, None]).astype(f)
    t[:, T_COS:T_COS + S] = np.tile(np.cos(ang.astype(np.float64)), (2, 1))
    t[:, T_SIN:T_SIN + S] = np.tile(np.sin(ang.astype(np.float64)), (2, 1))
    key = np.arange(P, dtype=np.float64)[:, None]
    qry = np.arange(S, dtype=np.float64)[None, :]
    lg = np.log1p(-np.exp(np.linspace(np.log(1.0 / 32), np.log(1.0 / 512), RH)))
    for h in range(RH):
        m = np.where(qry >= key, np.exp((qry - key) * lg[h]), 0.0) * RQK ** -0.5
        t[:, T_RET + h * S:T_RET + (h + 1) * S] = m
    q = P + np.arange(P)[:, None]
    k = np.arange(S)[None, :]
    for g, (window, dil) in enumerate(((128, 1), (512, 4), (2048, 16))):
        ok = (q >= k) & ((q - k) % dil == 0) & (q - k <= window)
        t[:, T_ATT + g * S:T_ATT + (g + 1) * S] = np.where(ok, 0.0, -1e30)
    low = (np.arange(P)[None, :] >= np.arange(P)[:, None]).astype(f)
    t[:, T_CB:T_CB + P] = low
    t[:, T_CB + P:T_CB + 2 * P] = 1.0
    t[:, T_CB + 2 * P:T_CB + 3 * P] = low
    t[:, T_TRI:T_TRI + P] = low - 1.0
    t[:, T_ID:T_ID + P] = np.eye(P)
    return t


_INS = ["x", "c", "ada_w", "ada_b", "norm1_w", "w_in", "ssm_conv_w", "ssm_conv_b", "ssm_dt_bias",
        "ssm_a_log", "ssm_d", "ssm_norm_w", "w_br_ret", "w_br_ssm", "w_br_att", "w_out", "norm2_w",
        "w_ff1", "w_ff3", "w_ff2", "final_norm_w"]


def kernel(**inputs):
    import numpy as _np
    import concourse.bacc as _bacc
    from concourse import mybir as _mybir
    from concourse.bass_utils import run_bass_kernel_spmd as _run

    nc = _bacc.Bacc("TRN2", target_bir_lowering=False, num_devices=1, dynamic_dma_scratch_size=1024)
    arrays, args = {}, []
    named = {name: _np.ascontiguousarray(inputs[name]) for name in _INS}
    named["table"] = tables()
    for name, a in named.items():
        arrays[f"in_{name}_dram"] = a
        args.append(nc.dram_tensor(f"in_{name}_dram", a.shape, _mybir.dt.from_np(a.dtype), kind="ExternalInput").ap())
    args.append(nc.dram_tensor("out_0_dram", (1, S, D), _mybir.dt.float32, kind="ExternalOutput").ap())
    build(nc, *args)
    r = _run(nc, [arrays], core_ids=[0])
    return r.results[0]["out_0_dram"]
```

```python
from contextlib import ExitStack

import numpy as np
import concourse.bass as bass
from concourse import mybir

P = 128
D = 1024
KB = D // P
S = 256
NT = S // P
L = 2
EPS = 1e-6
RH, RQK, RV = 4, 128, 256
SH, SHD, SG = 16, 64, 4
AG, AS, AHD = 3, 4, 64
FF = 2816
FB = FF // P
COL = 256
HALF = KB * COL // 2
XBC = 2048
C_QK, C_TOK, C_XBC = 0, 1024, 4096
C_DT = C_XBC + XBC
C_AQK = C_DT + SH
C_AV = C_AQK + 2 * AG * AS * AHD
C_GATE = C_AV + AG * AS * AHD
EARLY, LATE = 8, 16
EARLY_SLOTS = 6
EARLY_PE = 6
PLAN = [("ada", 1), ("qk", 1), ("ada", 1), ("qk", 2), ("ada", 1), ("qk", 1), ("xbc", 2)]
PLAN += [("ada", 1), ("xbc", 3)] * 2 + [("ada", 1), ("aqk", 3)] * 2 + [("ada", 1), ("tok", 3)] * 2
PLAN += [("ada", 1), ("tok", 1), ("dt", 1), ("av", 1), ("ada", 1), ("av", 2)]
PLAN += [("tok", 1), ("ada", 1), ("gate", 2), ("ada", 1), ("z", 1)]
PLAN += [("gate", 2), ("ada", 1), ("gate", 1), ("z", 1)] * 3 + [("gate", 1)]
PLAN += [("ret", 4), ("att", 1), ("ssm", 4), ("out", 4), ("ff", 22), ("ff2", 11)]
KIND = [k for k, n in PLAN for _ in range(n)]
UNITS = len(KIND)
SPLIT_UNITS = [r for r, k in enumerate(KIND) if k != "ada"]
SPLITS = len(SPLIT_UNITS)
S_OF = {r: i for i, r in enumerate(SPLIT_UNITS)}
A_OF = {r: i for i, r in enumerate(r for r, k in enumerate(KIND) if k == "ada")}
N_QK, N_XBC, N_AQK, N_TOK, N_AV = 4, 8, 6, 8, 3
U_DT, U_ATT, U_SSM = (KIND.index(k) for k in ("dt", "att", "ssm"))
U_OUT, N_OUT = KIND.index("out"), 4
U_FF, N_FF = KIND.index("ff"), 22
U_FF2, N_FF2 = KIND.index("ff2"), 11
assert UNITS % 4 == 0 and SPLITS % 2 == 0
RAW = 4
SPL = 2
ROW_BANK = (6, 7, 0)

F32 = mybir.dt.float32
F32R = mybir.dt.float32r
ALU = mybir.AluOpType
ACT = mybir.ActivationFunctionType
AXX = mybir.AxisListType.X

T_COS, T_SIN, T_RET, T_ATT = 0, 256, 512, 1536
T_CB, T_TRI, T_ID = 2304, 2688, 2816
T_END = 2944
Q_ADAB, Q_N1, Q_N2, Q_SN, Q_CB = 0, 48, 56, 64, 72
Q_CW, Q_DTB, Q_ALOG, Q_DSK = 88, 152, 168, 184
Q_END = 200
N_ROW0 = 88


class Unit:

    def __init__(self, base, per=0, j=None):
        self.base, self.per, self.j = base, per, j

    def plus(self, d):
        return Unit(self.base + d, self.per, self.j)

    def over(self, k, times=1, off=0):
        c = self.base // k * times + off
        return c if self.j is None else self.j * (self.per // k * times) + c

    def mod(self, k):
        assert self.j is None or self.per % k == 0
        return self.base % k

    def split(self):
        return Unit(S_OF[self.base], self.per, self.j)

    def ahead(self):
        n = S_OF[self.base] + SPL
        if self.j is not None:
            return self.plus(SPL)
        return Unit(SPLIT_UNITS[n]) if n < SPLITS else None


def nth(kind, i):
    return Unit([r for r, k in enumerate(KIND) if k == kind][i])


SUM_LAG = 5


def sums_due(kind, i):
    r = nth(kind, i).base
    before = max(q for q in [-SUM_LAG - 1] + SPLIT_UNITS if q < r)
    return [a for q, a in A_OF.items() if before - SUM_LAG < q <= r - SUM_LAG]


def units(eng, base, count, per, fn):
    full = count // per
    done = 0
    if full > 1:
        with eng.Fori(0, full) as j:
            for b in range(per):
                fn(Unit(base + b, per, j), Unit(b, per, j))
        done = full * per
    for b in range(done, count):
        fn(Unit(base + b), Unit(b))


def build(nc, x, c, ada_w, ada_b, norm1_w, w_in, conv_w, conv_b, dt_bias, a_log, ssm_d, ssm_norm_w,
          w_br_ret, w_br_ssm, w_br_att, w_out, norm2_w, w_ff1, w_ff3, w_ff2, final_norm_w,
          table, out):
    with ExitStack() as ctx:
        at = [nc.sbuf_base + (-nc.sbuf_base) % 64]

        def sb(name, shape, dt=F32, offset=None):
            size = 4 * int(np.prod(shape[1:]))
            if offset is None:
                offset = at[0]
                at[0] += size + (-size) % 32
            return nc.alloc_sbuf_tensor_at(name, shape, dt, offset=offset)

        def region(size):
            at[0] += size
            return at[0] - size

        def sem(name):
            return ctx.enter_context(nc.semaphore(name))

        raw = sb("raw", [P, RAW, 2 * HALF])
        w_hi = sb("w_hi", [P, SPL, 2 * HALF], F32R)
        w_lo = sb("w_lo", [P, SPL, 2 * HALF], F32R)
        xf = sb("xf", [P, KB, S])
        r_h = region(2 * KB * S * 4)
        h_hi = sb("h_hi", [P, KB, S], F32R, r_h)
        h_lo = sb("h_lo", [P, KB, S], F32R, r_h + KB * S * 4)
        m_hi = sb("m_hi", [P, KB, S], F32R, r_h)
        m_lo = sb("m_lo", [P, KB, S], F32R, r_h + KB * S * 4)
        r_z1 = region(36 * S * 4)
        xbc = sb("xbc", [P, 16, S], F32, r_z1)
        aqk = sb("aqk", [P, 12, S], F32, r_z1 + 16 * S * 4)
        qk = sb("qk", [P, 4, 2, S], F32, r_z1 + 28 * S * 4)
        y_hi = sb("y_hi", [P, 18, S], F32R, r_z1)
        y_lo = sb("y_lo", [P, 18, S], F32R, r_z1 + 18 * S * 4)
        sq = sb("sq", [P, KB, S], F32, r_z1)
        hn = sb("hn", [P, KB, S], F32, r_z1 + KB * S * 4)
        r_tok = region(3 * NT * D * 4)
        tok = sb("tok", [P, 3, NT, D], F32, r_tok)
        mixed = sb("mixed", [P, KB, S], F32, r_tok + NT * D * 4)
        av = sb("av", [P, NT, AG * AS * AHD])
        yatt = sb("yatt", [P, NT, AS * AHD])
        r_gate = region(24 * S * 4)
        gates = sb("gates", [P, 24, S], F32, r_gate)
        x_tok = sb("x_tok", [P, NT, D], F32, r_gate)
        ada_row = sb("ada_row", [1, EARLY * COL], F32, r_gate + 16 * S * 4)
        tab = sb("tab", [P, T_END])
        f_hi = sb("f_hi", [P, FB, S], F32R, r_z1)
        f_lo = sb("f_lo", [P, FB, S], F32R, r_gate)
        r_l = region(SG * 384 * 4)
        decay = sb("decay", [P, 4, 384], F32, r_l)
        p_t = sb("p_t", [P, 9, P], F32, r_l)
        xpad = sb("xpad", [P, 2, 2, S + 3], F32, r_l)
        rope_c = sb("rope_c", [P, 2, S], F32, r_l)
        rope_s = sb("rope_s", [P, 2, S], F32, r_l + 2 * S * 4)
        sil = sb("sil", [P, 2 * S], F32, r_l)
        hid = sb("hid", [P, 2 * S], F32, r_l + 2 * S * 4)
        br = sb("br", [P, 2, 2 * S], F32, r_l)
        att_s = sb("att_s", [P, 9 * P])
        cbm = sb("cbm", [P, 384])
        xdt = sb("xdt", [P, NT, 4 * SHD])
        ytmp = sb("ytmp", [P, NT, 4 * SHD])
        m_ret = sb("m_ret", [P, 384])
        mac = sb("mac", [P, 4, COL])
        acc = sb("acc", [P, 2, COL])
        junk = sb("junk", [P, S])
        std2 = sb("std2", [P, NT])
        root = sb("root", [P, NT])
        rows = sb("rows", [P, 2, P])
        rowv = sb("rowv", [1, 3 * SH])
        crow = sb("crow", [16, P], F32, r_gate + NT * D * 4)
        early_t = sb("early_t", [P, 3, 2 * HALF], F32, r_tok)
        early_h = sb("early_h", [P, 2, 2 * HALF], F32, r_h)
        early_z = sb("early_z", [P, 2 * HALF], F32, r_z1 + 24 * S * 4)
        early = [early_t[:, 0, :], early_t[:, 1, :], early_t[:, 2, :], early_h[:, 0, :], early_h[:, 1, :],
                 early_z[:, :]]
        acc_first = sb("acc_first", [P, EARLY - EARLY_PE, COL], F32, r_gate + 10 * S * 4)
        acc_early = sb("acc_early", [P, EARLY, COL], F32, r_tok + 4 * HALF * 4)
        par = sb("par", [P, Q_END])
        fnw = sb("fnw", [P, KB])
        c32 = sb("c32", [P, KB])
        ada = sb("ada", [P, 48])
        a1 = sb("a1", [P, 2, KB])
        g1h = sb("g1h", [P, KB])
        eps = sb("eps", [P, 1])
        one = sb("one", [P, 1])
        dt_f = sb("dt_f", [P, S])
        dt_x = sb("dt_x", [P, NT * SH])
        dt_e = sb("dt_e", [P, NT * SH])
        dt = sb("dt", [P, NT, SH])
        exp_a = sb("exp_a", [P, SH])
        d_a = sb("d_a", [P, NT, SH])
        cs = sb("cs", [P, NT, SH])
        negmax = sb("negmax", [P, 2])
        ssum = sb("ssum", [P, 2])
        rsum = sb("rsum", [P, 2])
        bst = sb("bst", [P, NT, 6])
        mv = sb("mv", [P, RH, NT, 2])
        ss = sb("ss", [P, SG, NT])
        sd = sb("sd", [P, 2, 8])
        ri = sb("ri", [P, 2, 8])
        assert at[0] <= nc.sbuf_usable_end, (at[0], nc.sbuf_usable_end)

        bank = [ctx.enter_context(nc.psum_tensor(f"bank{i}", [P, 512], F32)) for i in range(8)]
        cos, sin = tab[:, T_COS:T_COS + S], tab[:, T_SIN:T_SIN + S]
        ret_mask = tab[:, T_RET:T_RET + RH * S].rearrange("p (h t) -> p h t", h=RH)
        att_mask = tab[:, T_ATT:T_ATT + AG * S].rearrange("p (g t) -> p g t", g=AG)
        cb_mask = tab[:, T_CB:T_CB + 384]
        ones = tab[:, T_CB + P:T_CB + 2 * P]
        tri = [tab[:, T_TRI:T_TRI + P], tab[:, T_CB:T_CB + P]]
        ident = tab[:, T_ID:T_ID + P]
        conv_wp = par[:, Q_CW:Q_CW + 64].rearrange("p (j k) -> p j k", j=4)

        s_c = sem("c_and_identity_landed")
        s_x = sem("x_landed")
        s_tab = sem("masks_landed")
        early_landed = [sem(f"early_landed{i}") for i in range(EARLY_SLOTS)]
        s_par = sem("params_landed")
        landed = [sem(f"raw_landed{i}") for i in range(RAW)]
        hi_ready = sem("w_hi_ready")
        lo_ready = sem("w_lo_ready")
        half_done = sem("half_multiplied")
        bank_free = [sem("bank0_free"), sem("bank1_free")]
        x_turned = sem("x_transposed")
        c_turned = sem("c_transposed")
        c_ready = sem("c_silu_ready")
        x_ready = sem("x_ready")
        par_turned = sem("params_transposed")
        row_ps = sem("modulation_row_in_psum")
        row_ready = sem("modulation_row_copied")
        first_ready = sem("first_partial_sums_ready")
        early_read = sem("early_raw_read")
        early_ready = sem("early_partial_sums_ready")
        mac_done = sem("ada_raw_read")
        acc_ready = sem("ada_partial_sums_ready")
        acc_summed = sem("ada_partial_sums_read")
        ada_taken = sem("late_modulation_taken")
        sq_ready = sem("squares_ready")
        ss_ready = sem("sumsq_ready")
        sum_ready = sem("squares_added_over_blocks")
        sd_ready = sem("std_ready")
        root_ready = sem("inverse_std_ready")
        root_ps = sem("inverse_std_as_rows")
        hn_ready = sem("normed_ready")
        h_rounded = sem("h_hi_ready")
        h_split = sem("h_split")
        rot_out = sem("rotary_done")
        xpad_ready = sem("conv_input_ready")
        conv_ready = sem("conv_ready")
        xbc_ready = sem("xbc_ready")
        dtf_ready = sem("dt_input_copied")
        dt_turned = sem("dt_input_transposed")
        dtx_ready = sem("dt_input_ready")
        dte_ready = sem("dt_exp_ready")
        da_ready = sem("dA_ready")
        cs_ps = sem("cumsum_in_psum")
        sc_ps = sem("scores_in_psum")
        mret_ready = sem("retention_weights_ready")
        max_ready = sem("attention_max_ready")
        p_ready = sem("attention_exp_ready")
        pv_ret = sem("retention_out_in_psum")
        pt_ps = sem("attention_probs_turned")
        pt_ready = sem("attention_probs_copied")
        yret_ready = sem("retention_out_ready")
        s2_ps = sem("attention_out_xs_cb_in_psum")
        s2_ready = sem("attention_out_xs_cb_ready")
        csb_ps = sem("cumsum_rows_in_psum")
        seg_ready = sem("segments_ready")
        dec_ready = sem("decay_ready")
        mssd_ready = sem("ssd_weights_ready")
        y_ps = sem("ssd_out_in_psum")
        yssd_ready = sem("ssd_out_ready")
        ssq_ready = sem("group_stats_ready")
        gsd_ready = sem("group_std_ready")
        ynorm_ready = sem("branch_normed")
        yt_ps = sem("branch_turned")
        yt_hi = sem("branch_hi_ready")
        yt_lo = sem("branch_lo_ready")
        mix_ready = sem("mixed_ready")
        mix_hi = sem("mixed_hi_ready")
        mix_lo = sem("mixed_lo_ready")
        hid_ready = sem("hidden_ready")
        hid_hi = sem("hidden_hi_ready")
        hid_lo = sem("hidden_lo_ready")
        ffn_pair = sem("ffn_pair_in_psum")
        out_turned = sem("out_transposed")
        out_ready = sem("out_ready")
        stored = sem("out_stored")

        rearr = {
            "ada": ada_w, "in": w_in, "ret": w_br_ret, "ssm": w_br_ssm, "att": w_br_att,
            "out": w_out, "ff1": w_ff1, "ff3": w_ff3, "ff2": w_ff2,
        }
        w_dram = {k: v.rearrange("l (k p) n -> p (l k) n", p=P) for k, v in rearr.items()}

        def n_landed(l, u):
            return l * (16 * UNITS // RAW) + u.over(RAW, 16, 16)

        def n_half(l, u, h):
            return l * (2 * SPLITS) + u.split().over(1, 2, h + 1)

        def n_bank(l, u):
            return l * (SPLITS // 2) + u.split().over(2, 1, 1)

        FREE_HALVES = 2 * SPL
        FREE_RAW = 2 * RAW

        def cols_of(u):
            return KB * SH if u.j is None and u.base == U_DT else 2 * HALF

        def parts(u, h, dst, src, lead=None):
            cn = cols_of(u)
            half = slice(h * HALF, h * HALF + cn // 2)
            from_raw = slice(h * cn // 2, (h + 1) * cn // 2)
            if KIND[u.base] == "qk":
                mine = dict(b=2, a=2, c=RQK // 2)
                for b in range(2):
                    ops = [dst[:, half].rearrange("p (k b a c) -> p k b a c", **mine)[:, :, b, :, :],
                           src[:, half].rearrange("p (k a b c) -> p k a b c", **mine)[:, :, :, b, :]]
                    if lead is not None:
                        ops.append(lead[:, half].rearrange("p (k b a c) -> p k b a c", **mine)[:, :, b, :, :])
                    yield ops
            else:
                yield [dst[:, half], src[:, from_raw]] + ([lead[:, half]] if lead is not None else [])

        block = ctx.enter_context(nc.Block())

        @block.sync
        def _(sp):
            sp.dma_start(crow[0:8, :], c.rearrange("a (k p) -> (a k) p", p=P)).then_inc(s_c, 16)
            sp.dma_start(crow[8:16, :], final_norm_w.rearrange("(k p) -> k p", p=P)).then_inc(s_c, 16)

            def load_early(layer, i, slot):
                sp.dma_start(early[slot].rearrange("p (k n) -> p k n", k=KB),
                             w_dram["ada"][:, bass.ds(layer * KB, KB), i * COL:(i + 1) * COL])\
                  .then_inc(early_landed[slot], 16)
            for i in range(EARLY):
                if i >= EARLY_SLOTS:
                    sp.wait_ge(row_ps, i - EARLY_SLOTS + 1)
                load_early(0, i, i % EARLY_SLOTS)
            with sp.Fori(0, L) as l:
                pieces = [(ada_b, 48, Q_ADAB), (norm1_w, 8, Q_N1), (norm2_w, 8, Q_N2),
                          (ssm_norm_w, 8, Q_SN), (conv_b, 16, Q_CB)]
                for src, n, q in pieces:
                    sp.dma_start(rows[q:q + n, 0, :],
                                 src.rearrange("l (k p) -> (l k) p", p=P)[bass.ds(l * n, n), :])\
                      .then_inc(s_par, 16)
                sp.dma_start(rows[0:64, 1, :],
                             conv_w.rearrange("l j (k p) -> (l j k) p", p=P)[bass.ds(l * 64, 64), :])\
                  .then_inc(s_par, 16)
                for n, src in enumerate((dt_bias, a_log, ssm_d)):
                    sp.dma_start(rowv[0:1, n * SH:(n + 1) * SH], src[bass.ds(l, 1), :]).then_inc(s_par, 16)

                def load(u, name, k0, kn, col, cn):
                    s = u.mod(RAW)
                    before = u.plus(-RAW)
                    a = A_OF.get(before.base)
                    if a is not None:
                        sp.wait_ge(mac_done, l * LATE + a + 1)
                    elif before.base >= 0:
                        sp.wait_ge(lo_ready, n_half(l, before, FREE_RAW + 1))
                    else:
                        sp.wait_ge(lo_ready, l * (2 * SPLITS) + FREE_RAW + 2 * before.base + 2)
                    dst = raw[:, s, 0:kn * cn].rearrange("p (k n) -> p k n", k=kn)
                    sp.dma_start(dst, w_dram[name][:, bass.ds(k0, kn), bass.ds(col, cn)])\
                      .then_inc(landed[s], 16)

                first = {"qk": C_QK, "xbc": C_XBC, "aqk": C_AQK, "tok": C_TOK, "av": C_AV, "gate": C_GATE,
                         "z": C_TOK + N_TOK * COL}
                seen = {}
                for r, kind in enumerate(KIND[:U_FF]):
                    i = seen[kind] = seen.get(kind, -1) + 1
                    if kind == "ada":
                        i += EARLY
                    if kind == "dt":
                        load(Unit(r), "in", l * KB, KB, C_DT, SH)
                    elif kind == "att":
                        load(Unit(r), "att", l * 2, 2, 0, D)
                    elif kind in first:
                        load(Unit(r), "in", l * KB, KB, first[kind] + i * COL, COL)
                    else:
                        load(Unit(r), kind, l * KB, KB, i * COL, COL)

                def ff(u, i):
                    load(u, "ff3" if i.base % 2 else "ff1", l * KB, KB, i.over(2, COL, 0), COL)
                next_rows = sp.snap((l + 1) % L * KB)
                for i in range(6):
                    ff(Unit(U_FF + i), Unit(i))
                with sp.Fori(0, 4) as j:
                    for b in range(4):
                        ff(Unit(U_FF + 6 + b, 4, j), Unit(6 + b, 4, j))
                        if b % 2:
                            with sp.If(l < L - 1):
                                sp.wait_ge(early_read, l * EARLY + j * 2 + 1 + b // 2)
                                sp.dma_start(early[b // 2].rearrange("p (k n) -> p k n", k=KB),
                                             w_dram["ada"][:, bass.ds(next_rows, KB),
                                                           bass.ds(j * (2 * COL) + b // 2 * COL, COL)])\
                                  .then_inc(early_landed[b // 2], 16)

                def ff2(u, i):
                    load(u, "ff2", l * FB + i.over(1, 2, 0), 2, 0, D)
                for i in range(3):
                    ff2(Unit(U_FF2 + i), Unit(i))
                units_from(sp, U_FF2, 3, N_FF2, 4, ff2)
            for t in range(NT):
                sp.wait_ge(out_ready, t + 1)
                sp.dma_start(out[0, t * P:(t + 1) * P, :], x_tok[:, t, :]).then_inc(stored, 16)
            sp.wait_ge(stored, 16 * NT)

        @block.tensor
        def _(pe):
            pe.sem_inc(half_done, FREE_HALVES)
            pe.sem_inc(acc_summed, 1)

            def three(o, hi, lo, xh, xl, first, last, swap=False):
                ps = [(hi, xh), (hi, xl), (lo, xh)]
                if swap:
                    ps = [(xh, hi), (xh, lo), (xl, hi)]
                for n, (a, b) in enumerate(ps):
                    done = pe.matmul(o, a, b, start=first and n == 0, stop=last and n == 2,
                                     skip_group_check=True)
                return done

            def two_halves(l, u, body, own_bank=True, before=None):
                s = u.split().mod(SPL)
                for h in range(2):
                    pe.wait_ge(lo_ready, n_half(l, u, FREE_RAW + h))
                    if h == 0 and own_bank:
                        pe.wait_ge(bank_free[u.split().mod(2)], n_bank(l, u))
                    if before:
                        before(h)
                    body(s, h).then_inc(half_done, 1)
                if not own_bank:
                    pe.sem_inc(bank_free[u.split().mod(2)], 1)

            def feature(l, u, ah=h_hi, al=h_lo, k0=0, before=None):
                def body(s, h):
                    hi, lo = (w[:, s, :].rearrange("p (k n) -> p k n", n=COL) for w in (w_hi, w_lo))
                    for k in range(h * 4, h * 4 + 4):
                        if before and k % 2 == 0:
                            before(k // 2)
                        for m in range(2):
                            o = bank[u.split().mod(2)][:, m * S:(m + 1) * S]
                            mc = slice(m * P, (m + 1) * P)
                            last = three(o, hi[:, k, mc], lo[:, k, mc], ah[:, k0 + k, :], al[:, k0 + k, :],
                                         k == 0 and m == 0, k == KB - 1)
                    return last
                two_halves(l, u, body)

            def token(l, u):
                def body(s, h):
                    hi, lo = (w[:, s, :].rearrange("p (k n) -> p k n", n=COL) for w in (w_hi, w_lo))
                    for t in range(NT):
                        o = bank[u.split().mod(2)][:, t * S:(t + 1) * S]
                        tk = slice(t * P, (t + 1) * P)
                        for k in range(h * 4, h * 4 + 4):
                            last = three(o, hi[:, k, :], lo[:, k, :], h_hi[:, k, tk], h_lo[:, k, tk],
                                         k == 0 and t == 0, k == KB - 1, swap=True)
                    return last
                two_halves(l, u, body)

            def narrow(l, u):
                def body(s, h):
                    hi, lo = (w[:, s, h * HALF:h * HALF + KB * SH // 2].rearrange("p (k n) -> p k n", n=SH)
                              for w in (w_hi, w_lo))
                    for k in range(4):
                        last = three(bank[u.split().mod(2)][0:SH, 0:S], hi[:, k, :], lo[:, k, :],
                                     h_hi[:, 4 * h + k, :], h_lo[:, 4 * h + k, :],
                                     h == 0 and k == 0, h == 1 and k == 3)
                    return last
                two_halves(l, u, body)

            def row_unit(i):
                pe.wait_ge(early_landed[i % EARLY_SLOTS], 16 * (i // EARLY_SLOTS + 1))
                w = early[i % EARLY_SLOTS].rearrange("p (k n) -> p k n", n=COL)
                for k in range(KB):
                    last = pe.matmul(bank[ROW_BANK[i // 2]][0:1, i % 2 * COL:(i % 2 + 1) * COL],
                                     c32[:, k:k + 1], w[:, k, :], start=k == 0, stop=k == KB - 1)
                last.then_inc(row_ps, 1)

            def turn_row(q):
                pe.wait_ge(row_ready, q + 1)
                for m in range(4 * q, min(4 * q + 4, 2 * EARLY_PE)):
                    pe.matmul(bank[3][:, S + m:S + m + 1], ada_row[0:1, m * P:(m + 1) * P],
                              ones[0:1, 0:1], start=True, stop=True)

            def ada_sum(l, a):
                pe.wait_ge(acc_ready, l * LATE + a + 1)
                for m in range(2):
                    last = pe.matmul(bank[4][:, 2 * a + m:2 * a + m + 1],
                                     acc[:, a % 2, m * P:(m + 1) * P], ones[:, 0:1], start=True, stop=True)
                last.then_inc(acc_summed, 1)

            def whole_rows(l, u, ah, al, k0, first, last_unit, before=None, pair_done=None):
                def body(s, h):
                    hi, lo = (w[:, s, :].rearrange("p (k n) -> p k n", n=D) for w in (w_hi, w_lo))
                    for m in range(KB):
                        o = bank[4 + m // 2][:, m % 2 * S:(m % 2 + 1) * S]
                        mc = slice(m * P, (m + 1) * P)
                        last = three(o, hi[:, h, mc], lo[:, h, mc], ah[:, k0 + h, :], al[:, k0 + h, :],
                                     first and h == 0 and m % 2 == 0, last_unit and h == 1)
                        if pair_done and h == 1 and m % 2 and m < KB - 1:
                            last.then_inc(pair_done, 1)
                    return last
                two_halves(l, u, body, own_bank=False, before=before)

            def norm_sum(n):
                pe.wait_ge(sum_ready, n + 1)
                for t in range(NT):
                    last = pe.matmul(bank[2][:, t:t + 1], sq[:, 0, t * P:(t + 1) * P], ones[:, 0:1],
                                     start=True, stop=True)
                last.then_inc(ss_ready, 1)

            def root_rows(n):
                pe.wait_ge(root_ready, n + 1)
                for t in range(NT):
                    last = pe.matmul(bank[2][:, S + t * P:S + (t + 1) * P],
                                     root[:, t:t + 1].to_broadcast([P, P]), ident, start=True, stop=True)
                last.then_inc(root_ps, 1)

            pe.wait_ge(s_c, 16 * 3)
            pe.transpose(bank[6][:, 0:16], crow[:, :], ident[0:16, 0:16]).then_inc(c_turned, 1)
            pe.wait_ge(c_ready, 1)
            for i in range(EARLY_PE):
                row_unit(i)
                if i == 1:
                    pe.wait_ge(s_x, 16)
                    for k in range(KB):
                        for t in range(NT):
                            last = pe.transpose(bank[2 + k // 2][:, k % 2 * S + t * P:k % 2 * S + (t + 1) * P],
                                                x_tok[:, t, k * P:(k + 1) * P], ident)
                    last.then_inc(x_turned, 1)
                if i == 2:
                    pe.wait_ge(x_ready, 4)
                if i % 2 == 0 and i:
                    turn_row(i // 2 - 1)
                if i == 4:
                    norm_sum(0)
            root_rows(0)
            turn_row(EARLY_PE // 2 - 1)
            for i in range(EARLY - EARLY_PE):
                pe.wait_ge(first_ready, i + 1)
                for m in range(2):
                    c0 = S + 2 * (EARLY_PE + i) + m
                    pe.matmul(bank[3][:, c0:c0 + 1], acc_first[:, i, m * P:(m + 1) * P], ones[:, 0:1],
                              start=True, stop=True)

            with pe.Fori(0, L) as l:
                pe.wait_ge(s_par, l * 144 + 144)
                pe.transpose(bank[3][:, 0:N_ROW0], rows[0:N_ROW0, 0, :], ident[0:N_ROW0, 0:N_ROW0])
                pe.transpose(bank[3][:, Q_CW:Q_CW + 64], rows[0:64, 1, :], ident[0:64, 0:64])
                pe.matmul(bank[3][:, Q_DTB:Q_END], ones[0:1, :], rowv[:, :], start=True, stop=True)\
                  .then_inc(par_turned, 1)
                def h_pairs(n):
                    return lambda i: pe.wait_ge(h_split, (l * 2 + n) * 4 + i + 1)
                def sums(kind, i):
                    for a in sums_due(kind, i):
                        ada_sum(l, a)

                for i in range(N_QK):
                    feature(l, nth("qk", i), before=h_pairs(0))
                    sums("qk", i)
                for i in range(N_XBC):
                    feature(l, nth("xbc", i))
                    sums("xbc", i)
                for i in range(N_AQK):
                    feature(l, nth("aqk", i))
                    sums("aqk", i)
                for i in range(N_TOK - 1):
                    token(l, nth("tok", i))
                    sums("tok", i)
                narrow(l, Unit(U_DT))
                for i in range(N_AV):
                    token(l, nth("av", i))
                    sums("av", i)
                    if i == 0:
                        pe.wait_ge(dtf_ready, l + 1)
                        for t in range(NT):
                            last = pe.transpose(bank[3][:, t * P:(t + 1) * P], dt_f[:, t * P:(t + 1) * P], ident)
                        last.then_inc(dt_turned, 1)

                def s_scores(j):
                    q0, pr = j % 2 * 64, j // 2
                    hd = slice(q0, q0 + 64)
                    if j == 0:
                        pe.wait_ge(rot_out, l * 4 + 4)
                    else:
                        pe.wait_ge(seg_ready, l * 4 + j)
                    for t in range(NT):
                        for b in range(2):
                            pe.matmul(bank[2][:, t * S:t * S + S - t * P],
                                      qk[hd, 2 + pr, b, t * P:(t + 1) * P], qk[hd, pr, b, t * P:S],
                                      start=b == 0, stop=b == 1)
                    for g in range(AG):
                        pe.matmul(bank[5][:, g * P:(g + 1) * P], aqk[hd, 2 * g + pr, 0:P],
                                  aqk[hd, 6 + 2 * g + pr, 0:P], start=True, stop=True)
                    for g in range(AG):
                        last = pe.matmul(bank[6 + g // 2][:, g % 2 * S:(g % 2 + 1) * S],
                                         aqk[hd, 2 * g + pr, P:S], aqk[hd, 6 + 2 * g + pr, :],
                                         start=True, stop=True)
                    last.then_inc(sc_ps, 1)

                def s_ret_out_and_turn(j):
                    n = l * 4 + j + 1
                    pe.wait_ge(mret_ready, n)
                    v = [tok[:, 0, t, j * RV:(j + 1) * RV] for t in range(NT)]
                    pe.matmul(bank[2][:, 0:S], m_ret[:, 0:P], v[0], start=True, stop=True)
                    pe.matmul(bank[2][:, S:2 * S], m_ret[:, P:2 * P], v[0], start=True, stop=False)
                    pe.matmul(bank[2][:, S:2 * S], m_ret[:, 2 * P:3 * P], v[1], start=False, stop=True)\
                      .then_inc(pv_ret, 1)
                    pe.wait_ge(p_ready, n)
                    for i in range(9):
                        last = pe.transpose(bank[5 + i // 4][:, i % 4 * P:(i % 4 + 1) * P],
                                            att_s[:, i * P:(i + 1) * P], ident)
                    last.then_inc(pt_ps, 1)

                def s_att_out_xs_cb(j):
                    n = l * 4 + j + 1
                    pe.wait_ge(pt_ready, n)

                    def value(g, t):
                        hcol = (g * AS + j) * AHD
                        return av[:, t, hcol:hcol + AHD]
                    for g in range(AG):
                        pe.matmul(bank[5][:, 0:AHD], p_t[:, g, :], value(g, 0), start=g == 0, stop=g == AG - 1)
                    for i in range(6):
                        pe.matmul(bank[5][:, AHD:2 * AHD], p_t[:, 3 + i, :], value(i // 2, i % 2),
                                  start=i == 0, stop=i == 5)
                    if j == 0:
                        pe.wait_ge(xbc_ready, l * N_XBC + N_XBC)
                    else:
                        pe.wait_ge(yssd_ready, n - 1)
                    for t in range(NT):
                        for b in range(2):
                            pe.transpose(bank[6][:, t * S + b * P:t * S + (b + 1) * P],
                                         xbc[:, 2 * j + b, t * P:(t + 1) * P], ident)
                    pe.matmul(bank[3][:, 0:S], xbc[:, 8 + j, 0:P], xbc[:, 12 + j, :], start=True, stop=True)
                    pe.matmul(bank[3][:, S:S + P], xbc[:, 8 + j, P:S], xbc[:, 12 + j, P:S],
                              start=True, stop=True).then_inc(s2_ps, 1)

                def s_cumsum_rows(j):
                    for r in range(4):
                        h = 4 * j + r
                        for t in range(NT):
                            o = r % 2 * S + t * P
                            last = pe.matmul(bank[7 if r < 2 else 5][:, o:o + P],
                                             d_a[:, t, h:h + 1].to_broadcast([P, P]), tri[t],
                                             start=True, stop=True)
                    last.then_inc(csb_ps, 1)

                def s_ssd_out(j):
                    pe.wait_ge(mssd_ready, l * 4 + j + 1)
                    for r in range(4):
                        pc = slice(r * SHD, (r + 1) * SHD)
                        pe.matmul(bank[3][:, r * SHD:(r + 1) * SHD], decay[:, r, 0:P], xdt[:, 0, pc],
                                  start=True, stop=True)
                        o = bank[3][:, S + r * SHD:S + (r + 1) * SHD]
                        pe.matmul(o, decay[:, r, P:2 * P], xdt[:, 0, pc], start=True, stop=False)
                        last = pe.matmul(o, decay[:, r, 2 * P:3 * P], xdt[:, 1, pc], start=False, stop=True)
                    last.then_inc(y_ps, 1)

                def gate_unit(g):
                    if g < 0:
                        token(l, nth("tok", N_TOK - 1))
                        sums("tok", N_TOK - 1)
                    else:
                        feature(l, nth("gate", g))
                        sums("gate", g)

                for j in range(4):
                    gate_unit(3 * j - 1)
                    if j == 0:
                        pe.wait_ge(da_ready, l + 1)
                        for t in range(NT):
                            last = pe.matmul(bank[3][:, t * SH:(t + 1) * SH], tri[t], d_a[:, t, :],
                                             start=True, stop=True)
                        last.then_inc(cs_ps, 1)
                    s_scores(j)
                    gate_unit(3 * j)
                    if j:
                        s_ssd_out(j - 1)
                    s_ret_out_and_turn(j)
                    gate_unit(3 * j + 1)
                    s_att_out_xs_cb(j)
                    token(l, nth("z", j))
                    sums("z", j)
                    pe.wait_ge(s2_ready, l * 4 + j + 1)
                    s_cumsum_rows(j)
                gate_unit(11)
                done = nth("gate", 11).base - SUM_LAG
                for a in (a for q, a in A_OF.items() if q > done):
                    ada_sum(l, a)

                def turn(i):
                    if i == 0 or i == 5:
                        pe.wait_ge(ynorm_ready, l * 2 + i // 5 + 1)
                    if i == 4:
                        pe.wait_ge(ada_taken, l + 1)
                    if i == 2:
                        pe.wait_ge(seg_ready, l * 4 + 4)
                    if i >= 7:
                        pe.wait_ge(yt_lo, l * 9 + i - 1)
                    for b in range(2):
                        for t in range(NT):
                            if i == 4:
                                src = yatt[:, t, b * P:(b + 1) * P]
                            else:
                                k = (i if i < 4 else i - 5) * 2 + b
                                src = tok[:, 0 if i < 4 else 2, t, k * P:(k + 1) * P]
                            last = pe.transpose(bank[turn_bank(i)][:, b * S + t * P:b * S + (t + 1) * P],
                                                src, ident)
                    last.then_inc(yt_ps, 1)
                for i in range(5):
                    turn(i)

                def from_turned(first):
                    return lambda i: pe.wait_ge(yt_lo, l * 9 + first + i + 1)
                for i in range(4):
                    feature(l, nth("ret", i), y_hi, y_lo, 0, from_turned(0))
                    if i == 1:
                        s_ssd_out(3)
                turn(5)
                turn(6)

                def banks_free(h):
                    pe.wait_ge(yt_lo, l * 9 + 5)
                whole_rows(l, Unit(U_ATT), y_hi, y_lo, 8, True, True, before=banks_free)
                turn(7)
                turn(8)
                for i in range(4):
                    feature(l, Unit(U_SSM + i), y_hi, y_lo, 10, from_turned(5))
                for i in range(N_OUT):
                    feature(l, Unit(U_OUT + i), m_hi, m_lo,
                            before=lambda i: pe.wait_ge(mix_lo, l * 4 + i + 1))
                norm_sum(l * 2 + 1)
                root_rows(l * 2 + 1)

                def ffn_in(u, i):
                    feature(l, u, before=h_pairs(1) if i.base % 4 == 0 else None)
                units(pe, U_FF, N_FF, 4, ffn_in)
                for i in range(N_FF2):
                    whole_rows(l, Unit(U_FF2 + i), f_hi, f_lo, 2 * i, i == 0, i == N_FF2 - 1,
                               before=lambda h, i=i: pe.wait_ge(hid_lo, l * (N_FF // 2) + i + 1),
                               pair_done=ffn_pair if i == N_FF2 - 1 else None)
                with pe.If(l < L - 1):
                    pe.wait_ge(early_ready, l * EARLY + EARLY)
                    for m in range(2 * EARLY):
                        pe.matmul(bank[3][:, S + m:S + m + 1], acc_early[:, m // 2, m % 2 * P:(m % 2 + 1) * P],
                                  ones[:, 0:1], start=True, stop=True)
                norm_sum(l * 2 + 2)
                root_rows(l * 2 + 2)

            for t in range(NT):
                for k in range(KB):
                    if t == 0 and k % 2 == 0:
                        pe.wait_ge(hn_ready, 2 * L * 4 + k // 2 + 1)
                    last = pe.transpose(bank[3 + 2 * t + k // 4][:, k % 4 * P:(k % 4 + 1) * P],
                                        hn[:, k, t * P:(t + 1) * P], ident)
                last.then_inc(out_turned, 1)

        @block.scalar
        def _(act):
            act.dma_start(tab[:, T_CB:T_END], table[:, T_CB:T_END]).then_inc(s_c, 16)
            act.dma_start(x_tok[:, :, :], x.rearrange("a (t p) n -> p (a t) n", p=P)).then_inc(s_x, 16)

            def hi(l, u):
                if u is None:
                    return
                s, r = u.split().mod(SPL), u.mod(RAW)
                act.wait_ge(landed[r], n_landed(l, u))
                for h in range(2):
                    act.wait_ge(half_done, n_half(l, u, h))
                    for dst, src in parts(u, h, w_hi[:, s, :], raw[:, r, :]):
                        last = act.activation(dst, src, ACT.Copy)
                    last.then_inc(hi_ready, 1)

            def result(l, u):
                act.wait_ge(half_done, n_half(l, u, 1 + FREE_HALVES))
                return bank[u.split().mod(2)]

            def squares(n, i):
                act.wait_ge(x_ready, n * 4 + i + 1)
                act.activation(sq[:, 2 * i:2 * i + 2, :], xf[:, 2 * i:2 * i + 2, :], ACT.Square,
                               scale=D ** -0.5)\
                   .then_inc(sq_ready, 1)

            def std(n):
                act.wait_ge(ss_ready, n + 1)
                act.activation(std2[:, :], bank[2][:, 0:NT], ACT.Sqrt, bias=eps[:, 0:1]).then_inc(sd_ready, 1)

            def round_h(n, sh):
                for i in range(4):
                    act.wait_ge(hn_ready, n * 4 + i + 1)
                    for k in (2 * i, 2 * i + 1):
                        last = act.activation(h_hi[:, k, :], hn[:, k, :], ACT.Identity,
                                              bias=ada[:, sh + k:sh + k + 1])
                    last.then_inc(h_rounded, 1)

            act.wait_ge(c_turned, 1)
            act.activation(fnw[:, :], bank[6][:, 8:16], ACT.Copy)
            act.activation(c32[:, :], bank[6][:, 0:8], ACT.Silu).then_inc(c_ready, 1)

            for i in range(4):
                squares(0, i)
            act.wait_ge(row_ps, 4)
            act.dma_start(tab[:, 0:T_CB], table[:, 0:T_CB]).then_inc(s_tab, 16)
            std(0)

            with act.Fori(0, L) as l:
                hi(l, Unit(SPLIT_UNITS[0]))
                round_h(l * 2, 0)
                hi(l, Unit(SPLIT_UNITS[1]))
                for i in range(N_QK):
                    hi(l, nth("qk", i).ahead())

                def silu_xbc(i):
                    act.wait_ge(conv_ready, l * N_XBC + i + 1)
                    v = xbc[:, 2 * i:2 * i + 2, :]
                    act.activation(v, v, ACT.Silu).then_inc(xbc_ready, 1)

                act.wait_ge(xpad_ready, l + 1)
                for i in range(N_XBC):
                    u = nth("xbc", i)
                    b = result(l, u)
                    act.activation(xpad[:, i % 2, :, 3:S + 3], b[:, :].rearrange("p (m t) -> p m t", m=2),
                                   ACT.Copy)
                    for m in range(2):
                        k = 2 * i + m
                        last = act.activation(xbc[:, k, :], b[:, m * S:(m + 1) * S], ACT.Identity,
                                              bias=par[:, Q_CB + k:Q_CB + k + 1], scale=conv_wp[:, 3, k:k + 1])
                    last.then_inc(bank_free[u.split().mod(2)], 1)
                    hi(l, u.ahead())
                    if i:
                        silu_xbc(i - 1)
                silu_xbc(N_XBC - 1)

                for i in range(N_AQK):
                    u = nth("aqk", i)
                    b = result(l, u)
                    act.activation(aqk[:, 2 * i:2 * i + 2, :], b[:, :].rearrange("p (m t) -> p m t", m=2),
                                   ACT.Copy).then_inc(bank_free[u.split().mod(2)], 1)
                    hi(l, u.ahead())
                def value_or_gate(i):
                    u = nth("tok", i)
                    b = result(l, u)
                    act.activation(tok[:, i // 4, :, i % 4 * COL:(i % 4 + 1) * COL],
                                   b[:, :].rearrange("p (t n) -> p t n", t=NT),
                                   ACT.Silu if i >= 4 else ACT.Copy).then_inc(bank_free[u.split().mod(2)], 1)
                    hi(l, u.ahead())
                for i in range(N_TOK - 1):
                    value_or_gate(i)
                hi(l, Unit(U_DT).ahead())
                for i in range(N_AV):
                    u = nth("av", i)
                    b = result(l, u)
                    act.activation(av[:, :, i * COL:(i + 1) * COL], b[:, :].rearrange("p (t n) -> p t n", t=NT),
                                   ACT.Copy).then_inc(bank_free[u.split().mod(2)], 1)
                    hi(l, u.ahead())
                    if i == 1:
                        act.wait_ge(dtx_ready, l + 1)
                        act.activation(dt_e[:, :], dt_e[:, :], ACT.Exp, scale=-1.0)
                        act.activation(exp_a[:, :], par[:, Q_ALOG:Q_ALOG + SH], ACT.Exp)
                        act.drain()
                        act.activation(dt_e[:, :], dt_e[:, :], ACT.Ln, bias=one[:, 0:1]).then_inc(dte_ready, 1)

                def gate(g):
                    if g < 0:
                        return value_or_gate(N_TOK - 1)
                    u = nth("gate", g)
                    b = result(l, u)
                    act.activation(gates[:, 2 * g:2 * g + 2, :], b[:, :].rearrange("p (m t) -> p m t", m=2),
                                   ACT.Tanh, scale=0.5).then_inc(bank_free[u.split().mod(2)], 1)
                    hi(l, u.ahead())

                def square_sums(j):
                    act.wait_ge(yssd_ready, l * 4 + j + 1)
                    for t in range(NT):
                        last = act.activation(junk[:, :], tok[:, 2, t, j * COL:(j + 1) * COL], ACT.Square,
                                              scale=COL ** -0.5, accum_out=ss[:, j, t:t + 1])
                        if t == 0:
                            act.drain()
                    last.then_inc(ssq_ready, 1)

                def turned_hi(i):
                    act.wait_ge(yt_ps, l * 9 + i + 1)
                    b = bank[turn_bank(i)]
                    if i >= 5:
                        for m in range(2):
                            k = (i - 5) * 2 + m
                            last = act.activation(y_hi[:, 2 * i + m, :], b[:, m * S:(m + 1) * S], ACT.Copy,
                                                  scale=par[:, Q_SN + k:Q_SN + k + 1])
                    else:
                        last = act.activation(y_hi[:, 2 * i:2 * i + 2, :],
                                              b[:, :].rearrange("p (m t) -> p m t", m=2), ACT.Copy)
                    last.then_inc(yt_hi, 1)

                def decays(j):
                    act.wait_ge(seg_ready, l * 4 + j + 1)
                    act.activation(decay[:, :, :], decay[:, :, :], ACT.Exp).then_inc(dec_ready, 1)

                for j in range(4):
                    n = l * 4 + j + 1
                    if j:
                        decays(j - 1)
                    gate(3 * j - 1)
                    act.wait_ge(max_ready, n)
                    act.activation(att_s[:, 0:384], att_s[:, 0:384], ACT.Exp, bias=negmax[:, 0:1],
                                   accum_out=ssum[:, 0:1])
                    act.activation(att_s[:, 384:1152], att_s[:, 384:1152], ACT.Exp, bias=negmax[:, 1:2],
                                   accum_out=ssum[:, 1:2]).then_inc(p_ready, 1)
                    gate(3 * j)
                    act.wait_ge(pt_ps, n)
                    act.activation(p_t[:, 0:4, :], bank[5][:, :].rearrange("p (i n) -> p i n", i=4), ACT.Copy)
                    act.activation(p_t[:, 4:8, :], bank[6][:, :].rearrange("p (i n) -> p i n", i=4), ACT.Copy)
                    act.activation(p_t[:, 8, :], bank[7][:, 0:P], ACT.Copy).then_inc(pt_ready, 1)
                    gate(3 * j + 1)
                    if j:
                        square_sums(j - 1)
                    if j == 3:
                        act.wait_ge(yret_ready, n)
                        act.activation(sd[:, 0, :], mv[:, :, :, 1].rearrange("p h t -> p (h t)"), ACT.Sqrt,
                                       bias=eps[:, 0:1]).then_inc(gsd_ready, 1)
                    u = nth("z", j)
                    b = result(l, u)
                    act.activation(tok[:, 2, :, j * COL:(j + 1) * COL], b[:, :].rearrange("p (t n) -> p t n", t=NT),
                                   ACT.Silu).then_inc(bank_free[u.split().mod(2)], 1)
                    hi(l, u.ahead())
                decays(3)
                gate(11)
                for i in range(5):
                    turned_hi(i)
                for i in range(4):
                    hi(l, nth("ret", i).ahead())
                    if i == 2:
                        square_sums(3)
                        act.wait_ge(ssq_ready, l * 4 + 4)
                        act.activation(sd[:, 1, :], ss[:, :, :].rearrange("p h t -> p (h t)"), ACT.Sqrt,
                                       bias=eps[:, 0:1]).then_inc(gsd_ready, 1)
                for i in range(5, 7):
                    turned_hi(i)
                hi(l, Unit(U_ATT).ahead())
                for i in range(7, 9):
                    turned_hi(i)
                for i in range(4):
                    if i < 3:
                        hi(l, Unit(U_SSM + i).ahead())
                    act.wait_ge(mix_ready, l * 4 + i + 1)
                    act.activation(m_hi[:, 2 * i:2 * i + 2, :], mixed[:, 2 * i:2 * i + 2, :], ACT.Copy)\
                       .then_inc(mix_hi, 1)
                hi(l, Unit(U_SSM + 3).ahead())
                for i in range(N_OUT):
                    if i < 3:
                        hi(l, Unit(U_OUT + i).ahead())
                    squares(l * 2 + 1, i)
                hi(l, Unit(U_OUT + 3).ahead())
                std(l * 2 + 1)
                round_h(l * 2 + 1, 24)

                def hidden_hi(i):
                    act.wait_ge(hid_ready, l * (N_FF // 2) + i.over(2, 1, 0))
                    act.activation(f_hi[:, bass.ds(i.over(2, 2, -2), 2), :],
                                   hid[:, :].rearrange("p (m t) -> p m t", m=2), ACT.Copy).then_inc(hid_hi, 1)

                def ffn(u, i, first=False):
                    if i.base % 2 == 0:
                        if not first:
                            hidden_hi(i)
                        b = result(l, u)
                        act.activation(sil[:, :], b[:, :], ACT.Silu).then_inc(bank_free[u.split().mod(2)], 1)
                    hi(l, u.ahead())
                ffn(Unit(U_FF), Unit(0), True)
                ffn(Unit(U_FF + 1), Unit(1))
                units_from(act, U_FF, 2, N_FF, 4, ffn)
                hidden_hi(Unit(N_FF))
                for i in range(N_FF2):
                    hi(l, Unit(U_FF2 + i).ahead())
                for i in range(4):
                    squares(l * 2 + 2, i)
                std(l * 2 + 2)

        @block.vector
        def _(dve):
            dve.sem_inc(lo_ready, FREE_RAW)
            dve.sem_inc(bank_free[0], 1)
            dve.sem_inc(bank_free[1], 1)
            dve.memset(eps[:, :], EPS)
            dve.memset(one[:, :], 1.0)
            dve.memset(dt_f[:, :], 0.0)

            def lo(l, u, halves=(0, 1)):
                if u is None:
                    return
                s, r = u.split().mod(SPL), u.mod(RAW)
                for h in halves:
                    dve.wait_ge(hi_ready, n_half(l, u, h))
                    for dst, src, lead in parts(u, h, w_lo[:, s, :], raw[:, r, :], w_hi[:, s, :].bitcast(F32)):
                        last = dve.tensor_tensor(dst, src, lead, ALU.subtract)
                    last.then_inc(lo_ready, 1)

            def result(l, u):
                dve.wait_ge(half_done, n_half(l, u, 1 + FREE_HALVES))
                return bank[u.split().mod(2)]

            def add_squares(n, i):
                dve.wait_ge(sq_ready, n * 4 + i + 1)
                if i:
                    dve.tensor_tensor(sq[:, 0:2, :], sq[:, 0:2, :], sq[:, 2 * i:2 * i + 2, :], ALU.add)
                    dve.drain()
                if i == 3:
                    dve.tensor_tensor(sq[:, 0, :], sq[:, 0, :], sq[:, 1, :], ALU.add).then_inc(sum_ready, 1)

            def inverse_std(n):
                dve.wait_ge(sd_ready, n + 1)
                dve.reciprocal(root[:, :], std2[:, :]).then_inc(root_ready, 1)

            def normed(n, weight, pairs):
                dve.wait_ge(root_ps, n + 1)
                for k in range(2 * pairs[0], 2 * pairs[-1] + 2):
                    last = dve.scalar_tensor_tensor(out=hn[:, k, :], in0=xf[:, k, :], scalar=weight[:, k:k + 1],
                                                    in1=bank[2][:, S:2 * S], op0=ALU.mult, op1=ALU.mult)
                    if k % 2:
                        last.then_inc(hn_ready, 1)

            def split_h(n, sh, pairs):
                for i in pairs:
                    dve.wait_ge(h_rounded, n * 4 + i + 1)
                    for k in (2 * i, 2 * i + 1):
                        last = dve.scalar_tensor_tensor(out=h_lo[:, k, :], in0=hn[:, k, :],
                                                        scalar=ada[:, sh + k:sh + k + 1],
                                                        in1=h_hi[:, k, :].bitcast(F32),
                                                        op0=ALU.add, op1=ALU.subtract)
                    last.then_inc(h_split, 1)

            def norm_and_split(n, a, sh):
                for i in range(4):
                    normed(n, a1[:, a, :], (i,))
                    if i:
                        split_h(n, sh, (i - 1,))
                split_h(n, sh, (3,))

            def ada_take(first, count, src):
                v = slice(2 * first, 2 * (first + count))
                return dve.tensor_tensor(ada[:, v], src, par[:, v], ALU.add)

            def norm_scale(a, sc, w):
                dve.drain()
                dve.scalar_tensor_tensor(out=a1[:, a, :], in0=ada[:, sc:sc + KB], scalar=1.0,
                                         in1=par[:, w:w + KB], op0=ALU.add, op1=ALU.mult)

            dve.wait_ge(x_turned, 1)
            for i in range(4):
                dve.tensor_copy(xf[:, 2 * i:2 * i + 2, :], bank[2 + i][:, :].rearrange("p (m t) -> p m t", m=2))\
                   .then_inc(x_ready, 1)

            def copy_row(q):
                dve.wait_ge(row_ps, 2 * q + 2)
                dve.tensor_copy(ada_row[0:1, 2 * q * COL:(2 * q + 2) * COL], bank[ROW_BANK[q]][0:1, :])\
                   .then_inc(row_ready, 1)

            def first_early(i):
                slot = i % EARLY_SLOTS
                dve.wait_ge(early_landed[slot], 16 * (i // EARLY_SLOTS + 1))
                w = early[slot].rearrange("p (k n) -> p k n", k=KB)
                dve.tensor_tensor(w, w, c32[:, :, None].to_broadcast([P, KB, COL]), ALU.mult)
                for half in (4, 2):
                    dve.drain()
                    dve.tensor_tensor(w[:, 0:half, :], w[:, 0:half, :], w[:, half:2 * half, :], ALU.add)
                dve.drain()
                dve.tensor_tensor(acc_first[:, i - EARLY_PE, :], w[:, 0, :], w[:, 1, :], ALU.add)\
                   .then_inc(first_ready, 1)
            copy_row(0)
            for i in range(4):
                add_squares(0, i)
            first_early(6)
            copy_row(1)
            inverse_std(0)
            first_early(7)
            copy_row(2)

            with dve.Fori(0, L) as l:
                dve.wait_ge(par_turned, l + 1)
                dve.tensor_copy(par[:, :], bank[3][:, 0:Q_END])
                dve.drain()
                ada_take(0, EARLY, bank[3][:, S:S + 2 * EARLY])
                norm_scale(0, 8, Q_N1)
                dve.drain()
                lo(l, Unit(SPLIT_UNITS[0]), (0,))
                norm_and_split(l * 2, 0, 0)
                lo(l, Unit(SPLIT_UNITS[0]), (1,))
                lo(l, Unit(SPLIT_UNITS[1]))
                dve.wait_ge(s_tab, 16)
                for i in range(N_QK):
                    u = nth("qk", i)
                    b = result(l, u)[:, :].rearrange("p (m t) -> p m t", m=2)
                    dve.tensor_tensor(rope_c[:, :, :], b, cos[:, None, :].to_broadcast([P, 2, S]), ALU.mult)
                    dve.tensor_tensor(rope_s[:, :, :], b, sin[:, None, :].to_broadcast([P, 2, S]), ALU.mult)\
                       .then_inc(bank_free[u.split().mod(2)], 1)
                    dve.drain()
                    dve.tensor_tensor(qk[:, i, 0, :], rope_c[:, 0, :], rope_s[:, 1, :], ALU.subtract)
                    dve.tensor_tensor(qk[:, i, 1, :], rope_s[:, 0, :], rope_c[:, 1, :], ALU.add)
                    dve.drain().then_inc(rot_out, 1)
                    lo(l, u.ahead())
                dve.memset(xpad[:, :, :, 0:3], 0.0).then_inc(xpad_ready, 1)
                for i in range(N_XBC):
                    u = nth("xbc", i)
                    lo(l, u.ahead())
                    dve.wait_ge(bank_free[u.split().mod(2)], n_bank(l, u) + 1)
                    for t in range(3):
                        for m in range(2):
                            k = 2 * i + m
                            last = dve.scalar_tensor_tensor(out=xbc[:, k, :], in0=xpad[:, i % 2, m, t:t + S],
                                                            scalar=conv_wp[:, t, k:k + 1],
                                                            in1=xbc[:, k, :], op0=ALU.mult, op1=ALU.add)
                        if t < 2:
                            dve.drain()
                    last.then_inc(conv_ready, 1)
                for i in range(N_AQK):
                    lo(l, nth("aqk", i).ahead())
                for i in range(N_TOK - 1):
                    lo(l, nth("tok", i).ahead())
                u = Unit(U_DT)
                b = result(l, u)
                dve.tensor_copy(dt_f[0:SH, :], b[0:SH, 0:S]).then_inc(bank_free[u.split().mod(2)], 1)
                dve.drain().then_inc(dtf_ready, 1)
                lo(l, u.ahead())
                lo(l, nth("av", 0).ahead())
                dve.wait_ge(dt_turned, l + 1)
                dve.tensor_tensor(dt_x[:, :].rearrange("p (t h) -> p t h", t=NT),
                                  bank[3][:, 0:S].rearrange("p (t h) -> p t h", t=NT)[:, :, 0:SH],
                                  par[:, None, Q_DTB:Q_DTB + SH].to_broadcast([P, NT, SH]), ALU.add)
                dve.drain()
                dve.scalar_tensor_tensor(out=dt_e[:, :], in0=dt_x[:, :], scalar=-1.0, in1=dt_x[:, :],
                                         op0=ALU.mult, op1=ALU.max).then_inc(dtx_ready, 1)
                lo(l, nth("av", 1).ahead())
                dve.wait_ge(dte_ready, l + 1)
                dt_flat = dt[:, :, :].rearrange("p t h -> p (t h)")
                dve.scalar_tensor_tensor(out=dt_flat, in0=dt_x[:, :], scalar=0.0, in1=dt_e[:, :],
                                         op0=ALU.max, op1=ALU.add)
                dve.drain()
                for t in range(NT):
                    last = dve.scalar_tensor_tensor(out=d_a[:, t, :], in0=dt[:, t, :], scalar=-1.0,
                                                    in1=exp_a[:, :], op0=ALU.mult, op1=ALU.mult)
                last.then_inc(da_ready, 1)
                lo(l, nth("av", 2).ahead())

                def gate_unit(g):
                    return nth("gate", g) if g >= 0 else nth("tok", N_TOK - 1)

                def ssd_out(j):
                    dve.wait_ge(y_ps, l * 4 + j + 1)
                    f = ytmp[:, :, :].rearrange("p t n -> p (t n)")
                    dve.tensor_tensor(f, bank[3][:, :], f, ALU.add)
                    dve.drain()
                    z = tok[:, 2, :, j * COL:(j + 1) * COL]
                    dve.tensor_tensor(z, z, ytmp[:, :, :], ALU.mult).then_inc(yssd_ready, 1)

                def segments(j):
                    dve.wait_ge(csb_ps, l * 4 + j + 1)
                    for r in range(4):
                        h = 4 * j + r
                        b = bank[7 if r < 2 else 5][:, r % 2 * S:(r % 2 + 1) * S]
                        dve.tensor_scalar(decay[:, r, 0:S], b, cs[:, 0, h:h + 1], 0.0, ALU.subtract, ALU.min)
                        last = dve.tensor_scalar(decay[:, r, S:S + P], b[:, P:S], cs[:, 1, h:h + 1], 0.0,
                                                 ALU.subtract, ALU.min)
                    last.then_inc(seg_ready, 1)

                def scale_branch(which):
                    for j in range(4):
                        for t in range(NT):
                            y = tok[:, 2 * which, t, j * COL:(j + 1) * COL]
                            r = ri[:, which, 2 * j + t:2 * j + t + 1]
                            if which == 0:
                                last = dve.scalar_tensor_tensor(out=y, in0=y, scalar=r,
                                                                in1=tok[:, 1, t, j * COL:(j + 1) * COL],
                                                                op0=ALU.mult, op1=ALU.mult)
                            else:
                                last = dve.tensor_scalar(y, y, r, None, ALU.mult)
                    last.then_inc(ynorm_ready, 1)

                def turned_lo(i):
                    dve.wait_ge(yt_hi, l * 9 + i + 1)
                    b = bank[turn_bank(i)]
                    if i >= 5:
                        for m in range(2):
                            k = (i - 5) * 2 + m
                            last = dve.scalar_tensor_tensor(out=y_lo[:, 2 * i + m, :], in0=b[:, m * S:(m + 1) * S],
                                                            scalar=par[:, Q_SN + k:Q_SN + k + 1],
                                                            in1=y_hi[:, 2 * i + m, :].bitcast(F32),
                                                            op0=ALU.mult, op1=ALU.subtract)
                    else:
                        last = dve.tensor_tensor(y_lo[:, 2 * i:2 * i + 2, :],
                                                 b[:, :].rearrange("p (m t) -> p m t", m=2),
                                                 y_hi[:, 2 * i:2 * i + 2, :].bitcast(F32), ALU.subtract)
                    last.then_inc(yt_lo, 1)

                for j in range(4):
                    n = l * 4 + j + 1
                    if j:
                        segments(j - 1)
                    lo(l, gate_unit(3 * j - 1).ahead())
                    if j == 0:
                        dve.wait_ge(cs_ps, l + 1)
                        dve.tensor_copy(cs[:, :, :], bank[3][:, 0:2 * SH].rearrange("p (t h) -> p t h", t=NT))
                    dve.wait_ge(sc_ps, n)
                    dve.tensor_tensor(m_ret[:, 0:S], bank[2][:, 0:S], ret_mask[:, j, :], ALU.mult)
                    dve.tensor_tensor(m_ret[:, S:S + P], bank[2][:, S:S + P], ret_mask[:, j, 0:P], ALU.mult)\
                       .then_inc(mret_ready, 1)
                    a3 = att_s[:, :].rearrange("p (i n) -> p i n", n=P)
                    dve.scalar_tensor_tensor(out=a3[:, 0:3, :],
                                             in0=bank[5][:, 0:384].rearrange("p (g n) -> p g n", g=AG),
                                             scalar=AHD ** -0.5, in1=att_mask[:, :, P:S], op0=ALU.mult, op1=ALU.add)
                    dve.scalar_tensor_tensor(out=att_s[:, 384:896], in0=bank[6][:, :], scalar=AHD ** -0.5,
                                             in1=tab[:, T_ATT:T_ATT + 512], op0=ALU.mult, op1=ALU.add)
                    dve.scalar_tensor_tensor(out=att_s[:, 896:1152], in0=bank[7][:, 0:S], scalar=AHD ** -0.5,
                                             in1=att_mask[:, 2, :], op0=ALU.mult, op1=ALU.add)
                    dve.drain()
                    dve.tensor_reduce(rsum[:, 0:1], att_s[:, 0:384], AXX, ALU.max)
                    dve.tensor_reduce(rsum[:, 1:2], att_s[:, 384:1152], AXX, ALU.max)
                    dve.drain()
                    dve.tensor_scalar(negmax[:, :], rsum[:, :], -1.0, None, ALU.mult).then_inc(max_ready, 1)
                    lo(l, gate_unit(3 * j).ahead())
                    dve.wait_ge(pv_ret, n)
                    for t in range(NT):
                        dve.bn_stats(bst[:, t, :], bank[2][:, t * S:(t + 1) * S])
                    dve.drain()
                    for t in range(NT):
                        dve.bn_aggr(mv[:, j, t, :], bst[:, t, :])
                    dve.drain()
                    for t in range(NT):
                        last = dve.tensor_scalar(tok[:, 0, t, j * RV:(j + 1) * RV], bank[2][:, t * S:(t + 1) * S],
                                                 mv[:, j, t, 0:1], None, ALU.subtract)
                    last.then_inc(yret_ready, 1)
                    if j:
                        ssd_out(j - 1)
                    lo(l, gate_unit(3 * j + 1).ahead())
                    dve.wait_ge(s2_ps, n)
                    dve.reciprocal(rsum[:, :], ssum[:, :])
                    dve.drain()
                    for t in range(NT):
                        dve.tensor_scalar(yatt[:, t, j * AHD:(j + 1) * AHD], bank[5][:, t * AHD:(t + 1) * AHD],
                                          rsum[:, t:t + 1], None, ALU.mult)
                    for t in range(NT):
                        xs = bank[6][:, t * S:(t + 1) * S].rearrange("p (r n) -> p r n", r=4)
                        dve.tensor_tensor(xdt[:, t, :].rearrange("p (r n) -> p r n", r=4), xs,
                                          dt[:, t, 4 * j:4 * j + 4, None].to_broadcast([P, 4, SHD]), ALU.mult)
                        dve.tensor_tensor(ytmp[:, t, :].rearrange("p (r n) -> p r n", r=4), xs,
                                          par[:, Q_DSK + 4 * j:Q_DSK + 4 * j + 4, None].to_broadcast([P, 4, SHD]),
                                          ALU.mult)
                    dve.tensor_tensor(cbm[:, :], bank[3][:, 0:384], cb_mask, ALU.mult).then_inc(s2_ready, 1)
                    if j == 3:
                        dve.wait_ge(gsd_ready, l * 2 + 1)
                        dve.reciprocal(ri[:, 0, :], sd[:, 0, :])
                        dve.drain()
                        scale_branch(0)
                    lo(l, nth("z", j).ahead())
                segments(3)
                lo(l, nth("gate", 11).ahead())
                dve.wait_ge(acc_summed, l * LATE + LATE + 1)
                ada_take(EARLY, LATE, bank[4][:, 0:2 * LATE]).then_inc(ada_taken, 1)
                dve.drain()
                dve.tensor_scalar(g1h[:, :], ada[:, 16:24], 0.5, None, ALU.mult)
                norm_scale(1, 32, Q_N2)
                for i in range(5):
                    turned_lo(i)

                def gated(ps, g, k, first):
                    gt = gates[:, g * KB + k:g * KB + k + 2, :].rearrange("p m t -> p (m t)")
                    mx = mixed[:, k:k + 2, :].rearrange("p m t -> p (m t)")
                    return dve.scalar_tensor_tensor(out=mx if first else br[:, k // 2 % 2, :], in0=gt, scalar=1.0,
                                                    in1=ps, op0=ALU.add, op1=ALU.mult)

                def add_branch(k):
                    dve.drain()
                    mx = mixed[:, k:k + 2, :].rearrange("p m t -> p (m t)")
                    return dve.tensor_tensor(mx, mx, br[:, k // 2 % 2, :], ALU.add)
                for i in range(4):
                    u = nth("ret", i)
                    b = result(l, u)
                    gated(b[:, :], 0, 2 * i, True).then_inc(bank_free[u.split().mod(2)], 1)
                    if i == 1:
                        ssd_out(3)
                    lo(l, u.ahead())
                    if i == 2:
                        dve.wait_ge(gsd_ready, l * 2 + 2)
                        dve.reciprocal(ri[:, 1, :], sd[:, 1, :])
                        dve.drain()
                        scale_branch(1)
                for q in range(5, 7):
                    turned_lo(q)
                lo(l, Unit(U_ATT).ahead())
                for q in range(7, 9):
                    turned_lo(q)
                result(l, Unit(U_ATT))
                for i in range(4):
                    u = Unit(U_SSM + i)
                    gated(bank[4 + i][:, :], 2, 2 * i, False)
                    add_branch(2 * i)
                    dve.drain()
                    b = result(l, u)
                    gated(b[:, :], 1, 2 * i, False).then_inc(bank_free[u.split().mod(2)], 1)
                    add_branch(2 * i).then_inc(mix_ready, 1)
                    if i < 3:
                        lo(l, u.ahead())
                lo(l, Unit(U_SSM + 3).ahead())
                for i in range(N_OUT):
                    u = Unit(U_OUT + i)
                    b = result(l, u)
                    for m in range(2):
                        k = 2 * i + m
                        last = dve.scalar_tensor_tensor(out=xf[:, k, :], in0=b[:, m * S:(m + 1) * S],
                                                        scalar=g1h[:, k:k + 1], in1=xf[:, k, :],
                                                        op0=ALU.mult, op1=ALU.add)
                    last.then_inc(bank_free[u.split().mod(2)], 1)
                    dve.drain().then_inc(x_ready, 1)
                    if i < 3:
                        lo(l, u.ahead())
                    add_squares(l * 2 + 1, i)
                lo(l, u.ahead(), (0,))
                inverse_std(l * 2 + 1)
                lo(l, u.ahead(), (1,))
                norm_and_split(l * 2 + 1, 1, 24)

                def hidden_lo(i):
                    dve.wait_ge(hid_hi, l * (N_FF // 2) + i.over(2, 1, 0))
                    v = bass.ds(i.over(2, 2, -2), 2)
                    dve.tensor_tensor(f_lo[:, v, :], hid[:, :].rearrange("p (m t) -> p m t", m=2),
                                      f_hi[:, v, :].bitcast(F32), ALU.subtract).then_inc(hid_lo, 1)

                def ffn(u, i, first=False):
                    if i.base % 2 == 0:
                        if not first:
                            hidden_lo(i)
                    else:
                        b = result(l, u)
                        if not first:
                            dve.wait_ge(hid_lo, l * (N_FF // 2) + i.over(2, 1, 0))
                        dve.tensor_tensor(hid[:, :], b[:, :], sil[:, :], ALU.mult)\
                           .then_inc(bank_free[u.split().mod(2)], 1)
                        dve.drain().then_inc(hid_ready, 1)
                    lo(l, u.ahead())
                ffn(Unit(U_FF), Unit(0), True)
                ffn(Unit(U_FF + 1), Unit(1), True)
                units_from(dve, U_FF, 2, N_FF, 4, ffn)
                hidden_lo(Unit(N_FF))
                for i in range(N_FF2):
                    lo(l, Unit(U_FF2 + i).ahead())
                for k in range(KB):
                    if k == KB - 2:
                        result(l, Unit(U_FF2 + N_FF2 - 1))
                    elif k % 2 == 0:
                        dve.wait_ge(ffn_pair, l * (KB // 2 - 1) + k // 2 + 1)
                    last = dve.scalar_tensor_tensor(out=xf[:, k, :], in0=bank[4 + k // 2][:, k % 2 * S:(k % 2 + 1) * S],
                                                    scalar=ada[:, 40 + k:41 + k], in1=xf[:, k, :],
                                                    op0=ALU.mult, op1=ALU.add)
                    if k % 2:
                        last.then_inc(x_ready, 1)
                for i in range(4):
                    add_squares(l * 2 + 2, i)
                inverse_std(l * 2 + 2)
            normed(2 * L, fnw[:, :], range(4))
            for t in range(NT):
                dve.wait_ge(out_turned, t + 1)
                for q in range(2):
                    last = dve.tensor_copy(x_tok[:, t, q * 512:(q + 1) * 512], bank[3 + 2 * t + q][:, :])
                last.then_inc(out_ready, 1)

        @block.gpsimd
        def _(pool):
            pool.wait_ge(c_ready, 1)
            pool.sem_inc(early_read, 2)
            with pool.Fori(0, L) as l:
                def products(w, read, out, ready, out_free=None):
                    pool.tensor_tensor(w, w, c32[:, :, None].to_broadcast([P, KB, COL]), ALU.mult)
                    pool.drain()
                    pool.tensor_tensor(mac[:, :, :], w[:, 0:4, :], w[:, 4:8, :], ALU.add).then_inc(read, 1)
                    pool.drain()
                    pool.tensor_tensor(mac[:, 0:2, :], mac[:, 0:2, :], mac[:, 2:4, :], ALU.add)
                    pool.drain()
                    if out_free:
                        out_free()
                    pool.tensor_tensor(out, mac[:, 0, :], mac[:, 1, :], ALU.add).then_inc(ready, 1)

                def late(a):
                    u = nth("ada", a)
                    r = u.mod(RAW)
                    pool.wait_ge(landed[r], n_landed(l, u))
                    products(raw[:, r, :].rearrange("p (k n) -> p k n", k=KB), mac_done, acc[:, a % 2, :],
                             acc_ready, lambda: pool.wait_ge(acc_summed, l * LATE + max(a, 1)))

                def next_early(i):
                    pool.wait_ge(early_landed[i % 2], l * (8 * EARLY) + 32 + i // 2 * 16 + 16)
                    products(early[i % 2].rearrange("p (k n) -> p k n", k=KB), early_read,
                             acc_early[:, i, :], early_ready)

                def decayed_scores(j):
                    pool.wait_ge(dec_ready, l * SG + j + 1)
                    pool.tensor_tensor(decay[:, :, :], decay[:, :, :],
                                       cbm[:, None, :].to_broadcast([P, 4, 384]), ALU.mult)\
                        .then_inc(mssd_ready, 1)
                for a in range(11):
                    late(a)
                for j in range(SG):
                    if j:
                        decayed_scores(j - 1)
                    for a in ((11, 12), (13,), (14,), (15,))[j]:
                        late(a)
                decayed_scores(3)
                for i in range(4):
                    pool.wait_ge(mix_hi, l * 4 + i + 1)
                    v = slice(2 * i, 2 * i + 2)
                    pool.tensor_tensor(m_lo[:, v, :], mixed[:, v, :], m_hi[:, v, :].bitcast(F32), ALU.subtract)\
                        .then_inc(mix_lo, 1)
                with pool.If(l < L - 1):
                    for i in range(EARLY):
                        next_early(i)


def turn_bank(i):
    return (2, 6, 5, 7, 4, 2, 3, 2, 3)[i]


def units_from(eng, base, start, count, per, fn):
    full = (count - start) // per
    assert start + full * per == count
    with eng.Fori(0, full) as j:
        for b in range(per):
            fn(Unit(base + start + b, per, j), Unit(start + b, per, j))


def tables():
    f = np.float32
    t = np.zeros((P, T_END), f)
    half = RQK // 2
    inv = f(10000.0) ** (-np.arange(half, dtype=f) / f(half))
    ang = (np.arange(S, dtype=f)[None, :] * inv.astype(f)[:, None]).astype(f)
    t[:, T_COS:T_COS + S] = np.tile(np.cos(ang.astype(np.float64)), (2, 1))
    t[:, T_SIN:T_SIN + S] = np.tile(np.sin(ang.astype(np.float64)), (2, 1))
    key = np.arange(P, dtype=np.float64)[:, None]
    qry = np.arange(S, dtype=np.float64)[None, :]
    lg = np.log1p(-np.exp(np.linspace(np.log(1.0 / 32), np.log(1.0 / 512), RH)))
    for h in range(RH):
        m = np.where(qry >= key, np.exp((qry - key) * lg[h]), 0.0) * RQK ** -0.5
        t[:, T_RET + h * S:T_RET + (h + 1) * S] = m
    q = P + np.arange(P)[:, None]
    k = np.arange(S)[None, :]
    for g, (window, dil) in enumerate(((128, 1), (512, 4), (2048, 16))):
        ok = (q >= k) & ((q - k) % dil == 0) & (q - k <= window)
        t[:, T_ATT + g * S:T_ATT + (g + 1) * S] = np.where(ok, 0.0, -1e30)
    low = (np.arange(P)[None, :] >= np.arange(P)[:, None]).astype(f)
    t[:, T_CB:T_CB + P] = low
    t[:, T_CB + P:T_CB + 2 * P] = 1.0
    t[:, T_CB + 2 * P:T_CB + 3 * P] = low
    t[:, T_TRI:T_TRI + P] = low - 1.0
    t[:, T_ID:T_ID + P] = np.eye(P)
    return t


_INS = ["x", "c", "ada_w", "ada_b", "norm1_w", "w_in", "ssm_conv_w", "ssm_conv_b", "ssm_dt_bias",
        "ssm_a_log", "ssm_d", "ssm_norm_w", "w_br_ret", "w_br_ssm", "w_br_att", "w_out", "norm2_w",
        "w_ff1", "w_ff3", "w_ff2", "final_norm_w"]


def kernel(**inputs):
    import numpy as _np
    import concourse.bacc as _bacc
    from concourse import mybir as _mybir
    from concourse.bass_utils import run_bass_kernel_spmd as _run

    nc = _bacc.Bacc("TRN2", target_bir_lowering=False, num_devices=1, dynamic_dma_scratch_size=1024)
    arrays, args = {}, []
    named = {name: _np.ascontiguousarray(inputs[name]) for name in _INS}
    named["table"] = tables()
    for name, a in named.items():
        arrays[f"in_{name}_dram"] = a
        args.append(nc.dram_tensor(f"in_{name}_dram", a.shape, _mybir.dt.from_np(a.dtype), kind="ExternalInput").ap())
    args.append(nc.dram_tensor("out_0_dram", (1, S, D), _mybir.dt.float32, kind="ExternalOutput").ap())
    build(nc, *args)
    r = _run(nc, [arrays], core_ids=[0])
    return r.results[0]["out_0_dram"]
```
